# Optimizing a Trainium2 kernel written in Bass

```python
import math
import jax, jax.numpy as jnp
from jax import lax
import numpy as np

D_MODEL = 1024
BATCH = 1
SEQ = 512
DEPTH = 2
DEC_BATCH = 8
DEC_SEQ = 16
PAST_LEN = 1024

CHUNK = 64
N_EVEN = (DEPTH + 1) // 2
N_ODD = DEPTH // 2
H_A = 4
DK_A = 64
DV_A = 128
R_A = 16
GATE_NORM_A = 16.0
A_QK = H_A * DK_A
A_V = H_A * DV_A
H_B = 8
D_B = 64
B_W = H_B * D_B
BAND_CHUNKS = 8
WIN_B = BAND_CHUNKS * CHUNK
MAX_REL = 128
H_C = 16
D_C = 64
C_W = H_C * D_C
Q_BLOCK = 128
FOX_BIAS_INIT = 2.0
D_FF = 2816
EPS = 1e-6
E_IN = 2 * A_QK + 2 * A_V + R_A + 3 * B_W
O_IN = 3 * C_W + H_C

kernel_name = "hybrid_streaming_gla_band_fox_macaron"

def rmsnorm(x, g):
    xf = x.astype(jnp.float32)
    y = xf * lax.rsqrt(jnp.mean(xf * xf, axis=-1, keepdims=True) + EPS)
    return (y * g.astype(jnp.float32)).astype(x.dtype)

def swiglu(x, w_gu, w_down):
    g, u = jnp.split(x @ w_gu, 2, axis=-1)
    return (jax.nn.silu(g) * u) @ w_down

def split_cols(h, sizes):
    idx = np.cumsum(sizes)[:-1].tolist()
    return jnp.split(h, idx, axis=-1)

def gla_blocked(q, k, v, log_a, s0):
    B, T, H, _ = q.shape
    L = min(CHUNK, T)
    n = T // L
    f32 = jnp.float32

    def blk(t):
        return t.astype(f32).reshape(B, n, L, H, -1).transpose(1, 0, 3, 2, 4)

    qc, kc, vc, ac = blk(q), blk(k), blk(v), blk(log_a)
    bcum = jnp.cumsum(ac, axis=-2)
    b_last = bcum[..., -1:, :]
    q_in = qc * jnp.exp(bcum)
    k_in = kc * jnp.exp(-bcum)
    causal = np.tril(np.ones((L, L), dtype=bool))
    att = jnp.where(causal, jnp.einsum('nbhik,nbhjk->nbhij', q_in, k_in), 0.0)
    o_intra = jnp.einsum('nbhij,nbhjv->nbhiv', att, vc)
    k_state = kc * jnp.exp(b_last - bcum)
    a_total = jnp.exp(b_last[..., 0, :])

    def step(s, inp):
        qi, ks, vi, at = inp
        o = jnp.einsum('bhik,bhkv->bhiv', qi, s)
        s = at[..., None] * s + jnp.einsum('bhjk,bhjv->bhkv', ks, vi)
        return s, o

    s_fin, o_inter = lax.scan(step, s0.astype(f32), (q_in, k_state, vc, a_total))
    o = (o_intra + o_inter).transpose(1, 0, 3, 2, 4).reshape(B, T, H, -1)
    return o, s_fin

def band_attention_prompt(q, k, v, rel_bias):
    B, T, H, D = q.shape
    n = T // CHUNK
    P = BAND_CHUNKS
    pad = ((0, 0), (P * CHUNK, 0), (0, 0), (0, 0))
    kp = jnp.pad(k, pad).reshape(B, n + P, CHUNK, H, D)
    vp = jnp.pad(v, pad).reshape(B, n + P, CHUNK, H, D)
    kb = jnp.concatenate([kp[:, o:o + n] for o in range(P + 1)], axis=2)
    vb = jnp.concatenate([vp[:, o:o + n] for o in range(P + 1)], axis=2)
    qc = q.reshape(B, n, CHUNK, H, D)
    s = jnp.einsum('bnihd,bnjhd->bnhij', qc, kb).astype(jnp.float32) * (D ** -0.5)
    i = np.arange(CHUNK)[:, None]
    j = np.arange((P + 1) * CHUNK)[None, :]
    dist = i - (j - P * CHUNK)
    bias = rel_bias[:, np.clip(dist, -MAX_REL, MAX_REL) + MAX_REL].astype(jnp.float32)
    kpos = (np.arange(n)[:, None] - P) * CHUNK + j
    valid = (kpos >= 0)[None, :, None, None, :]
    s = jnp.where(valid, s + bias[None, None], -jnp.inf)
    p = jax.nn.softmax(s, axis=-1).astype(v.dtype)
    return jnp.einsum('bnhij,bnjhd->bnihd', p, vb).reshape(B, T, H * D)

def band_attention_sample(q, k, v, ck, cv, rel_bias):
    B, S, H, D = q.shape
    Lc = ck.shape[1]
    kk = jnp.concatenate([ck, k], axis=1)
    vv = jnp.concatenate([cv, v], axis=1)
    s = jnp.einsum('bihd,bjhd->bhij', q, kk).astype(jnp.float32) * (D ** -0.5)
    qpos = PAST_LEN + np.arange(S)
    kpos = np.concatenate([PAST_LEN - Lc + np.arange(Lc), PAST_LEN + np.arange(S)])
    dist = qpos[:, None] - kpos[None, :]
    bias = rel_bias[:, np.clip(dist, -MAX_REL, MAX_REL) + MAX_REL].astype(jnp.float32)
    p = jax.nn.softmax(s + bias[None], axis=-1).astype(vv.dtype)
    return jnp.einsum('bhij,bjhd->bihd', p, vv).reshape(B, S, H * D)

def fox_prompt(q, k, v, logf):
    B, T, H, D = q.shape
    nq = T // Q_BLOCK
    F = jnp.cumsum(logf, axis=1)
    Fk = F.transpose(0, 2, 1)[:, :, None, :]
    qb = q.reshape(B, nq, Q_BLOCK, H, D).transpose(1, 0, 2, 3, 4)
    Fb = F.reshape(B, nq, Q_BLOCK, H).transpose(1, 0, 3, 2)
    kpos = jnp.arange(T)

    def one(args):
        qi, Fi, bi = args
        s = jnp.einsum('bihd,bjhd->bhij', qi, k).astype(jnp.float32) * (D ** -0.5)
        s = s + Fi[..., :, None] - Fk
        qpos = bi * Q_BLOCK + jnp.arange(Q_BLOCK)
        s = jnp.where(qpos[:, None] >= kpos[None, :], s, -jnp.inf)
        p = jax.nn.softmax(s, axis=-1).astype(v.dtype)
        return jnp.einsum('bhij,bjhd->bihd', p, v)

    o = lax.map(one, (qb, Fb, jnp.arange(nq)))
    return o.transpose(1, 0, 2, 3, 4).reshape(B, T, H * D)

def fox_sample(q, k, v, logf, ck, cv, clogf):
    B, S, H, D = q.shape
    Lc = ck.shape[1]
    clogf = clogf.astype(jnp.float32)
    fq = jnp.cumsum(logf, axis=1)
    c_after = lax.cumsum(clogf, axis=1, reverse=True) - clogf
    fk = jnp.concatenate([-c_after, fq], axis=1)
    kk = jnp.concatenate([ck, k], axis=1)
    vv = jnp.concatenate([cv, v], axis=1)
    s = jnp.einsum('bihd,bjhd->bhij', q, kk).astype(jnp.float32) * (D ** -0.5)
    s = s + fq.transpose(0, 2, 1)[..., :, None] - fk.transpose(0, 2, 1)[..., None, :]
    valid = np.concatenate([np.ones((S, Lc), dtype=bool), np.tril(np.ones((S, S), dtype=bool))], axis=1)
    s = jnp.where(valid, s, -jnp.inf)
    p = jax.nn.softmax(s, axis=-1).astype(vv.dtype)
    return jnp.einsum('bhij,bjhd->bihd', p, vv).reshape(B, S, H * D)

def even_mixer(xn, w_in, w_alpha_up, b_alpha, gla_g, rel_bias, w_out, state):
    B, T, _ = xn.shape
    aq, ak, av, ag, ar, bq, bk, bv = split_cols(xn @ w_in, [A_QK, A_QK, A_V, A_V, R_A, B_W, B_W, B_W])
    q = aq.reshape(B, T, H_A, DK_A) * (DK_A ** -0.5)
    k = ak.reshape(B, T, H_A, DK_A)
    v = av.reshape(B, T, H_A, DV_A)
    log_a = (jax.nn.log_sigmoid((ar @ w_alpha_up + b_alpha).astype(jnp.float32)) / GATE_NORM_A).reshape(B, T, H_A, DK_A)
    s0 = jnp.zeros((B, H_A, DK_A, DV_A), jnp.float32) if state is None else state[0]
    o_a, s_fin = gla_blocked(q, k, v, log_a, s0)
    o_a = rmsnorm(o_a, gla_g).reshape(B, T, A_V).astype(xn.dtype) * jax.nn.silu(ag)
    qb = bq.reshape(B, T, H_B, D_B)
    kb = bk.reshape(B, T, H_B, D_B)
    vb = bv.reshape(B, T, H_B, D_B)
    if state is None:
        o_b = band_attention_prompt(qb, kb, vb, rel_bias)
        keep = min(WIN_B, T)
        nk, nv = kb[:, T - keep:], vb[:, T - keep:]
    else:
        o_b = band_attention_sample(qb, kb, vb, state[1], state[2], rel_bias)
        nk, nv = kb, vb
    y = jnp.concatenate([o_a, o_b], axis=-1) @ w_out
    return y, (s_fin, nk, nv)

def odd_mixer(xn, w_in, b_f, w_out, state):
    B, T, _ = xn.shape
    cq, ck, cv, cf = split_cols(xn @ w_in, [C_W, C_W, C_W, H_C])
    q = cq.reshape(B, T, H_C, D_C)
    k = ck.reshape(B, T, H_C, D_C)
    v = cv.reshape(B, T, H_C, D_C)
    logf = jax.nn.log_sigmoid((cf + b_f).astype(jnp.float32))
    if state is None:
        o = fox_prompt(q, k, v, logf)
    else:
        o = fox_sample(q, k, v, logf, state[0], state[1], state[2])
    return o @ w_out, (k, v, logf)

def trunk(x, layer_states, norm_g, ffn_w_gu, ffn_w_down, even_w_in, gla_w_alpha_up, gla_b_alpha,
          gla_norm_g, band_rel_bias, even_w_out, odd_w_in, fox_b_f, odd_w_out, final_norm_g):
    new_states = []
    for l in range(DEPTH):
        x = x + 0.5 * swiglu(rmsnorm(x, norm_g[l, 0]), ffn_w_gu[l, 0], ffn_w_down[l, 0])
        xn = rmsnorm(x, norm_g[l, 1])
        st = None if layer_states is None else layer_states[l]
        i = l // 2
        if l % 2 == 0:
            y, ns = even_mixer(xn, even_w_in[i], gla_w_alpha_up[i], gla_b_alpha[i], gla_norm_g[i],
                               band_rel_bias[i], even_w_out[i], st)
        else:
            y, ns = odd_mixer(xn, odd_w_in[i], fox_b_f[i], odd_w_out[i], st)
        x = x + y
        x = x + 0.5 * swiglu(rmsnorm(x, norm_g[l, 2]), ffn_w_gu[l, 1], ffn_w_down[l, 1])
        new_states.append(ns)
    return rmsnorm(x, final_norm_g), new_states

def setup_inputs(seed: int = 0) -> dict:
    key = jax.random.key(seed)
    ks = iter(jax.random.split(key, 32))

    def nrm(shape, scale):
        return jax.random.normal(next(ks), shape, jnp.float32) * scale

    lb = min(WIN_B, PAST_LEN)
    return {
        "x_prompt": nrm((BATCH, SEQ, D_MODEL), 1.0),
        "x_sample": nrm((DEC_BATCH, DEC_SEQ, D_MODEL), 1.0),
        "state_gla": nrm((N_EVEN, DEC_BATCH, H_A, DK_A, DV_A), 0.5),
        "cache_band_k": nrm((N_EVEN, DEC_BATCH, lb, H_B, D_B), 1.0),
        "cache_band_v": nrm((N_EVEN, DEC_BATCH, lb, H_B, D_B), 1.0),
        "cache_fox_k": nrm((N_ODD, DEC_BATCH, PAST_LEN, H_C, D_C), 1.0),
        "cache_fox_v": nrm((N_ODD, DEC_BATCH, PAST_LEN, H_C, D_C), 1.0),
        "cache_fox_logf": jax.nn.log_sigmoid(FOX_BIAS_INIT + nrm((N_ODD, DEC_BATCH, PAST_LEN, H_C), 1.0)),
        "norm_g": 1.0 + nrm((DEPTH, 3, D_MODEL), 0.05),
        "ffn_w_gu": nrm((DEPTH, 2, D_MODEL, 2 * D_FF), D_MODEL ** -0.5),
        "ffn_w_down": nrm((DEPTH, 2, D_FF, D_MODEL), D_FF ** -0.5),
        "even_w_in": nrm((N_EVEN, D_MODEL, E_IN), D_MODEL ** -0.5),
        "gla_w_alpha_up": nrm((N_EVEN, R_A, A_QK), R_A ** -0.5),
        "gla_b_alpha": nrm((N_EVEN, A_QK), 0.1),
        "gla_norm_g": 1.0 + nrm((N_EVEN, DV_A), 0.05),
        "band_rel_bias": nrm((N_EVEN, H_B, 2 * MAX_REL + 1), 0.5),
        "even_w_out": nrm((N_EVEN, A_V + B_W, D_MODEL), (A_V + B_W) ** -0.5),
        "odd_w_in": nrm((N_ODD, D_MODEL, O_IN), D_MODEL ** -0.5),
        "fox_b_f": FOX_BIAS_INIT + nrm((N_ODD, H_C), 0.1),
        "odd_w_out": nrm((N_ODD, C_W, D_MODEL), C_W ** -0.5),
        "final_norm_g": 1.0 + nrm((D_MODEL,), 0.05),
    }

def reference(x_prompt, x_sample, state_gla, cache_band_k, cache_band_v, cache_fox_k, cache_fox_v,
              cache_fox_logf, norm_g, ffn_w_gu, ffn_w_down, even_w_in, gla_w_alpha_up, gla_b_alpha,
              gla_norm_g, band_rel_bias, even_w_out, odd_w_in, fox_b_f, odd_w_out, final_norm_g):
    weights = (norm_g, ffn_w_gu, ffn_w_down, even_w_in, gla_w_alpha_up, gla_b_alpha, gla_norm_g,
               band_rel_bias, even_w_out, odd_w_in, fox_b_f, odd_w_out, final_norm_g)
    sample_states = []
    for l in range(DEPTH):
        i = l // 2
        if l % 2 == 0:
            sample_states.append((state_gla[i], cache_band_k[i], cache_band_v[i]))
        else:
            sample_states.append((cache_fox_k[i], cache_fox_v[i], cache_fox_logf[i]))
    y_prompt, ns_p = trunk(x_prompt, None, *weights)
    y_sample, ns_s = trunk(x_sample, sample_states, *weights)
    ev = range(0, DEPTH, 2)
    od = range(1, DEPTH, 2)
    p_state_gla = jnp.stack([ns_p[l][0] for l in ev])
    p_band_k = jnp.stack([ns_p[l][1] for l in ev])
    p_band_v = jnp.stack([ns_p[l][2] for l in ev])
    p_fox_k = jnp.stack([ns_p[l][0] for l in od])
    p_fox_v = jnp.stack([ns_p[l][1] for l in od])
    p_fox_logf = jnp.stack([ns_p[l][2] for l in od])
    s_state_gla = jnp.stack([ns_s[l][0] for l in ev])
    s_band_k = jnp.stack([ns_s[l][1] for l in ev])
    s_band_v = jnp.stack([ns_s[l][2] for l in ev])
    s_fox_k = jnp.stack([ns_s[l][0] for l in od])
    s_fox_v = jnp.stack([ns_s[l][1] for l in od])
    s_fox_logf = jnp.stack([ns_s[l][2] for l in od])
    return (y_prompt, y_sample, p_state_gla, p_band_k, p_band_v, p_fox_k, p_fox_v, p_fox_logf,
            s_state_gla, s_band_k, s_band_v, s_fox_k, s_fox_v, s_fox_logf)


_drawn_inputs = setup_inputs


def setup_inputs(seed=0):
    import zlib

    import numpy as np

    out = dict(_drawn_inputs(seed))
    spreads = {}
    factors = {}
    for name, (base, spread) in spreads.items():
        noise = np.random.default_rng([zlib.crc32(name.encode()), seed]).standard_normal(out[name].shape)
        drawn = base * np.exp(spread * noise) if base else spread * noise
        out[name] = __import__('jax').numpy.asarray(drawn.astype(out[name].dtype))
    for name, factor in factors.items():
        out[name] = (out[name] * factor).astype(out[name].dtype)
    return out
```

```python
import numpy as np
import concourse.bass as bass
from concourse import mybir
from contextlib import ExitStack

F32 = mybir.dt.float32
F32R = mybir.dt.float32r
BF16 = mybir.dt.bfloat16
I32 = mybir.dt.int32
ALU = mybir.AluOpType
ACT = mybir.ActivationFunctionType

P = 128
D_MODEL, SEQ, DEC_BATCH, DEC_SEQ, PAST = 1024, 512, 8, 16, 1024
T = SEQ + DEC_BATCH * DEC_SEQ
TT = T // P
KT = D_MODEL // P
HALF = T // 2
D_FF = 2816
FF_A = 12
FF_B = D_FF // P - FF_A
CHUNK, WIN = 64, 512
H_A, DK, DV = 4, 64, 128
R_A = 16
H_B, H_C, DH = 8, 16, 64
SCALE = DH ** -0.5
EPS = 1e-6
SLAB = 16 * P
NEG = -1e30
LOWEST = -3e38
RSQRT_SEED = 1597463007.0

FFN_SLABS = FF_A + KT + FF_B + KT
FFN_UNITS = 2 * FF_A + KT + 2 * FF_B + KT
IN_SLABS = 8
TOK_SLABS = 4
OUT_SLABS = 4
MIX_SLABS = 1 + IN_SLABS + TOK_SLABS + OUT_SLABS
NORM_UNITS = 4
IN_UNITS = 4 + 2 * IN_SLABS + 4 * TOK_SLABS
OUT_UNITS = KT
SQ_STEPS = KT + 1


def plan():
    out, slab, unit, norm = [], 0, 0, 0
    for kind, index in (("ffn", 0), ("even", 0), ("ffn", 1), ("ffn", 2), ("odd", 0), ("ffn", 3)):
        out.append(dict(kind=kind, index=index, slab=slab, unit=unit, norm=norm))
        slab += FFN_SLABS if kind == "ffn" else MIX_SLABS
        unit += NORM_UNITS + (FFN_UNITS if kind == "ffn" else IN_UNITS + OUT_UNITS)
        norm += 1
    return out, slab, unit, norm


def trunk_program(nc, ins, outs):
    PLAN, SLABS, UNITS, NORMS = plan()
    ctx = ExitStack()

    base = (nc.sbuf_base + 63) // 64 * 64
    kib = 1024
    at_x = base
    at_xn = at_x + KT * T * 4
    at_w = at_xn + 2 * KT * T * 4
    at_h = at_w + 6 * SLAB * 4
    at_g = at_h + 2 * FF_A * T * 4
    at_acc = at_g + 4 * T * 4
    at_c = at_acc + T * 4

    def place(name, shape, dt, at):
        return nc.alloc_sbuf_tensor_at(name, shape, dt, offset=at)

    x_res = place("x_res", [P, KT, T], F32, at_x)
    xn_hi = place("xn_hi", [P, KT, T], F32R, at_xn)
    xn_lo = place("xn_lo", [P, KT, T], F32R, at_xn + KT * T * 4)
    y_out = place("y_out", [P, KT, T], F32, at_xn)
    w_raw = place("w_raw", [P, 2, SLAB], F32, at_w)
    w_hi = place("w_hi", [P, 2, SLAB], F32R, at_w + 2 * SLAB * 4)
    w_lo = place("w_lo", [P, 2, SLAB], F32R, at_w + 4 * SLAB * 4)
    h_hi = place("h_hi", [P, FF_A, T], F32R, at_h)
    h_lo = place("h_lo", [P, FF_A, T], F32R, at_h + FF_A * T * 4)
    gate = place("gate", [P, 2, T], F32, at_g)
    prod = place("prod", [P, 2, T], F32, at_g + 2 * T * 4)
    sq_sum = place("sq_sum", [P, T], F32, at_acc)

    c_at = [at_c]

    def const(name, shape, dt=F32):
        size = int(np.prod(shape[1:])) * (2 if dt == BF16 else 4)
        t = place(name, shape, dt, c_at[0])
        c_at[0] += (size + 31) // 32 * 32
        return t

    ident = const("ident", [P, P])
    ones = const("ones", [P, P])
    mean_model = const("mean_model", [P, 1])
    mean_head = const("mean_head", [P, 1])
    gains = const("gains", [P, (NORMS + 1) * KT])
    cum64 = const("cum64", [P, P])
    cum16 = const("cum16", [P, P])
    keep64 = const("keep64", [P, P])
    keep16 = const("keep16", [P, P])
    own_rows = const("own_rows", [P, DEC_BATCH])
    w_alpha = const("w_alpha", [R_A + 1, H_A * DK])
    head_gain = const("head_gain", [P, 1])
    bias_f = const("bias_f", [H_C, 1])
    ident_b = const("ident_b", [P, P], BF16)
    causal_b = const("causal_b", [P, P], BF16)
    own_causal_b = const("own_causal_b", [P, 240], BF16)
    causal = place("causal", [P, P], F32, at_g + 2 * T * 4)
    own_causal = place("own_causal", [P, 240], F32, at_g + 2 * T * 4 + P * 4)
    rs = [const(f"rs{i}", [P, 20]) for i in range(4)]
    neg_max = const("neg_max", [P, 8])
    row_sum = const("row_sum", [P, 8])
    row_inv = const("row_inv", [P, 8])
    row_max = const("row_max", [P, 8])
    mark = const("mark", [P, 1])
    marks = const("marks", [P, 8])
    chunk_last = const("chunk_last", [P, 2, 16])
    at_e = (c_at[0] + 63) // 64 * 64
    end = nc.sbuf_usable_end

    tile_b = T * 4
    qa = place("qa", [P, 2, T], F32, at_h)
    ka = place("ka", [P, 2, T], F32, at_h + 2 * tile_b)
    ag = place("ag", [P, 4, T], F32, at_h + 4 * tile_b)
    va = place("va", [P, TT, 512], F32, at_h + 8 * tile_b)
    qb = place("qb", [P, 4, T], F32, at_h + 12 * tile_b)
    kb = place("kb", [P, 4, T], F32, at_h + 16 * tile_b)
    vb = place("vb", [P, TT, 512], F32, at_h + 20 * tile_b)
    ls_tmp = place("ls_tmp", [P, TT * 256], F32, at_g)
    decay = place("decay", [P, 2, T], F32, at_g)
    o_head = place("o_head", [P, H_A, T], F32, at_g)
    ar = place("ar", [R_A + 1, T], F32, at_e)
    log_a = place("log_a", [P, TT * 256], F32, at_e + tile_b)
    e_cum = place("e_cum", [P, 2, T], F32, at_e + 3 * tile_b)
    qa1 = place("qa1", [P, 2, T], F32, at_e + tile_b)
    k_in = place("k_in", [P, 2, T], F32, at_e + 5 * tile_b)
    assert at_e + 7 * tile_b <= end
    sq_head = place("sq_head", [P, T], F32, at_e)
    diag_a = place("diag_a", [P, TT, P], F32, at_e + tile_b)
    o_tmp = place("o_tmp", [P, T], F32, at_e + 2 * tile_b)
    att = place("att", [P, TT, 512], F32, at_xn)
    k_own = place("k_own", [P, DEC_BATCH, 256], F32, at_xn + 10240)
    s_hist = place("s_hist", [P, 9, 2, P], F32, at_xn + 18432)
    k_tok = place("k_tok", [P, TT, 256], F32, at_xn + 27648)
    s_dec = place("s_dec", [P, DEC_BATCH, 2, P], F32, at_xn + 32768)
    qz = place("qz", [P, 2, SEQ], F32, at_g)
    p_pt = place("p_pt", [P, 2, SEQ], F32, at_g + 4096)
    p_o = place("p_o", [P, 2, P], F32, at_g + 8192)
    p_s = place("p_s", [P, 3, SEQ], F32, at_e)
    p_bias = place("p_bias", [P, 2, 2, SEQ], F32, at_e + 6144)
    assert at_e + 6144 + 8192 <= end
    dead = at_h
    kc_b = place("kc_b", [P, 2, 4, WIN], F32, dead)
    vc_b0 = place("vc_b0", [P, 4, 512], F32, dead + 16384)
    sb_bias = place("sb_bias", [P, 2, 640], F32, dead + 24576)
    vc_b1 = place("vc_b1", [P, 4, 512], F32, at_e)
    sb_s = place("sb_s", [P, 640], F32, at_e + 8192)
    sb_pt = place("sb_pt", [P, 640], F32, at_e + 8192 + 2560)
    qz_s = place("qz_s", [P, 2, 4, 32], F32, at_g)
    s_o = place("s_o", [P, P], F32, at_g + 1024)
    qc = place("qc", [P, KT, T], F32, at_h)
    kc = place("kc", [P, KT, T], F32, at_h + KT * tile_b)
    vc = place("vc", [P, TT, D_MODEL], F32, at_h + 2 * KT * tile_b)
    clf = place("clf", [P, 8, P], F32, at_xn)
    after_w = place("after_w", [P, 1024], F32, at_xn + 4096)
    upto_w = place("upto_w", [P, SEQ], F32, at_xn + 8192)
    c_after = place("c_after", [P, 1024], F32, at_xn + 12288)
    lf = place("lf", [H_C, T], F32, at_xn + 16384)
    lf_tmp = place("lf_tmp", [H_C, T], F32, at_xn + 16384 + tile_b)
    lf_tok = place("lf_tok", [P, TT, H_C], F32, at_xn + 16384 + 2 * tile_b)
    neg_f = place("neg_f", [H_C, T], F32, at_xn + 16384 + 3 * tile_b)
    logit = place("logit", [H_C, T], F32, at_g)
    v_extra = place("v_extra", [P, 8, 512], F32, at_e)
    sf_bias = place("sf_bias", [P, 1152], F32, at_g + 1536)
    sf_s = place("sf_s", [P, 1152], F32, at_g + 1536 + 4608)
    sf_pt = place("sf_pt", [P, 1152], F32, at_e + 16384)
    assert at_e + 16384 + 4608 <= end and at_g + 1536 + 2 * 4608 <= at_c, (at_e, end)

    ps = ctx.enter_context(nc.psum_tensor("ps", [P, 8, 512], F32))

    def unit_ap(u):
        return ps[:, 2 * u:2 * u + 2, 0:HALF]

    def flat(bank, n, cols):
        return ps[:, bank:bank + n, :].rearrange("p b c -> p (b c)")[:, 0:cols]

    def halves(ap):
        return ap.rearrange("p (a c) -> p a c", a=2)

    def tile_of(t, j):
        if isinstance(j, int):
            return halves(t[:, j, :])
        return t[:, bass.ds(j, 1), :].rearrange("p o (a c) -> p (o a) c", a=2)

    def row_of(t, j, lo=0, hi=None):
        if isinstance(j, int):
            return t[:, j, lo:hi]
        return t[:, bass.ds(j, 1), lo:hi].rearrange("p o c -> p (o c)")

    made = {}

    def sem(name):
        if name not in made:
            made[name] = ctx.enter_context(nc.semaphore(name))
        return made[name]

    x_loaded, consts_loaded = sem("x_loaded"), sem("consts_loaded")
    raw_loaded = [sem("raw_loaded0"), sem("raw_loaded1")]
    hi_done, lo_done = sem("hi_done"), sem("lo_done")
    unit_ready, unit_free = sem("unit_ready"), sem("unit_free")
    silu_done, h_hi_done, h_lo_done = sem("silu_done"), sem("h_hi_done"), sem("h_lo_done")
    sq_done, acc_done = sem("sq_done"), sem("acc_done")
    rs_step, diag_done = sem("rs_step"), sem("diag_done")
    xf_done, xn_hi_done, xn_lo_done = sem("xf_done"), sem("xn_hi_done"), sem("xn_lo_done")
    y_stored, masks_cast = sem("y_stored"), sem("masks_cast")

    def slab_src(ph, kind, s):
        k = ph["index"]
        mix = 0 if ph["kind"] == "even" else 1
        src = {"up_a": ins["w_up"][k], "down_a": ins["w_down_a"][k], "up_b": ins["w_up"][k],
               "down_b": ins["w_down_b"][k], "in": ins["w_in"][mix], "out": ins["w_out"][mix]}[kind]
        return src[bass.ds(s, 1)].rearrange("o p c -> p (o c)"), src.shape[2]

    def load_slabs(sp, ph, kind, first, count, n0, fresh=0):
        def one(s, n, slot):
            src, width = slab_src(ph, kind, s)
            sp.wait_ge(lo_done, n - 1)
            sp.dma_start(w_raw[:, slot, 0:width], src).then_inc(raw_loaded[slot], 16)
        for s in range(fresh):
            src, width = slab_src(ph, kind, first + s)
            sp.dma_start(w_raw[:, (n0 + s) % 2, 0:width], src).then_inc(raw_loaded[(n0 + s) % 2], 16)
        with sp.Fori(fresh // 2, count // 2) as i:
            for u in range(2):
                one(first + 2 * i + u, n0 + 2 * i + u, (n0 + u) % 2)

    def small_load(sp, ph):
        n = ph["slab"]
        sp.wait_ge(lo_done, n - 1)
        dst = w_raw[:, n % 2, 0:KT * P].rearrange("p (k c) -> p k c", c=P)[:, :, 0:R_A]
        sp.dma_start(dst, ins["w_small"][0 if ph["kind"] == "even" else 1]).then_inc(raw_loaded[n % 2], 16)

    def hi_next(i, step, u, n0, units_before):
        slot = (n0 + u + 1) % 2
        first_loads = (n0 + u + 1 - slot) // 2 + 1
        nc.scalar.wait_ge(raw_loaded[slot], (i * (step // 2) + first_loads) * 16)
        nc.scalar.wait_ge(unit_ready, units_before)
        nc.scalar.activation(w_hi[:, slot, :], w_raw[:, slot, :], ACT.Copy).then_inc(hi_done, 1)

    def lo_next(pool, n, slot):
        pool.wait_ge(hi_done, n + 1)
        nc.gpsimd.tensor_tensor(out=w_lo[:, slot, :], in0=w_raw[:, slot, :], in1=w_hi[:, slot, :].bitcast(F32),
                                op=ALU.subtract).then_inc(lo_done, 1)

    def mm_tile(unit, slot, tile0, kts, a_hi, a_lo, before_k=None):
        last = None
        for k in range(kts):
            if before_k:
                before_k(k)
            w = (tile0 + k) * P
            terms = [(w_hi, a_hi), (w_hi, a_lo), (w_lo, a_hi)]
            for t, (w_part, a_part) in enumerate(terms):
                for half in range(2):
                    last = nc.tensor.matmul(ps[:, 2 * unit + half, 0:HALF], w_part[:, slot, w:w + P],
                                            a_part[:, k, half * HALF:(half + 1) * HALF],
                                            start=k == 0 and t == 0, stop=k == kts - 1 and t == 2)
        return last

    def pe_slab_start(pe, n):
        pe.wait_ge(lo_done, n + 1)

    RS_OPS = 2 + 3 * 3

    def rs_chain(dve, src, cols, done0, scale=None):
        ms, y, a, b = (t[:, 0:cols] for t in rs)
        nc.vector.tensor_scalar(out=ms, in0=src, scalar1=EPS, scalar2=None, op0=ALU.add).then_inc(rs_step, 1)
        dve.wait_ge(rs_step, done0 + 1)
        nc.vector.tensor_scalar(out=y.bitcast(I32), in0=ms.bitcast(I32), scalar1=-0.5, scalar2=RSQRT_SEED,
                                op0=ALU.mult, op1=ALU.add).then_inc(rs_step, 1)
        n = done0 + 2
        for _ in range(3):
            dve.wait_ge(rs_step, n)
            nc.vector.tensor_tensor(out=a, in0=y, in1=y, op=ALU.mult).then_inc(rs_step, 1)
            dve.wait_ge(rs_step, n + 1)
            nc.vector.scalar_tensor_tensor(out=b, in0=a, scalar=-0.5, in1=ms, op0=ALU.mult,
                                           op1=ALU.mult).then_inc(rs_step, 1)
            dve.wait_ge(rs_step, n + 2)
            nc.vector.scalar_tensor_tensor(out=y, in0=b, scalar=1.5, in1=y, op0=ALU.add,
                                           op1=ALU.mult).then_inc(rs_step, 1)
            n += 3

    RS_NORM0 = {}
    at = 0
    for r in range(NORMS + 1):
        RS_NORM0[r] = at
        at += RS_OPS
        if r < len(PLAN) and PLAN[r]["kind"] == "even":
            RS_NORM0["gla"] = at
            at += RS_OPS
    DIAG0 = {}
    at = 0
    for r in range(NORMS + 1):
        DIAG0[r] = at
        at += TT
        if r < len(PLAN) and PLAN[r]["kind"] == "even":
            DIAG0["gla"] = at
            at += TT * H_A

    XN0 = {}
    at = 0
    for r in range(NORMS + 1):
        XN0[r] = at
        at += KT

    def norm_pe(pe, r, q0):
        pe.wait_ge(acc_done, SQ_STEPS * (r + 1))
        pe.wait_ge(unit_free, q0)
        for tt in range(TT):
            last = nc.tensor.matmul(ps[:, 0, tt:tt + 1], sq_sum[:, tt * P:(tt + 1) * P], mean_model[:, :],
                                    start=True, stop=True)
        last.then_inc(unit_ready, 1)
        pe.wait_ge(diag_done, DIAG0[r] + TT)
        for tt in range(TT):
            last = nc.tensor.matmul(ps[:, 2 + tt // 4, (tt % 4) * P:(tt % 4 + 1) * P], ones[:, :],
                                    gate[:, 0, tt * P:(tt + 1) * P], start=True, stop=True)
        last.then_inc(unit_ready, 3)

    def release(units):
        nc.vector.memset(mark[:, 0:1], 0.0).then_inc(unit_free, units)

    def norm_dve(dve, r, q0, final=False):
        dve.wait_ge(unit_ready, q0 + 1)
        rs_chain(dve, ps[:, 0, 0:TT], TT, RS_NORM0[r])
        dve.wait_ge(rs_step, RS_NORM0[r] + RS_OPS)
        release(1)
        for tt in range(TT):
            nc.vector.tensor_scalar(out=gate[:, 0, tt * P:(tt + 1) * P], in0=ident[:, :],
                                    scalar1=rs[1][:, tt:tt + 1], scalar2=None,
                                    op0=ALU.mult).then_inc(diag_done, 1)
        dve.wait_ge(unit_ready, q0 + 4)
        if r == 0:
            dve.wait_ge(masks_cast, 3)
        for k in range(KT):
            if final:
                dst = y_out[:, k, :]
            else:
                dst = prod[:, k % 2, :]
                if k >= 2:
                    dve.wait_ge(xn_lo_done, XN0[r] + k - 1)
            ins_ = nc.vector.scalar_tensor_tensor(out=dst, in0=x_res[:, k, :],
                                                  scalar=gains[:, r * KT + k:r * KT + k + 1],
                                                  in1=flat(2, 2, T), op0=ALU.mult, op1=ALU.mult)
            ins_.then_inc(xf_done, 1)
        dve.wait_ge(xf_done, XN0[r] + KT)
        release(NORM_UNITS - 1)

    def norm_act(act, r):
        for k in range(KT):
            act.wait_ge(xf_done, XN0[r] + k + 1)
            nc.scalar.activation(xn_hi[:, k, :], prod[:, k % 2, :], ACT.Copy).then_inc(xn_hi_done, 1)

    def norm_pool(pool, r):
        for k in range(KT):
            pool.wait_ge(xn_hi_done, XN0[r] + k + 1)
            nc.gpsimd.tensor_tensor(out=xn_lo[:, k, :], in0=prod[:, k % 2, :], in1=xn_hi[:, k, :].bitcast(F32),
                                    op=ALU.subtract).then_inc(xn_lo_done, 1)

    def add_dve(dve, m, q, u, coef, sq, sq_base):
        dve.wait_ge(unit_ready, q + 1)
        nc.vector.scalar_tensor_tensor(out=tile_of(x_res, m), in0=unit_ap(u), scalar=coef, in1=tile_of(x_res, m),
                                       op0=ALU.mult, op1=ALU.add).then_inc(unit_free, 1)
        if sq:
            acc_dve(dve, m, u, sq_base)

    def acc_dve(dve, m, u, sq_base):
        r_sq, r_acc = sq_base
        dve.wait_ge(sq_done, r_sq + m + 1)
        dve.wait_ge(acc_done, r_acc + 1 + m)
        nc.vector.tensor_tensor(out=sq_sum[:, :], in0=sq_sum[:, :], in1=gate[:, u % 2, :],
                                op=ALU.add).then_inc(acc_done, 1)

    def sq_act(act, m, u, sq_base):
        r_sq, r_acc = sq_base
        if isinstance(m, int):
            if m >= 2:
                act.wait_ge(acc_done, r_acc + m)
        else:
            act.wait_ge(acc_done, r_acc + m)
        nc.scalar.activation(gate[:, u % 2, :], row_of(x_res, m), ACT.Square).then_inc(sq_done, 1)

    def clear_sum(dve, r, after):
        nc.vector.memset(sq_sum[:, :], 0.0).then_inc(acc_done, 1)

    def ffn_segments(ph):
        q = ph["unit"] + NORM_UNITS
        n = ph["slab"]
        segs = []
        for kind, count, per in (("up_a", FF_A, 2), ("down_a", KT, 1), ("up_b", FF_B, 2), ("down_b", KT, 1)):
            segs.append((kind, count, per, n, q))
            n += count
            q += count * per
        return segs

    def ffn_pe(pe, ph):
        f = ph["index"]
        norm_pe(pe, ph["norm"], ph["unit"])
        h0 = f * (FF_A + FF_B)
        for kind, count, per, n0, q0 in ffn_segments(ph):
            if kind.startswith("up"):
                def body(s, u):
                    pe_slab_start(pe, s + n0)
                    for part in range(2):
                        un = (q0 + 2 * u + part) % 4
                        pe.wait_ge(unit_free, s * 2 + (q0 + part - 3))
                        before = (lambda k: pe.wait_ge(xn_lo_done, XN0[ph["norm"]] + k + 1)) if part == 0 else None
                        mm_tile(un, (n0 + u) % 2, part * KT, KT, xn_hi, xn_lo, before).then_inc(unit_ready, 1)
                with pe.Fori(0, count // 2) as i:
                    for u in range(2):
                        body(i * 2 + u, u)
            else:
                kts = FF_A if kind == "down_a" else FF_B
                hb = h0 + (0 if kind == "down_a" else FF_A)
                with pe.Fori(0, count // 4) as i:
                    for u in range(4):
                        s = i * 4 + u
                        pe_slab_start(pe, s + n0)
                        pe.wait_ge(unit_free, s + (q0 - 3))
                        mm_tile((q0 + u) % 4, (n0 + u) % 2, 0, kts, h_hi, h_lo,
                                lambda k: pe.wait_ge(h_lo_done, hb + k + 1)).then_inc(unit_ready, 1)

    def ffn_act(act, ph):
        f = ph["index"]
        norm_act(act, ph["norm"])
        h0 = f * (FF_A + FF_B)
        last_ph = ph is PLAN[-1]
        for kind, count, per, n0, q0 in ffn_segments(ph):
            if kind.startswith("up"):
                hb = h0 + (0 if kind == "up_a" else FF_A)
                with act.Fori(0, count // 2) as i:
                    for u in range(2):
                        s = i * 2 + u
                        hi_next(i, 2, u, n0, s * 2 + q0)
                        act.wait_ge(unit_ready, s * 2 + (q0 + 1))
                        act.wait_ge(unit_free, s * 2 + (q0 - 2))
                        nc.scalar.activation(halves(gate[:, u, :]), unit_ap((q0 + 2 * u) % 4),
                                             ACT.Silu).then_inc(silu_done, 1)
                        act.wait_ge(unit_free, s * 2 + (q0 + 2))
                        nc.scalar.activation(row_of(h_hi, s), prod[:, u, :], ACT.Copy).then_inc(h_hi_done, 1)
            else:
                sq = kind == "down_b"
                r = ph["norm"] + 1
                def body(i, u, step, nxt=True):
                    s = i * step + u
                    if nxt:
                        hi_next(i, step, u, n0, s + q0)
                    if sq:
                        act.wait_ge(unit_free, s + (q0 + 1))
                        sq_act(act, s, u, (KT * r, SQ_STEPS * r))
                if last_ph and kind == "down_b":
                    for s in range(count):
                        body(0, s, 8, s < count - 1)
                else:
                    with act.Fori(0, count // 4) as i:
                        for u in range(4):
                            body(i, u, 4)

    def ffn_pool(pool, ph):
        f = ph["index"]
        norm_pool(pool, ph["norm"])
        h0 = f * (FF_A + FF_B)
        for kind, count, per, n0, q0 in ffn_segments(ph):
            last = ph is PLAN[-1] and kind == "down_b"
            if last:
                for s in range(count - 1):
                    lo_next(pool, n0 + s + 1, (n0 + s + 1) % 2)
                continue
            hb = h0 + (0 if kind == "up_a" else FF_A)
            with pool.Fori(0, count // 2) as i:
                for u in range(2):
                    s = i * 2 + u
                    lo_next(pool, s + (n0 + 1), (n0 + u + 1) % 2)
                    if kind.startswith("up"):
                        pool.wait_ge(h_hi_done, s + (hb + 1))
                        nc.gpsimd.tensor_tensor(out=row_of(h_lo, s), in0=prod[:, u, :],
                                                in1=row_of(h_hi, s).bitcast(F32),
                                                op=ALU.subtract).then_inc(h_lo_done, 1)

    def ffn_dve(dve, ph):
        f = ph["index"]
        norm_dve(dve, ph["norm"], ph["unit"])
        h0 = f * (FF_A + FF_B)
        for kind, count, per, n0, q0 in ffn_segments(ph):
            if kind.startswith("up"):
                hb = h0 + (0 if kind == "up_a" else FF_A)
                if kind == "up_a":
                    dve.wait_ge(xn_lo_done, XN0[ph["norm"]] + KT)
                with dve.Fori(0, count // 2) as i:
                    for u in range(2):
                        s = i * 2 + u
                        dve.wait_ge(unit_ready, s * 2 + (q0 + 2))
                        dve.wait_ge(silu_done, s + (hb + 1))
                        dve.wait_ge(h_lo_done, s + hb)
                        nc.vector.tensor_tensor(out=halves(prod[:, u, :]), in0=halves(gate[:, u, :]),
                                                in1=unit_ap((q0 + 2 * u + 1) % 4),
                                                op=ALU.mult).then_inc(unit_free, 2)
            else:
                sq = kind == "down_b"
                r = ph["norm"] + 1
                if sq:
                    clear_sum(dve, r, None)
                with dve.Fori(0, count // 4) as i:
                    for u in range(4):
                        s = i * 4 + u
                        add_dve(dve, s, s + q0, (q0 + u) % 4, 0.5, False, None)
                        if sq:
                            acc_dve(dve, s, u, (KT * r, SQ_STEPS * r))

    def mix_at(ph):
        q = ph["unit"] + NORM_UNITS
        n = ph["slab"]
        return dict(small=(n, q), fm=(n + 1, q + 4), tok=(n + 1 + IN_SLABS, q + 4 + 2 * IN_SLABS),
                    out=(n + 1 + IN_SLABS + TOK_SLABS, q + IN_UNITS))

    def proj_pe(pe, ph):
        norm_pe(pe, ph["norm"], ph["unit"])
        m = mix_at(ph)
        n0, q0 = m["small"]
        pe_slab_start(pe, n0)
        mm_tile(0, n0 % 2, 0, KT, xn_hi, xn_lo,
                lambda k: pe.wait_ge(xn_lo_done, XN0[ph["norm"]] + k + 1)).then_inc(unit_ready, 4)
        n0, q0 = m["fm"]
        with pe.Fori(0, IN_SLABS // 2) as i:
            for u in range(2):
                s = i * 2 + u
                pe_slab_start(pe, s + n0)
                for part in range(2):
                    pe.wait_ge(unit_free, s * 2 + (q0 + part - 3))
                    mm_tile(2 * u + part, (n0 + u) % 2, part * KT, KT, xn_hi, xn_lo).then_inc(unit_ready, 1)
        n0, q0 = m["tok"]
        with pe.Fori(0, TOK_SLABS // 2) as i:
            for u in range(2):
                s = i * 2 + u
                slot = (n0 + u) % 2
                pe_slab_start(pe, s + n0)
                for tt in range(TT):
                    if tt % 2 == 0:
                        pe.wait_ge(unit_free, s * 4 + (q0 + tt // 2 - 3))
                    for k in range(KT):
                        for t, (a_part, w_part) in enumerate(((xn_hi, w_hi), (xn_hi, w_lo), (xn_lo, w_hi))):
                            last = nc.tensor.matmul(ps[:, tt, 0:256], a_part[:, k, tt * P:(tt + 1) * P],
                                                    w_part[:, slot, k * 256:(k + 1) * 256],
                                                    start=k == 0 and t == 0, stop=k == KT - 1 and t == 2)
                    if tt in (1, 3):
                        last.then_inc(unit_ready, 1)
                    elif tt == 4:
                        last.then_inc(unit_ready, 2)

    def out_pe(pe, ph, ready):
        n0, q0 = mix_at(ph)["out"]
        ready(pe)
        with pe.Fori(0, OUT_SLABS // 2) as i:
            for u in range(2):
                s = i * 2 + u
                pe_slab_start(pe, s + n0)
                for part in range(2):
                    pe.wait_ge(unit_free, s * 2 + (q0 + part - 3))
                    mm_tile(2 * u + part, (n0 + u) % 2, part * KT, KT, xn_hi, xn_lo).then_inc(unit_ready, 1)

    def proj_act(act, ph):
        norm_act(act, ph["norm"])
        m = mix_at(ph)
        n0, q0 = m["small"]
        hi_next(0, 2, 0, n0, q0)
        for key, count, per in (("fm", IN_SLABS, 2), ("tok", TOK_SLABS, 4)):
            n0, q0 = m[key]
            with act.Fori(0, count // 2) as i:
                for u in range(2):
                    hi_next(i, 2, u, n0, (i * 2 + u) * per + q0)

    def out_act(act, ph):
        n0, q0 = mix_at(ph)["out"]
        r = ph["norm"] + 1
        for s in range(OUT_SLABS):
            hi_next(0, 8, s, n0, q0 + 2 * s)
            for part in range(2):
                act.wait_ge(unit_free, q0 + 2 * s + part + 1)
                sq_act(act, 2 * s + part, part, (KT * r, SQ_STEPS * r))

    def proj_pool(pool, ph):
        norm_pool(pool, ph["norm"])
        n0 = ph["slab"]
        lo_next(pool, n0 + 1, (n0 + 1) % 2)
        with pool.Fori(0, (IN_SLABS + TOK_SLABS) // 2) as i:
            for u in range(2):
                lo_next(pool, i * 2 + (n0 + 2 + u), (n0 + u) % 2)

    def out_pool(pool, ph):
        n0 = mix_at(ph)["out"][0]
        with pool.Fori(0, OUT_SLABS // 2) as i:
            for u in range(2):
                lo_next(pool, i * 2 + (n0 + 1 + u), (n0 + 1 + u) % 2)

    def proj_dve(dve, ph, small, fm_tiles, tok_dst):
        norm_dve(dve, ph["norm"], ph["unit"])
        m = mix_at(ph)
        n0, q0 = m["small"]
        dve.wait_ge(unit_ready, q0 + 4)
        small()
        n0, q0 = m["fm"]
        for j, (dst, tile, scale) in enumerate(fm_tiles):
            dve.wait_ge(unit_ready, q0 + j + 1)
            nc.vector.tensor_scalar(out=halves(dst[:, tile, :]), in0=unit_ap(j % 4), scalar1=scale, scalar2=None,
                                    op0=ALU.mult).then_inc(unit_free, 1)
        n0, q0 = m["tok"]
        for s in range(TOK_SLABS):
            dst = tok_dst(s)
            for tt, n, inc in ((0, 2, 1), (2, 2, 1), (4, 1, 2)):
                dve.wait_ge(unit_ready, q0 + 4 * s + (1, 2, 4)[tt // 2])
                nc.vector.tensor_copy(dst[:, tt:tt + n, :], ps[:, tt:tt + n, 0:256]).then_inc(unit_free, inc)

    def out_dve(dve, ph):
        n0, q0 = mix_at(ph)["out"]
        r = ph["norm"] + 1
        clear_sum(dve, r, None)
        with dve.Fori(0, KT // 4) as i:
            for u in range(4):
                s = i * 4 + u
                add_dve(dve, s, s + q0, u, 1.0, True, (KT * r, SQ_STEPS * r))

    class Prompt:
        def __init__(self, tag, pairs, q, k, v, out0, bias_src, bias_cols, masked):
            self.tag, self.pairs, self.q, self.k, self.v, self.out0 = tag, pairs, q, k, v, out0
            self.bias_src, self.bias_cols, self.masked = bias_src, bias_cols, masked
            s = lambda n: sem(f"{tag}_{n}")
            self.bias_loaded = [s("bias_loaded0"), s("bias_loaded1")]
            self.qz_done, self.logits_ready, self.max_step = s("qz_done"), s("logits_ready"), s("max_step")
            self.probs_ready, self.pt_ready, self.pt_copied = s("probs_ready"), s("pt_ready"), s("pt_copied")
            self.o_ready, self.inv_done, self.o_scaled = s("o_ready"), s("inv_done"), s("o_scaled")
            self.ot_ready, self.ot_hi, self.ot_lo = s("ot_ready"), s("ot_hi"), s("ot_lo")
            self.zeroed = s("qz_zeroed")

        def sp(self, sp, ready):
            ready(sp)
            for slot in range(2):
                sp.dma_start(p_bias[:, slot], self.bias_src(slot)).then_inc(self.bias_loaded[slot], 16)
            with sp.Fori(1, self.pairs // 2) as i:
                for u in range(2):
                    sp.wait_ge(self.max_step, i * 32 + (16 * u - 16))
                    sp.dma_start(p_bias[:, u], self.bias_src(i * 2 + u)).then_inc(self.bias_loaded[u], 16)

        def pe(self, pe):
            with pe.Fori(0, self.pairs) as i:
                c = i * 8
                pe.wait_ge(self.qz_done, i * 2 + 2)

                def logits(l):
                    it, hh, n = l // 2, l % 2, P * (l // 2 + 1)
                    nc_last = nc.tensor.matmul(ps[:, l % 3, 0:n], qz[:, hh, it * P:(it + 1) * P],
                                               row_of(self.k, i, 0, n), start=True, stop=not self.masked)
                    if self.masked:
                        nc_last = nc.tensor.matmul(ps[:, l % 3, n - P:n], ident_b[:, :], causal_b[:, :],
                                                   start=False, stop=True)
                    nc_last.then_inc(self.logits_ready, 1)

                def turn(it):
                    pe.wait_ge(self.o_scaled, c + (2 * it + 2))
                    pe.wait_ge(self.ot_lo, i * 4 + it)
                    nc.tensor.transpose(ps[:, 7, (it % 2) * P:(it % 2 + 1) * P], p_o[:, it % 2, :],
                                        ident[:, :]).then_inc(self.ot_ready, 1)

                logits(0)
                logits(1)
                for l in range(8):
                    it = l // 2
                    if l + 2 < 8:
                        logits(l + 2)
                    pe.wait_ge(self.probs_ready, c + (l + 1))
                    for jt in range(it + 1):
                        last = nc.tensor.transpose(ps[:, 3 + l % 2, jt * P:(jt + 1) * P],
                                                   p_s[:, l % 3, jt * P:(jt + 1) * P], ident[:, :])
                    last.then_inc(self.pt_ready, 1)
                    if l in (2, 4, 6):
                        turn(it - 1)
                    pe.wait_ge(self.pt_copied, c + (l + 1))
                    if l >= 2:
                        pe.wait_ge(self.o_scaled, c + (l - 1))
                    for jt in range(it + 1):
                        v = self.v[:, jt, bass.ds(i * P, P)]
                        last = nc.tensor.matmul(ps[:, 5 + l % 2, 0:P], p_pt[:, l % 2, jt * P:(jt + 1) * P], v,
                                                start=jt == 0, stop=jt == it)
                    last.then_inc(self.o_ready, 1)
                turn(3)

        def act(self, act):
            act.wait_ge(self.zeroed, 1)
            with act.Fori(0, self.pairs) as i:
                c = i * 8
                act.wait_ge(self.logits_ready, c)
                for hh in range(2):
                    rows = slice(64 * hh, 64 * hh + 64)
                    src = self.q[rows, bass.ds(i, 1), 0:SEQ].rearrange("p o c -> p (o c)")
                    nc.scalar.activation(qz[rows, hh, :], src, ACT.Copy).then_inc(self.qz_done, 1)

                def exps(l):
                    n = P * (l // 2 + 1)
                    act.wait_ge(self.max_step, (c + (l + 1)) * 2)
                    nc.scalar.activation(p_s[:, l % 3, 0:n], p_s[:, l % 3, 0:n], ACT.Exp, bias=neg_max[:, l:l + 1],
                                         accum_out=row_sum[:, l:l + 1]).then_inc(self.probs_ready, 1)

                def out_hi(it):
                    act.wait_ge(self.ot_ready, i * 4 + (it + 1))
                    dst = row_of(xn_hi, i + self.out0, it * P, (it + 1) * P)
                    nc.scalar.activation(dst, ps[:, 7, (it % 2) * P:(it % 2 + 1) * P],
                                         ACT.Copy).then_inc(self.ot_hi, 1)

                exps(0)
                for l in range(8):
                    n = P * (l // 2 + 1)
                    if l + 1 < 8:
                        exps(l + 1)
                    act.wait_ge(self.pt_ready, c + (l + 1))
                    nc.scalar.activation(p_pt[:, l % 2, 0:n], ps[:, 3 + l % 2, 0:n],
                                         ACT.Copy).then_inc(self.pt_copied, 1)
                    if l in (2, 4, 6):
                        out_hi(l // 2 - 1)
                out_hi(3)

        def dve(self, dve):
            nc.vector.memset(qz[:, :, :], 0.0).then_inc(self.zeroed, 1)
            with dve.Fori(0, self.pairs // 2) as ii:
                for par in range(2):
                    i = ii * 2 + par
                    c = i * 8

                    def maxes(l):
                        it, hh, n = l // 2, l % 2, P * (l // 2 + 1)
                        if l == 0:
                            dve.wait_ge(self.bias_loaded[par], ii * 16 + 16)
                        dve.wait_ge(self.logits_ready, c + (l + 1))
                        nc.vector.memset(marks[:, l:l + 1], 0.0)
                        b0 = self.bias_cols(it)
                        nc.vector.tensor_tensor_reduce(
                            out=p_s[:, l % 3, 0:n], in0=p_bias[:, par, hh, b0:b0 + n], in1=ps[:, l % 3, 0:n],
                            scale=1.0, scalar=LOWEST, op0=ALU.add, op1=ALU.max,
                            accum_out=row_max[:, l:l + 1]).then_inc(self.max_step, 1)
                        dve.wait_ge(self.max_step, (c + l) * 2 + 1)
                        nc.vector.tensor_scalar(out=neg_max[:, l:l + 1], in0=row_max[:, l:l + 1], scalar1=-1.0,
                                                scalar2=None, op0=ALU.mult).then_inc(self.max_step, 1)

                    def out_lo(it):
                        dve.wait_ge(self.ot_hi, i * 4 + (it + 1))
                        cols = (it * P, (it + 1) * P)
                        nc.vector.tensor_tensor(out=row_of(xn_lo, i + self.out0, *cols),
                                                in0=ps[:, 7, (it % 2) * P:(it % 2 + 1) * P],
                                                in1=row_of(xn_hi, i + self.out0, *cols).bitcast(F32),
                                                op=ALU.subtract).then_inc(self.ot_lo, 1)

                    maxes(0)
                    maxes(1)
                    for l in range(8):
                        it, hh = l // 2, l % 2
                        if l + 2 < 8:
                            maxes(l + 2)
                        if l in (2, 4, 6):
                            out_lo(it - 1)
                        dve.wait_ge(self.probs_ready, c + (l + 1))
                        nc.vector.reciprocal(row_inv[:, l:l + 1], row_sum[:, l:l + 1]).then_inc(self.inv_done, 1)
                        dve.wait_ge(self.inv_done, c + (l + 1))
                        dve.wait_ge(self.o_ready, c + (l + 1))
                        nc.vector.tensor_scalar(out=p_o[:, it % 2, 64 * hh:64 * hh + 64],
                                                in0=ps[:, 5 + l % 2, 64 * hh:64 * hh + 64],
                                                scalar1=row_inv[:, l:l + 1], scalar2=None,
                                                op0=ALU.mult).then_inc(self.o_scaled, 1)
                    out_lo(3)

    class Sample:
        def __init__(self, tag, cached, q, k, v, kcache, vcache, bias, s_buf, pt_buf, out0, groups, masked):
            self.tag, self.cached, self.q, self.k, self.v = tag, cached, q, k, v
            self.kcache, self.vcache, self.bias = kcache, vcache, bias
            self.s_buf, self.pt_buf, self.out0, self.groups, self.masked = s_buf, pt_buf, out0, groups, masked
            self.cols = cached + P
            s = lambda n: sem(f"{tag}_{n}")
            self.k_loaded = [s("k_loaded0"), s("k_loaded1")]
            self.v_loaded = [s("v_loaded0"), s("v_loaded1")]
            self.bias_loaded = [s("sbias_loaded0"), s("sbias_loaded1")]
            self.qz_done, self.logits_ready, self.max_step = s("sqz_done"), s("slogits_ready"), s("smax_step")
            self.probs_ready, self.pt_ready, self.pt_copied = s("sprobs_ready"), s("spt_ready"), s("spt_copied")
            self.o_ready, self.inv_done, self.o_scaled = s("so_ready"), s("sinv_done"), s("so_scaled")
            self.ot_ready, self.ot_hi, self.ot_lo = s("sot_ready"), s("sot_hi"), s("sot_lo")
            self.zeroed = s("sqz_zeroed")
            self.loops = DEC_BATCH * groups // 2

        def where(self, i, u):
            return (i, u) if self.groups == 2 else (i * 2 + u, 0)

        def sp(self, sp, ready, load):
            ready(sp)
            for u in range(2):
                load(sp, 0, u, True)
            with sp.Fori(1, self.loops) as i:
                for u in range(2):
                    load(sp, i, u, False)

        def pe(self, pe):
            tiles = self.cached // P + 1
            with pe.Fori(0, self.loops) as i:
                def logits(u):
                    b, g = self.where(i, u)
                    pe.wait_ge(self.k_loaded[u], i * 16 + 16)
                    pe.wait_ge(self.qz_done, i * 4 + (2 * u + 2))
                    for c0 in range(0, self.cached, 512):
                        for p in range(4):
                            nc.tensor.matmul(ps[32 * p:32 * p + 32, c0 // 512, 0:512], qz_s[:, u, p, :],
                                             self.kcache(u, p, c0), start=True, stop=True)
                    bank = self.cached // 512
                    if self.masked:
                        nc.tensor.matmul(ps[:, bank, 0:P], ident_b[:, :],
                                         own_causal_b[:, bass.ds(112 - b * DEC_SEQ, P)], start=True, stop=False)
                    for p in range(4):
                        last = nc.tensor.matmul(ps[32 * p:32 * p + 32, bank, 0:P], qz_s[:, u, p, :],
                                                self.k[:, 4 * g + p, SEQ:T], start=not self.masked, stop=True)
                    last.then_inc(self.logits_ready, 1)

                def turn_probs(u):
                    pe.wait_ge(self.probs_ready, i * 2 + (u + 1))
                    for jt in range(tiles):
                        last = nc.tensor.transpose(flat(3, 3, 1536)[:, jt * P:(jt + 1) * P],
                                                   self.s_buf[:, jt * P:(jt + 1) * P], ident[:, :])
                    last.then_inc(self.pt_ready, 1)

                def values(u):
                    b, g = self.where(i, u)
                    pe.wait_ge(self.pt_copied, i * 2 + (u + 1))
                    pe.wait_ge(self.v_loaded[u], i * 16 + 16)
                    for jt in range(tiles):
                        for p in range(4):
                            if jt < tiles - 1:
                                v = self.vcache(u, jt, p)
                            else:
                                v = self.v[:, TT - 1, (4 * g + p) * P:(4 * g + p + 1) * P]
                            last = nc.tensor.matmul(ps[32 * p:32 * p + 32, 6, 0:P],
                                                    self.pt_buf[:, jt * P + 32 * p:jt * P + 32 * p + 32], v,
                                                    start=jt == 0, stop=jt == tiles - 1)
                    last.then_inc(self.o_ready, 1)

                def turn_out(u):
                    pe.wait_ge(self.o_scaled, i * 2 + (u + 1))
                    pe.wait_ge(self.ot_lo, i * 4 + 2 * u)
                    nc.tensor.transpose(ps[:, 7, 0:P], s_o[:, :], ident[:, :]).then_inc(self.ot_ready, 1)

                logits(0)
                turn_probs(0)
                logits(1)
                values(0)
                turn_out(0)
                turn_probs(1)
                values(1)
                turn_out(1)

        def act(self, act):
            tiles = self.cached // P + 1
            with act.Fori(0, self.loops) as i:
                for u in range(2):
                    b, g = self.where(i, u)
                    act.wait_ge(self.max_step, i * 4 + (2 * u + 2))
                    nc.scalar.activation(self.s_buf[:, :], self.s_buf[:, :], ACT.Exp, bias=neg_max[:, u:u + 1],
                                         accum_out=row_sum[:, u:u + 1]).then_inc(self.probs_ready, 1)
                    act.wait_ge(self.pt_ready, i * 2 + (u + 1))
                    nc.scalar.activation(self.pt_buf[:, :], flat(3, 3, self.cols), ACT.Copy).then_inc(self.pt_copied, 1)
                    act.wait_ge(self.ot_ready, i * 2 + (u + 1))
                    for hh in range(2):
                        nc.scalar.activation(self.out_ap(xn_hi, b, g, hh), self.turned(hh),
                                             ACT.Copy).then_inc(self.ot_hi, 1)

        def out_ap(self, t, b, g, hh):
            return t[64 * hh:64 * hh + 64, self.out0 + 4 * g:self.out0 + 4 * g + 4,
                     bass.ds(b * DEC_SEQ + SEQ, DEC_SEQ)]

        def turned(self, hh):
            return ps[64 * hh:64 * hh + 64, 7, 0:P].rearrange("p (j h i) -> p j h i", j=4, h=2)[:, :, hh, :]

        def dve(self, dve):
            nc.vector.memset(qz_s[:, :, :, :], 0.0).then_inc(self.zeroed, 1)
            dve.wait_ge(self.zeroed, 1)
            with dve.Fori(0, self.loops) as i:
                def queries(u):
                    b, g = self.where(i, u)
                    dve.wait_ge(self.logits_ready, i * 2)
                    for hh in range(2):
                        rows = slice(64 * hh, 64 * hh + 64)
                        nc.vector.tensor_copy(qz_s[rows, u, :, 16 * hh:16 * hh + 16],
                                              self.q[rows, 4 * g:4 * g + 4, bass.ds(b * DEC_SEQ + SEQ, DEC_SEQ)]
                                              ).then_inc(self.qz_done, 1)

                queries(0)
                queries(1)
                for u in range(2):
                    b, g = self.where(i, u)
                    dve.wait_ge(self.bias_loaded[u], i * 16 * self.bias_dmas + 16 * self.bias_dmas)
                    dve.wait_ge(self.logits_ready, i * 2 + (u + 1))
                    nc.vector.memset(marks[:, u:u + 1], 0.0)
                    nc.vector.tensor_tensor_reduce(out=self.s_buf[:, :], in0=self.bias(u),
                                                   in1=flat(0, 3, self.cols), scale=1.0, scalar=LOWEST, op0=ALU.add,
                                                   op1=ALU.max, accum_out=row_max[:, u:u + 1]).then_inc(self.max_step, 1)
                    dve.wait_ge(self.max_step, i * 4 + (2 * u + 1))
                    nc.vector.tensor_scalar(out=neg_max[:, u:u + 1], in0=row_max[:, u:u + 1], scalar1=-1.0,
                                            scalar2=None, op0=ALU.mult).then_inc(self.max_step, 1)
                    dve.wait_ge(self.probs_ready, i * 2 + (u + 1))
                    nc.vector.reciprocal(row_inv[:, u:u + 1], row_sum[:, u:u + 1]).then_inc(self.inv_done, 1)
                    dve.wait_ge(self.inv_done, i * 2 + (u + 1))
                    dve.wait_ge(self.o_ready, i * 2 + (u + 1))
                    nc.vector.tensor_scalar(out=s_o[:, :], in0=ps[:, 6, 0:P], scalar1=row_inv[:, u:u + 1],
                                            scalar2=None, op0=ALU.mult).then_inc(self.o_scaled, 1)
                    for hh in range(2):
                        dve.wait_ge(self.ot_hi, i * 4 + (2 * u + hh + 1))
                        nc.vector.tensor_tensor(out=self.out_ap(xn_lo, b, g, hh), in0=self.turned(hh),
                                                in1=self.out_ap(xn_hi, b, g, hh).bitcast(F32),
                                                op=ALU.subtract).then_inc(self.ot_lo, 1)

    band_p = Prompt("band", H_B // 2, qb, kb, vb, 4,
                    lambda i: ins["band_bias"][bass.ds(i, 1)].rearrange("o p h c -> p (o h) c"),
                    lambda it: 384 - P * it, False)
    neg_f_dram = nc.dram_tensor("neg_f_dram", (H_C, T), F32, kind="Internal").ap()
    after_dram = nc.dram_tensor("after_dram", (P, PAST), F32, kind="Internal").ap()
    fox_p = Prompt("fox", H_C // 2, qc, kc, vc, 0,
                   lambda i: neg_f_dram[bass.ds(i * 2, 2), 0:SEQ].rearrange("(o h) c -> o h c", o=1)
                   .broadcast_to([P, 2, SEQ]),
                   lambda it: 0, True)
    band_s = Sample("band", WIN, qb, kb, vb, lambda u, p, c0: kc_b[:, u, p, c0:c0 + 512],
                    lambda u, jt, p: (vc_b0, vc_b1)[u][:, jt, p * P:(p + 1) * P], lambda u: sb_bias[:, u, :],
                    sb_s, sb_pt, 4, 1, False)
    band_s.bias_dmas = 1
    fox_s = Sample("fox", PAST, qc, kc, vc,
                   lambda u, p, c0: (qc, kc)[u][:, 2 * p + c0 // 512, 0:512],
                   lambda u, jt, p: (v_extra[:, jt, p * P:(p + 1) * P] if u else
                                     vc[:, jt // 2, (jt % 2) * 512 + p * P:(jt % 2) * 512 + (p + 1) * P]),
                   lambda u: sf_bias[:, :], sf_s, sf_pt, 0, 2, True)
    fox_s.bias_dmas = 2


    g = lambda name: sem("gla_" + name)
    g_pre, g_ls, g_loga, g_cum, g_exp, g_last, g_dec = (g(n) for n in ("pre", "ls", "loga", "cum", "exp", "last", "dec"))
    g_qk, g_kt, g_ktok, g_kown, g_att, g_attm = (g(n) for n in ("qk", "kt", "ktok", "kown", "att", "attm"))
    g_kv, g_s, g_sd, g_o, g_oc, g_sq, g_stat = (g(n) for n in ("kv", "s", "sd", "o", "oc", "sq", "stat"))
    g_r, g_on, g_sg, g_ohi, g_olo, g_ar = (g(n) for n in ("r", "on", "sg", "ohi", "olo", "ar"))
    s_dec_loaded, states_stored = sem("s_dec_loaded"), sem("states_stored")
    kv_even_stored, kv_odd_stored, logf_stored = sem("kv_even_stored"), sem("kv_odd_stored"), sem("logf_stored")
    q_head = (qa, qa1)
    head_rows = [slice(64 * (h % 2), 64 * (h % 2) + 64) for h in range(H_A)]

    def gla_pe(pe, ph):
        m = mix_at(ph)
        pe.wait_ge(unit_free, m["out"][1])
        for tt in range(TT):
            last = nc.tensor.matmul(flat(0, 3, 1280)[:, tt * 256:(tt + 1) * 256], ar[:, tt * P:(tt + 1) * P],
                                    w_alpha[:, :], start=True, stop=True)
        last.then_inc(g_pre, 1)
        pe.wait_ge(g_loga, 1)
        for ft in range(2):
            for tt in range(TT):
                last = nc.tensor.matmul(flat(3 + 2 * ft, 2, T)[:, tt * P:(tt + 1) * P],
                                        log_a[:, tt * 256 + ft * P:tt * 256 + (ft + 1) * P],
                                        (cum16 if tt == TT - 1 else cum64)[:, :], start=True, stop=True)
        last.then_inc(g_cum, 1)
        pe.wait_ge(g_qk, 6)
        for tt in range(TT):
            for ft in range(2):
                last = nc.tensor.transpose(flat(0, 3, 1280)[:, tt * 256 + ft * P:tt * 256 + (ft + 1) * P],
                                           ka[:, ft, tt * P:(tt + 1) * P], ident[:, :])
        last.then_inc(g_kt, 1)
        for tt in range(TT):
            for h in range(H_A):
                cols = slice(tt * P, (tt + 1) * P)
                last = nc.tensor.matmul(ps[:, 3 + tt, h * P:(h + 1) * P], k_in[:, h // 2, cols],
                                        q_head[h % 2][:, h // 2, cols], start=True, stop=True)
            last.then_inc(g_att, 1)
        pe.wait_ge(g_ktok, 1)
        for c in range(SEQ // CHUNK):
            rows = slice(64 * (c % 2), 64 * (c % 2) + 64)
            if c >= 2:
                pe.wait_ge(g_s, 4 * (c - 1))
            for pair in range(2):
                last = nc.tensor.matmul(ps[:, c % 2, pair * 256:(pair + 1) * 256],
                                        k_tok[rows, c // 2, pair * P:(pair + 1) * P],
                                        va[rows, c // 2, pair * 256:(pair + 1) * 256], start=True, stop=True)
            last.then_inc(g_kv, 1)
        pe.wait_ge(g_attm, TT)
        pe.wait_ge(g_s, 4 * (SEQ // CHUNK))
        pe.wait_ge(s_dec_loaded, 16)

        def head_out(h):
            q, pair = q_head[h % 2], h // 2
            o = flat(2 + 2 * (h % 2), 2, T)
            if h >= 2:
                pe.wait_ge(g_oc, h - 1)
            for tt in range(TT):
                nc.tensor.matmul(o[:, tt * P:(tt + 1) * P], va[:, tt, h * P:(h + 1) * P],
                                 att[:, tt, h * P:(h + 1) * P], start=True, stop=False)
                if tt < TT - 1:
                    for c in (2 * tt, 2 * tt + 1):
                        if c:
                            cols = slice(c * CHUNK, (c + 1) * CHUNK)
                            last = nc.tensor.matmul(o[:, cols], s_hist[:, c, pair, :], q[:, pair, cols],
                                                    start=False, stop=c % 2 == 1)
                else:
                    for b in range(DEC_BATCH):
                        cols = slice(SEQ + b * DEC_SEQ, SEQ + (b + 1) * DEC_SEQ)
                        last = nc.tensor.matmul(o[:, cols], s_dec[:, b, pair, :], q[:, pair, cols],
                                                start=False, stop=b == DEC_BATCH - 1)
            last.then_inc(g_o, 1)

        def head_stat(h):
            pe.wait_ge(g_sq, h + 1)
            for tt in range(TT):
                last = nc.tensor.matmul(ps[:, 6, h * TT + tt:h * TT + tt + 1], sq_head[:, tt * P:(tt + 1) * P],
                                        mean_head[:, :], start=True, stop=True)
            last.then_inc(g_stat, 1)

        head_out(0)
        for h in range(1, H_A):
            head_out(h)
            head_stat(h - 1)
        head_stat(H_A - 1)
        pe.wait_ge(g_kown, 1)
        for b in range(DEC_BATCH):
            if b >= 2:
                pe.wait_ge(g_sd, 4 * (b - 1))
            for pair in range(2):
                last = nc.tensor.matmul(ps[:, b % 2, pair * 256:(pair + 1) * 256],
                                        k_own[:, b, pair * P:(pair + 1) * P],
                                        va[:, TT - 1, pair * 256:(pair + 1) * 256], start=True, stop=True)
            last.then_inc(g_kv, 1)
        pe.wait_ge(g_sd, 4 * DEC_BATCH)
        for h in range(H_A):
            pe.wait_ge(diag_done, DIAG0["gla"] + TT * (h + 1))
            for tt in range(TT):
                last = nc.tensor.matmul(flat(0, 2, T)[:, tt * P:(tt + 1) * P], ones[:, :], diag_a[:, tt, :],
                                        start=True, stop=True)
            last.then_inc(g_r, 1)

    def gla_act(act, ph):
        act.wait_ge(g_pre, 1)
        nc.scalar.activation(ls_tmp[:, :], flat(0, 3, 1280), ACT.Abs).then_inc(g_ls, 1)
        act.wait_ge(g_ls, 1)
        nc.scalar.activation(ls_tmp[:, :], ls_tmp[:, :], ACT.Exp, scale=-1.0).then_inc(g_ls, 1)
        act.wait_ge(g_ls, 2)
        nc.scalar.activation(ls_tmp[:, :], ls_tmp[:, :], ACT.Ln, bias=1.0).then_inc(g_ls, 1)
        act.wait_ge(g_cum, 1)
        for ft in range(2):
            nc.scalar.activation(decay[:, ft, :], flat(3 + 2 * ft, 2, T), ACT.Copy).then_inc(g_exp, 1)
        act.wait_ge(g_exp, 2)
        nc.scalar.activation(e_cum[:, :, :], decay[:, :, :], ACT.Exp).then_inc(g_exp, 1)
        nc.scalar.activation(k_in[:, :, :], decay[:, :, :], ACT.Exp, scale=-1.0).then_inc(g_exp, 1)
        act.wait_ge(g_dec, 4)
        nc.scalar.activation(decay[:, :, :], decay[:, :, :], ACT.Exp, scale=-1.0).then_inc(g_exp, 1)
        act.wait_ge(g_kt, 1)
        nc.scalar.activation(k_tok[:, :, :].rearrange("p t c -> p (t c)"), flat(0, 3, 1280),
                             ACT.Copy).then_inc(g_ktok, 1)
        nc.scalar.activation(ag[:, :, :], ag[:, :, :], ACT.Silu).then_inc(g_sg, 1)
        for h in range(H_A):
            act.wait_ge(g_o, h + 1)
            nc.scalar.activation(o_head[:, h, :], flat(2 + 2 * (h % 2), 2, T), ACT.Copy).then_inc(g_oc, 1)
            act.wait_ge(g_oc, h + 1)
            if h:
                act.wait_ge(g_stat, h)
            nc.scalar.activation(sq_head[:, :], o_head[:, h, :], ACT.Square).then_inc(g_sq, 1)
        for h in range(H_A):
            act.wait_ge(g_on, 2 * h + 2)
            nc.scalar.activation(xn_hi[:, h, :], o_head[:, h, :], ACT.Copy).then_inc(g_ohi, 1)

    def gla_dve(dve, ph):
        dve.wait_ge(g_ls, 3)
        nc.vector.scalar_tensor_tensor(out=log_a[:, :], in0=flat(0, 3, 1280), scalar=0.0, in1=ls_tmp[:, :],
                                       op0=ALU.min, op1=ALU.subtract).then_inc(g_loga, 1)
        dve.wait_ge(g_exp, 2)
        spans = ((0, SEQ, CHUNK, 0), (SEQ, T, DEC_SEQ, 8))
        for ft in range(2):
            for lo, hi, n, at_ in spans:
                src = decay[:, ft, lo:hi].rearrange("p (c i) -> p c i", i=n)[:, :, n - 1]
                nc.vector.tensor_copy(chunk_last[:, ft, at_:at_ + 8], src).then_inc(g_last, 1)
        dve.wait_ge(g_last, 4)
        dve.wait_ge(g_exp, 4)
        for ft in range(2):
            for lo, hi, n, at_ in spans:
                nc.vector.tensor_tensor(
                    out=decay[:, ft, lo:hi].rearrange("p (c i) -> p c i", i=n),
                    in0=decay[:, ft, lo:hi].rearrange("p (c i) -> p c i", i=n),
                    in1=chunk_last[:, ft, at_:at_ + 8].unsqueeze(2).broadcast_to([P, 8, n]),
                    op=ALU.subtract).then_inc(g_dec, 1)
        nc.vector.tensor_tensor(out=qa1[64:P, :, :], in0=qa[64:P, :, :], in1=e_cum[64:P, :, :],
                                op=ALU.mult).then_inc(g_qk, 1)
        nc.vector.tensor_tensor(out=qa[0:64, :, :], in0=qa[0:64, :, :], in1=e_cum[0:64, :, :],
                                op=ALU.mult).then_inc(g_qk, 1)
        nc.vector.memset(qa1[0:64, :, :], 0.0).then_inc(g_qk, 1)
        dve.wait_ge(g_qk, 1)
        nc.vector.memset(qa[64:P, :, :], 0.0).then_inc(g_qk, 1)
        nc.vector.tensor_tensor(out=k_in[:, :, :], in0=k_in[:, :, :], in1=ka[:, :, :], op=ALU.mult).then_inc(g_qk, 1)
        dve.wait_ge(g_exp, 5)
        dve.wait_ge(g_qk, 5)
        nc.vector.tensor_tensor(out=ka[:, :, :], in0=ka[:, :, :], in1=decay[:, :, :], op=ALU.mult).then_inc(g_qk, 1)
        for tt in range(TT):
            dve.wait_ge(g_att, tt + 1)
            keep = (keep16 if tt == TT - 1 else keep64)[:, :].unsqueeze(1).broadcast_to([P, H_A, P])
            nc.vector.tensor_tensor(out=att[:, tt, :].rearrange("p (h c) -> p h c", h=H_A),
                                    in0=ps[:, 3 + tt, :].rearrange("p (h c) -> p h c", h=H_A), in1=keep,
                                    op=ALU.mult).then_inc(g_attm, 1)
        dve.wait_ge(g_ktok, 1)
        for c in range(SEQ // CHUNK):
            dve.wait_ge(g_kv, c + 1)
            if c:
                dve.wait_ge(g_s, 4 * c)
            for h in range(H_A):
                rows, pair = head_rows[h], h // 2
                kv = ps[rows, c % 2, pair * 256 + (h % 2) * P:pair * 256 + (h % 2 + 1) * P]
                if c == 0:
                    ins_ = nc.vector.tensor_copy(s_hist[rows, 1, pair, :], kv)
                else:
                    col = (c + 1) * CHUNK - 1
                    ins_ = nc.vector.scalar_tensor_tensor(out=s_hist[rows, c + 1, pair, :],
                                                          in0=s_hist[rows, c, pair, :],
                                                          scalar=e_cum[rows, pair, col:col + 1], in1=kv,
                                                          op0=ALU.mult, op1=ALU.add)
                ins_.then_inc(g_s, 1)
        nc.vector.tensor_tensor(out=k_own[:, :, :], in0=k_tok[:, TT - 1, :].unsqueeze(1).broadcast_to([P, DEC_BATCH, 256]),
                                in1=own_rows[:, :].unsqueeze(2).broadcast_to([P, DEC_BATCH, 256]),
                                op=ALU.mult).then_inc(g_kown, 1)
        for b in range(DEC_BATCH):
            dve.wait_ge(g_kv, SEQ // CHUNK + b + 1)
            for h in range(H_A):
                rows, pair = head_rows[h], h // 2
                col = SEQ + (b + 1) * DEC_SEQ - 1
                nc.vector.scalar_tensor_tensor(
                    out=s_dec[rows, b, pair, :], in0=s_dec[rows, b, pair, :], scalar=e_cum[rows, pair, col:col + 1],
                    in1=ps[rows, b % 2, pair * 256 + (h % 2) * P:pair * 256 + (h % 2 + 1) * P],
                    op0=ALU.mult, op1=ALU.add).then_inc(g_sd, 1)
        dve.wait_ge(g_stat, H_A)
        rs_chain(dve, ps[:, 6, 0:H_A * TT], H_A * TT, RS_NORM0["gla"])
        dve.wait_ge(rs_step, RS_NORM0["gla"] + RS_OPS)
        dve.wait_ge(g_sg, 1)
        dve.wait_ge(states_stored, 32)
        for h in range(H_A):
            if h:
                dve.wait_ge(g_r, h)
            for tt in range(TT):
                nc.vector.tensor_scalar(out=diag_a[:, tt, :], in0=ident[:, :],
                                        scalar1=rs[1][:, h * TT + tt:h * TT + tt + 1], scalar2=None,
                                        op0=ALU.mult).then_inc(diag_done, 1)
            dve.wait_ge(g_r, h + 1)
            if h:
                dve.wait_ge(g_on, 2 * h)
            nc.vector.scalar_tensor_tensor(out=o_tmp[:, :], in0=o_head[:, h, :], scalar=head_gain[:, 0:1],
                                           in1=flat(0, 2, T), op0=ALU.mult, op1=ALU.mult).then_inc(g_on, 1)
            dve.wait_ge(g_on, 2 * h + 1)
            nc.vector.tensor_tensor(out=o_head[:, h, :], in0=o_tmp[:, :], in1=ag[:, h, :],
                                    op=ALU.mult).then_inc(g_on, 1)
            dve.wait_ge(g_ohi, h + 1)
            nc.vector.tensor_tensor(out=xn_lo[:, h, :], in0=o_head[:, h, :], in1=xn_hi[:, h, :].bitcast(F32),
                                    op=ALU.subtract).then_inc(g_olo, 1)

    f_ls, f_lf, f_turned, f_tok, f_sums, f_sbuf = (sem("fgate_" + n) for n in ("ls", "lf", "turned", "tok", "sums", "sbuf"))
    f_loaded, f_scratch = sem("fgate_loaded"), sem("fgate_scratch")

    def fgate_pe(pe, ph):
        pe.wait_ge(unit_free, mix_at(ph)["out"][1])
        pe.wait_ge(f_lf, 1)
        for tt in range(TT):
            last = nc.tensor.transpose(ps[:, 0, tt * H_C:(tt + 1) * H_C], lf[:, tt * P:(tt + 1) * P],
                                       ident[0:H_C, 0:H_C])
        last.then_inc(f_turned, 1)
        pe.wait_ge(f_loaded, 48)
        for t in range(7, -1, -1):
            for bank in ((3, 4) if t >= 4 else (3,)):
                j0 = 512 * (bank - 3)
                n = min(512, P * (t + 1) - j0)
                c0 = 896 - P * t + j0
                nc.tensor.matmul(ps[:, bank, 0:n], clf[:, t, :], after_w[:, c0:c0 + n], start=t == 7,
                                 stop=t == 0 or (bank == 4 and t == 4))
        pe.wait_ge(f_tok, 1)
        for tt in range(TT - 1):
            nc.tensor.matmul(ps[0:H_C, 1, tt * P:SEQ], lf_tok[:, tt, :], upto_w[:, 0:SEQ - tt * P], start=tt == 0,
                             stop=tt == TT - 2)
        nc.tensor.matmul(ps[0:H_C, 2, 0:P], lf_tok[:, TT - 1, :], keep16[:, :], start=True,
                         stop=True).then_inc(f_sums, 1)

    def fgate_act(act, ph):
        act.wait_ge(unit_ready, mix_at(ph)["out"][1])
        act.wait_ge(unit_free, mix_at(ph)["out"][1])
        nc.scalar.activation(lf_tmp[:, :], logit[:, :], ACT.Abs).then_inc(f_ls, 1)
        act.wait_ge(f_ls, 1)
        nc.scalar.activation(lf_tmp[:, :], lf_tmp[:, :], ACT.Exp, scale=-1.0).then_inc(f_ls, 1)
        act.wait_ge(f_ls, 2)
        nc.scalar.activation(lf_tmp[:, :], lf_tmp[:, :], ACT.Ln, bias=1.0).then_inc(f_ls, 1)
        act.wait_ge(f_sums, 1)
        nc.scalar.activation(neg_f[:, :], ps[0:H_C, 1:3, :].rearrange("p b c -> p (b c)")[:, 0:T], ACT.Copy,
                             scale=-1.0).then_inc(f_sbuf, 1)
        nc.scalar.activation(c_after[:, :], flat(3, 2, PAST), ACT.Copy).then_inc(f_sbuf, 1)

    def fgate_dve(dve, ph):
        dve.wait_ge(f_ls, 3)
        nc.vector.scalar_tensor_tensor(out=lf[:, :], in0=logit[:, :], scalar=0.0, in1=lf_tmp[:, :], op0=ALU.min,
                                       op1=ALU.subtract).then_inc(f_lf, 1)
        dve.wait_ge(f_turned, 1)
        nc.vector.tensor_copy(lf_tok[:, :, :].rearrange("p t h -> p (t h)"), ps[:, 0, 0:TT * H_C]).then_inc(f_tok, 1)

    EVEN = next(ph for ph in PLAN if ph["kind"] == "even")
    ODD = next(ph for ph in PLAN if ph["kind"] == "odd")
    consts = [(ident, "ident"), (ones, "ones"), (mean_model, "mean_model"), (mean_head, "mean_head"),
              (gains, "gains"), (cum64, "cum64"), (cum16, "cum16"), (keep64, "keep64"), (keep16, "keep16"),
              (own_rows, "own_rows"), (w_alpha, "w_alpha"), (head_gain, "head_gain"), (bias_f, "bias_f"),
              (causal, "causal"), (own_causal, "own_causal")]
    block = ctx.enter_context(nc.Block())

    @block.sync
    def _(sp):
        for k in range(0, KT, 2):
            sp.dma_start(x_res[:, k:k + 2, :], ins["x"][:, k:k + 2, :]).then_inc(x_loaded, 16)
        for dst, name in consts:
            sp.dma_start(dst[tuple(slice(None) for _ in dst.shape)], ins[name]).then_inc(consts_loaded, 16)
        for ph in PLAN:
            if ph["kind"] == "ffn":
                for kind, count, per, n0, q0 in ffn_segments(ph):
                    first = FF_A if kind == "up_b" else 0
                    load_slabs(sp, ph, kind, first, count, n0, fresh=2 if n0 == 0 else 0)
                continue
            m = mix_at(ph)
            small_load(sp, ph)
            load_slabs(sp, ph, "in", 0, IN_SLABS + TOK_SLABS, m["fm"][0])
            load_slabs(sp, ph, "out", 0, 2, m["out"][0])
            if ph["kind"] == "even":
                sp.wait_ge(unit_free, m["out"][1])
                sp.dma_start(outs["band_k"], kb[:, :, :]).then_inc(kv_even_stored, 16)
                sp.dma_start(outs["band_v"], vb[:, :, :]).then_inc(kv_even_stored, 16)
                sp.dma_start(s_dec[:, :, :, :], ins["state"]).then_inc(s_dec_loaded, 16)
                sp.wait_ge(g_s, 4 * (SEQ // CHUNK))
                sp.dma_start(outs["p_state"], s_hist[:, SEQ // CHUNK, :, :]).then_inc(states_stored, 16)
                sp.wait_ge(g_sd, 4 * DEC_BATCH)
                sp.dma_start(outs["s_state"], s_dec[:, :, :, :]).then_inc(states_stored, 16)

                def band_load(sp, i, u, first):
                    b = i * 2 + u
                    if not first:
                        sp.wait_ge(band_s.logits_ready, i * 2 + (u - 1))
                    sp.dma_start(kc_b[:, u], ins["band_kc"][bass.ds(b, 1)].rearrange("o p j c -> p (o j) c")
                                 ).then_inc(band_s.k_loaded[u], 16)
                    if not first:
                        sp.wait_ge(band_s.max_step, i * 4 + (2 * u - 2))
                    sp.dma_start(sb_bias[:, u, :], ins["band_bias_s"][bass.ds(b, 1)].rearrange("o p c -> p (o c)")
                                 ).then_inc(band_s.bias_loaded[u], 16)
                    if first and u:
                        sp.wait_ge(band_p.ot_lo, 4 * (H_B // 2))
                    if not first:
                        sp.wait_ge(band_s.o_ready, i * 2 + (u - 1))
                    sp.dma_start((vc_b0, vc_b1)[u][:, :, :],
                                 ins["band_vc"][bass.ds(b, 1)].rearrange("o p j c -> p (o j) c")
                                 ).then_inc(band_s.v_loaded[u], 16)

                band_p.sp(sp, lambda sp: sp.wait_ge(g_olo, H_A))
                band_s.sp(sp, lambda sp: None, band_load)
            else:
                sp.wait_ge(unit_free, m["out"][1])
                sp.dma_start(outs["fox_k"], kc[:, :, :]).then_inc(kv_odd_stored, 16)
                sp.dma_start(outs["fox_v"], vc[:, :, :]).then_inc(kv_odd_stored, 16)
                sp.dma_start(clf[:, :, :], ins["fox_clogf"]).then_inc(f_loaded, 16)
                sp.dma_start(after_w[:, :], ins["after_w"]).then_inc(f_loaded, 16)
                sp.dma_start(upto_w[:, :], ins["upto_w"]).then_inc(f_loaded, 16)
                sp.wait_ge(f_sbuf, 2)
                sp.dma_start(outs["fox_logf"], lf[:, :]).then_inc(logf_stored, 16)
                sp.dma_start(neg_f_dram, neg_f[:, :]).then_inc(f_scratch, 16)
                sp.dma_start(after_dram, c_after[:, :]).then_inc(f_scratch, 16)

                def fox_load(sp, i, u, first):
                    if not first:
                        sp.wait_ge(fox_s.logits_ready, i * 2 + (u - 1))
                    sp.dma_start((qc, kc)[u][:, :, 0:512], ins["fox_kc"][u][bass.ds(i, 1)]
                                 .rearrange("o p j c -> p (o j) c")).then_inc(fox_s.k_loaded[u], 16)
                    if not first:
                        sp.wait_ge(fox_s.o_ready, i * 2 + (u - 1))
                    dst = v_extra[:, :, :] if u else vc[:, 0:4, :].rearrange("p t (a c) -> p (t a) c", a=2)
                    sp.dma_start(dst, ins["fox_vc"][u][bass.ds(i, 1)].rearrange("o p j c -> p (o j) c")
                                 ).then_inc(fox_s.v_loaded[u], 16)
                    if not first or u:
                        sp.wait_ge(fox_s.max_step, i * 4 + 2 * u)
                    sp.dma_start(sf_bias[:, 0:PAST], after_dram[bass.ds(i * H_C + 8 * u, 8), :].unsqueeze(1)
                                 .broadcast_to([8, DEC_SEQ, PAST])).then_inc(fox_s.bias_loaded[u], 16)
                    sp.dma_start(sf_bias[:, PAST:PAST + P], neg_f_dram[8 * u:8 * u + 8, SEQ:T].unsqueeze(1)
                                 .broadcast_to([8, DEC_SEQ, P])).then_inc(fox_s.bias_loaded[u], 16)

                fox_p.sp(sp, lambda sp: sp.wait_ge(f_scratch, 32))

                def fox_ready(sp):
                    sp.wait_ge(fox_p.ot_lo, 4 * (H_C // 2))
                    sp.wait_ge(kv_odd_stored, 32)

                fox_s.sp(sp, fox_ready, fox_load)
            load_slabs(sp, ph, "out", 2, 2, m["out"][0] + 2)
        for k in range(0, KT, 4):
            sp.wait_ge(xf_done, XN0[NORMS] + k + 4)
            sp.dma_start(outs["y"][:, k:k + 4, :], y_out[:, k:k + 4, :]).then_inc(y_stored, 16)
        sp.wait_ge(y_stored, 32)
        sp.wait_ge(states_stored, 32)
        sp.wait_ge(kv_even_stored, 32)
        sp.wait_ge(kv_odd_stored, 32)
        sp.wait_ge(logf_stored, 16)

    @block.gpsimd
    def _(pool):
        lo_next(pool, 0, 0)
        for ph in PLAN:
            if ph["kind"] == "ffn":
                ffn_pool(pool, ph)
            else:
                proj_pool(pool, ph)
                out_pool(pool, ph)

    @block.scalar
    def _(act):
        act.wait_ge(x_loaded, 64)
        act.wait_ge(consts_loaded, 16 * len(consts))
        for k in range(KT):
            sq_act(act, k, k, (0, 0))
        act.wait_ge(raw_loaded[0], 16)
        nc.scalar.activation(w_hi[:, 0, :], w_raw[:, 0, :], ACT.Copy).then_inc(hi_done, 1)
        for ph in PLAN:
            if ph["kind"] == "ffn":
                ffn_act(act, ph)
            elif ph["kind"] == "even":
                proj_act(act, ph)
                gla_act(act, ph)
                band_p.act(act)
                band_s.act(act)
                act.wait_ge(kv_even_stored, 32)
                out_act(act, ph)
            else:
                proj_act(act, ph)
                fgate_act(act, ph)
                fox_p.act(act)
                fox_s.act(act)
                out_act(act, ph)

    @block.vector
    def _(dve):
        dve.wait_ge(consts_loaded, 16 * len(consts))
        nc.vector.tensor_copy(ident_b[:, :], ident[:, :]).then_inc(masks_cast, 1)
        nc.vector.tensor_copy(causal_b[:, :], causal[:, :]).then_inc(masks_cast, 1)
        nc.vector.tensor_copy(own_causal_b[:, :], own_causal[:, :]).then_inc(masks_cast, 1)
        clear_sum(dve, 0, None)
        for k in range(KT):
            acc_dve(dve, k, k, (0, 0))
        for ph in PLAN:
            if ph["kind"] == "ffn":
                ffn_dve(dve, ph)
            elif ph["kind"] == "even":
                nc.vector.memset(ar[:, :], 1.0).then_inc(g_ar, 1)

                def take_ar():
                    dve.wait_ge(g_ar, 1)
                    nc.vector.tensor_copy(halves(ar[0:R_A, :]), ps[0:R_A, 0:2, 0:HALF]).then_inc(unit_free, 4)

                proj_dve(dve, ph, take_ar,
                         [(qa, 0, SCALE), (qa, 1, SCALE), (ka, 0, 1.0), (ka, 1, 1.0)]
                         + [(ag, j, 1.0) for j in range(4)] + [(qb, j, SCALE) for j in range(4)]
                         + [(kb, j, 1.0) for j in range(4)],
                         lambda s: (va, vb)[s // 2][:, :, (s % 2) * 256:(s % 2 + 1) * 256])
                gla_dve(dve, ph)
                band_p.dve(dve)
                band_s.dve(dve)
                out_dve(dve, ph)
            else:
                def take_logits():
                    nc.vector.tensor_scalar(out=halves(logit[:, :]), in0=ps[0:H_C, 0:2, 0:HALF],
                                            scalar1=bias_f[:, 0:1], scalar2=None, op0=ALU.add).then_inc(unit_free, 4)

                proj_dve(dve, ph, take_logits,
                         [(qc, j, SCALE) for j in range(KT)] + [(kc, j, 1.0) for j in range(KT)],
                         lambda s: vc[:, :, s * 256:(s + 1) * 256])
                fgate_dve(dve, ph)
                fox_p.dve(dve)
                fox_s.dve(dve)
                out_dve(dve, ph)
        norm_dve(dve, NORMS, UNITS, final=True)

    @block.tensor
    def _(pe):
        pe.wait_ge(consts_loaded, 16 * len(consts))
        pe.wait_ge(masks_cast, 3)
        for ph in PLAN:
            if ph["kind"] == "ffn":
                ffn_pe(pe, ph)
            elif ph["kind"] == "even":
                proj_pe(pe, ph)
                gla_pe(pe, ph)
                pe.wait_ge(g_olo, H_A)
                band_p.pe(pe)
                pe.wait_ge(band_p.ot_lo, 4 * (H_B // 2))
                band_s.pe(pe)
                out_pe(pe, ph, lambda pe: pe.wait_ge(band_s.ot_lo, 2 * DEC_BATCH))
            else:
                proj_pe(pe, ph)
                fgate_pe(pe, ph)
                pe.wait_ge(f_sbuf, 2)
                fox_p.pe(pe)
                pe.wait_ge(fox_p.ot_lo, 4 * (H_C // 2))
                fox_s.pe(pe)
                out_pe(pe, ph, lambda pe: pe.wait_ge(fox_s.ot_lo, 4 * DEC_BATCH))
        norm_pe(pe, NORMS, UNITS)

    ctx.close()


def _layout(i):
    f = np.float32
    a = {k: np.asarray(v) for k, v in i.items()}
    out = {}
    x = np.concatenate([a["x_prompt"].reshape(SEQ, D_MODEL), a["x_sample"].reshape(T - SEQ, D_MODEL)])
    out["x"] = x.T.reshape(KT, P, T).transpose(1, 0, 2)
    gu = a["ffn_w_gu"].reshape(4, KT, P, 2, D_FF // P, P)
    out["w_up"] = gu.transpose(0, 4, 2, 3, 1, 5).reshape(4, D_FF // P, P, SLAB)
    dn = a["ffn_w_down"].reshape(4, D_FF // P, P, KT, P)
    dn = dn.transpose(0, 3, 2, 1, 4)
    out["w_down_a"] = dn[:, :, :, :FF_A].reshape(4, KT, P, FF_A * P)
    out["w_down_b"] = dn[:, :, :, FF_A:].reshape(4, KT, P, FF_B * P)

    def fm(w):
        return w.reshape(KT, P, -1, 2, P).transpose(2, 1, 3, 0, 4).reshape(-1, P, SLAB)

    def tok(w):
        return w.reshape(KT, P, -1, 256).transpose(2, 1, 0, 3).reshape(-1, P, SLAB)

    e, o = a["even_w_in"][0], a["odd_w_in"][0]
    qk, v = H_A * DK, H_A * DV
    aq, ak, av, ag, ar, bq, bk, bv = np.split(e, np.cumsum([qk, qk, v, v, R_A, 512, 512]), axis=1)
    cq, ck, cv, cf = np.split(o, np.cumsum([1024, 1024, 1024]), axis=1)
    out["w_in"] = np.stack([np.concatenate([fm(np.concatenate([aq, ak, ag, bq, bk], 1)), tok(av), tok(bv)]),
                            np.concatenate([fm(np.concatenate([cq, ck], 1)), tok(cv)])])
    out["w_small"] = np.stack([w.reshape(KT, P, R_A).transpose(1, 0, 2) for w in (ar, cf)])
    out["w_out"] = np.stack([fm(a["even_w_out"][0]), fm(a["odd_w_out"][0])])
    out["gains"] = np.concatenate([a["norm_g"].reshape(6, D_MODEL), a["final_norm_g"][None]]
                                  ).reshape(7 * KT, P).T
    out["w_alpha"] = np.concatenate([a["gla_w_alpha_up"][0], a["gla_b_alpha"]])
    out["head_gain"] = a["gla_norm_g"].reshape(P, 1)
    out["bias_f"] = a["fox_b_f"].reshape(H_C, 1)
    st = a["state_gla"][0].reshape(DEC_BATCH, 2, 2, DK, DV)
    out["state"] = st.transpose(2, 3, 0, 1, 4).reshape(P, DEC_BATCH, 2, DV)
    kb = a["cache_band_k"][0].reshape(DEC_BATCH, WIN, 4, P)
    out["band_kc"] = kb.transpose(0, 3, 2, 1)
    out["band_vc"] = a["cache_band_v"][0].reshape(DEC_BATCH, 4, P, 512).transpose(0, 2, 1, 3)
    kf = a["cache_fox_k"][0].reshape(DEC_BATCH, 2, 512, 2, 4, P)
    out["fox_kc"] = kf.transpose(3, 0, 5, 4, 1, 2).reshape(2, DEC_BATCH, P, 8, 512)
    vf = a["cache_fox_v"][0].reshape(DEC_BATCH, 8, P, 2, 512)
    out["fox_vc"] = vf.transpose(3, 0, 2, 1, 4)
    out["fox_clogf"] = a["cache_fox_logf"][0].reshape(DEC_BATCH, 8, P, H_C).transpose(2, 1, 0, 3).reshape(P, 8, P)
    rel = a["band_rel_bias"][0]
    r = np.arange(P)
    c = np.arange(512) - 384
    pb = rel[:, np.clip(r[:, None] - c[None], -128, 128) + 128]
    pb = np.where((c[None] // CHUNK <= r[:, None] // CHUNK)[None], pb, f(NEG))
    out["band_bias"] = pb.reshape(4, 2, P, 512).transpose(0, 2, 1, 3)
    fr = np.arange(DEC_SEQ)
    sb = np.full((DEC_BATCH, H_B, DEC_SEQ, WIN + P), f(NEG))
    for b in range(DEC_BATCH):
        sb[b, :, :, :WIN] = rel[:, np.clip(WIN + fr[:, None] - np.arange(WIN)[None], -128, 128) + 128]
        own = slice(WIN + b * DEC_SEQ, WIN + (b + 1) * DEC_SEQ)
        sb[b, :, :, own] = rel[:, fr[:, None] - fr[None] + 128]
    out["band_bias_s"] = sb.reshape(DEC_BATCH, P, WIN + P)
    eye = np.eye(P, dtype=f)
    t, j = r[:, None], r[None]
    out["ident"], out["ones"] = eye, np.ones((P, P), f)
    out["mean_model"], out["mean_head"] = np.full((P, 1), 1 / D_MODEL, f), np.full((P, 1), 1 / DV, f)
    out["keep64"] = ((t <= j) & (t // CHUNK == j // CHUNK)).astype(f)
    out["keep16"] = ((t <= j) & (t // DEC_SEQ == j // DEC_SEQ)).astype(f)
    out["cum64"] = np.where((t <= j) & (t // CHUNK == j // CHUNK), f(1 / 16), f(0))
    out["cum16"] = np.where((t <= j) & (t // DEC_SEQ == j // DEC_SEQ), f(1 / 16), f(0))
    out["own_rows"] = (t // DEC_SEQ == np.arange(DEC_BATCH)[None]).astype(f)
    out["causal"] = np.where(j > t, f(NEG), f(0))
    d = np.arange(240)[None] - 112
    out["own_causal"] = np.where((d >= 0) & (d <= t % DEC_SEQ), f(0), f(NEG))
    out["after_w"] = (np.arange(1024)[None] - 896 < t).astype(f)
    out["upto_w"] = (np.arange(SEQ)[None] >= t).astype(f)
    return {k: np.ascontiguousarray(v) for k, v in out.items()}


_OUTS = {"y": (P, KT, T), "p_state": (P, 2, P), "s_state": (P, DEC_BATCH, 2, P), "band_k": (P, 4, T),
         "band_v": (P, TT, 512), "fox_k": (P, KT, T), "fox_v": (P, TT, D_MODEL), "fox_logf": (H_C, T)}


def kernel(**inputs):
    import concourse.bacc as bacc
    from concourse.bass_utils import run_bass_kernel_spmd

    arrays = _layout(inputs)
    nc = bacc.Bacc("TRN2", target_bir_lowering=False, num_devices=1)
    ins = {k: nc.dram_tensor("in_" + k, v.shape, mybir.dt.from_np(v.dtype), kind="ExternalInput").ap()
           for k, v in arrays.items()}
    outs = {k: nc.dram_tensor("out_" + k, s, F32, kind="ExternalOutput").ap() for k, s in _OUTS.items()}
    trunk_program(nc, ins, outs)
    r = run_bass_kernel_spmd(nc, [{"in_" + k: v for k, v in arrays.items()}], core_ids=[0]).results[0]
    got = {k: np.asarray(r["out_" + k]) for k in _OUTS}

    def frames(t, width):
        return t.transpose(2, 1, 0).reshape(T, width)

    def tok(t, width):
        return t.transpose(1, 0, 2).reshape(T, width)

    def split(t, tail):
        return (t[:SEQ].reshape(1, SEQ, *tail), t[SEQ:].reshape(DEC_BATCH, DEC_SEQ, *tail))

    yp, ys = split(frames(got["y"], D_MODEL), (D_MODEL,))
    bkp, bks = split(frames(got["band_k"], 512), (H_B, DH))
    bvp, bvs = split(tok(got["band_v"], 512), (H_B, DH))
    fkp, fks = split(frames(got["fox_k"], D_MODEL), (H_C, DH))
    fvp, fvs = split(tok(got["fox_v"], D_MODEL), (H_C, DH))
    flp, fls = split(got["fox_logf"].T, (H_C,))
    ps_ = got["p_state"].reshape(2, DK, 2, DV).transpose(2, 0, 1, 3).reshape(1, 1, H_A, DK, DV)
    ss_ = got["s_state"].reshape(2, DK, DEC_BATCH, 2, DV).transpose(2, 3, 0, 1, 4).reshape(1, DEC_BATCH, H_A, DK, DV)
    out = (yp, ys, ps_, bkp[None], bvp[None], fkp[None], fvp[None], flp[None], ss_, bks[None], bvs[None],
           fks[None], fvs[None], fls[None])
    return tuple(np.ascontiguousarray(t) for t in out)
```

```python
import numpy as np
import concourse.bass as bass
from concourse import mybir
from contextlib import ExitStack

F32 = mybir.dt.float32
F32R = mybir.dt.float32r
BF16 = mybir.dt.bfloat16
I32 = mybir.dt.int32
ALU = mybir.AluOpType
ACT = mybir.ActivationFunctionType

P = 128
D_MODEL, SEQ, DEC_BATCH, DEC_SEQ, PAST = 1024, 512, 8, 16, 1024
T = SEQ + DEC_BATCH * DEC_SEQ
TT = T // P
KT = D_MODEL // P
HALF = T // 2
D_FF = 2816
FF_A = 12
FF_B = D_FF // P - FF_A
CHUNK, WIN = 64, 512
H_A, DK, DV = 4, 64, 128
R_A = 16
H_B, H_C, DH = 8, 16, 64
SCALE = DH ** -0.5
EPS = 1e-6
SLAB = 16 * P
NEG = -1e30
LOWEST = -3e38
RSQRT_SEED = 1597463007.0

FFN_SLABS = FF_A + KT + FF_B + KT
FFN_UNITS = 2 * FF_A + KT + 2 * FF_B + KT
IN_SLABS = 8
TOK_SLABS = 4
OUT_SLABS = 4
MIX_SLABS = 1 + IN_SLABS + TOK_SLABS + OUT_SLABS
NORM_UNITS = 4
IN_UNITS = 4 + 2 * IN_SLABS + 4 * TOK_SLABS
OUT_UNITS = KT
SQ_STEPS = KT + 1


def plan():
    out, slab, unit, norm = [], 0, 0, 0
    for kind, index in (("ffn", 0), ("even", 0), ("ffn", 1), ("ffn", 2), ("odd", 0), ("ffn", 3)):
        out.append(dict(kind=kind, index=index, slab=slab, unit=unit, norm=norm))
        slab += FFN_SLABS if kind == "ffn" else MIX_SLABS
        unit += NORM_UNITS + (FFN_UNITS if kind == "ffn" else IN_UNITS + OUT_UNITS)
        norm += 1
    return out, slab, unit, norm


def trunk_program(nc, ins, outs):
    PLAN, SLABS, UNITS, NORMS = plan()
    ctx = ExitStack()

    base = (nc.sbuf_base + 63) // 64 * 64
    kib = 1024
    at_x = base
    at_xn = at_x + KT * T * 4
    at_w = at_xn + 2 * KT * T * 4
    at_h = at_w + 6 * SLAB * 4
    at_g = at_h + 2 * FF_A * T * 4
    at_acc = at_g + 4 * T * 4
    at_c = at_acc + T * 4

    def place(name, shape, dt, at):
        return nc.alloc_sbuf_tensor_at(name, shape, dt, offset=at)

    x_res = place("x_res", [P, KT, T], F32, at_x)
    xn_hi = place("xn_hi", [P, KT, T], F32R, at_xn)
    xn_lo = place("xn_lo", [P, KT, T], F32R, at_xn + KT * T * 4)
    y_out = place("y_out", [P, KT, T], F32, at_xn)
    w_raw = place("w_raw", [P, 2, SLAB], F32, at_w)
    w_hi = place("w_hi", [P, 2, SLAB], F32R, at_w + 2 * SLAB * 4)
    w_lo = place("w_lo", [P, 2, SLAB], F32R, at_w + 4 * SLAB * 4)
    h_hi = place("h_hi", [P, FF_A, T], F32R, at_h)
    h_lo = place("h_lo", [P, FF_A, T], F32R, at_h + FF_A * T * 4)
    gate = place("gate", [P, 2, T], F32, at_g)
    prod = place("prod", [P, 2, T], F32, at_g + 2 * T * 4)
    sq_sum = place("sq_sum", [P, T], F32, at_acc)

    c_at = [at_c]

    def const(name, shape, dt=F32):
        size = int(np.prod(shape[1:])) * (2 if dt == BF16 else 4)
        t = place(name, shape, dt, c_at[0])
        c_at[0] += (size + 31) // 32 * 32
        return t

    ident = const("ident", [P, P])
    ones = const("ones", [P, P])
    mean_model = const("mean_model", [P, 1])
    mean_head = const("mean_head", [P, 1])
    gains = const("gains", [P, (NORMS + 1) * KT])
    cum64 = const("cum64", [P, P])
    cum16 = const("cum16", [P, P])
    keep64 = const("keep64", [P, P])
    keep16 = const("keep16", [P, P])
    own_rows = const("own_rows", [P, DEC_BATCH])
    w_alpha = const("w_alpha", [R_A + 1, H_A * DK])
    head_gain = const("head_gain", [P, 1])
    bias_f = const("bias_f", [H_C, 1])
    ident_b = const("ident_b", [P, P], BF16)
    causal_b = const("causal_b", [P, P], BF16)
    own_causal_b = const("own_causal_b", [P, 240], BF16)
    causal = place("causal", [P, P], F32, at_g + 2 * T * 4)
    own_causal = place("own_causal", [P, 240], F32, at_g + 2 * T * 4 + P * 4)
    rs = [const(f"rs{i}", [P, 20]) for i in range(4)]
    neg_max = const("neg_max", [P, 8])
    row_sum = const("row_sum", [P, 8])
    row_inv = const("row_inv", [P, 8])
    row_max = const("row_max", [P, 8])
    s_neg_max, s_row_sum, s_row_inv, s_row_max, s_marks = (
        const(n, [P, 2]) for n in ("s_neg_max", "s_row_sum", "s_row_inv", "s_row_max", "s_marks"))
    mark = const("mark", [P, 1])
    marks = const("marks", [P, 8])
    chunk_last = const("chunk_last", [P, 2, 16])
    at_e = (c_at[0] + 63) // 64 * 64
    end = nc.sbuf_usable_end

    tile_b = T * 4
    qa = place("qa", [P, 2, T], F32, at_h)
    ka = place("ka", [P, 2, T], F32, at_h + 2 * tile_b)
    ag = place("ag", [P, 4, T], F32, at_h + 4 * tile_b)
    va = place("va", [P, TT, 512], F32, at_h + 8 * tile_b)
    qb = place("qb", [P, 4, T], F32, at_h + 12 * tile_b)
    kb = place("kb", [P, 4, T], F32, at_h + 16 * tile_b)
    vb = place("vb", [P, TT, 512], F32, at_h + 20 * tile_b)
    ls_tmp = place("ls_tmp", [P, TT * 256], F32, at_g)
    decay = place("decay", [P, 2, T], F32, at_g)
    o_head = place("o_head", [P, H_A, T], F32, at_g)
    ar = place("ar", [R_A + 1, T], F32, at_e)
    log_a = place("log_a", [P, TT * 256], F32, at_e + tile_b)
    e_cum = place("e_cum", [P, 2, T], F32, at_e + 3 * tile_b)
    qa1 = place("qa1", [P, 2, T], F32, at_e + tile_b)
    k_in = place("k_in", [P, 2, T], F32, at_e + 5 * tile_b)
    assert at_e + 7 * tile_b <= end
    sq_head = place("sq_head", [P, T], F32, at_e)
    diag_a = place("diag_a", [P, TT, P], F32, at_e + tile_b)
    o_tmp = place("o_tmp", [P, T], F32, at_e + 2 * tile_b)
    att = place("att", [P, TT, 512], F32, at_xn)
    k_own = place("k_own", [P, DEC_BATCH, 256], F32, at_xn + 10240)
    s_hist = place("s_hist", [P, 9, 2, P], F32, at_xn + 18432)
    k_tok = place("k_tok", [P, TT, 256], F32, at_xn + 27648)
    s_dec = place("s_dec", [P, DEC_BATCH, 2, P], F32, at_xn + 32768)
    qz = place("qz", [P, 2, SEQ], F32, at_e)
    p_s = place("p_s", [P, 2, SEQ], F32, at_e + 4096)
    p_bias = place("p_bias", [P, 2, SEQ], F32, at_e + 8192)
    p_pt = place("p_pt", [P, SEQ], F32, at_e + 12288)
    p_o = place("p_o", [P, P], F32, at_e + 14336)
    assert at_e + 14848 <= end
    s_s = place("s_s", [P, PAST + P], F32, at_g)
    s_bias = place("s_bias", [P, PAST + P], F32, at_g + 4608)
    s_pt = place("s_pt", [P, 512], F32, at_g + 9216)
    qz_s = place("qz_s", [P, 2, 4, 32], F32, at_g + 11264)
    s_o = place("s_o", [P, P], F32, at_g + 12288)
    assert at_g + 12800 <= at_c
    k_cache = place("k_cache", [P, 4, 4, 512], F32, at_w)
    v_cache = place("v_cache", [P, 2, 4, 512], F32, at_w + 4 * SLAB * 4)
    qc = place("qc", [P, KT, T], F32, at_h)
    kc = place("kc", [P, KT, T], F32, at_h + KT * tile_b)
    vc = place("vc", [P, TT, D_MODEL], F32, at_h + 2 * KT * tile_b)
    clf = place("clf", [P, 8, P], F32, at_xn)
    after_w = place("after_w", [P, 1024], F32, at_xn + 4096)
    upto_w = place("upto_w", [P, SEQ], F32, at_xn + 8192)
    c_after = place("c_after", [P, 1024], F32, at_xn + 12288)
    lf = place("lf", [H_C, T], F32, at_xn + 16384)
    lf_tmp = place("lf_tmp", [H_C, T], F32, at_xn + 16384 + tile_b)
    lf_tok = place("lf_tok", [P, TT, H_C], F32, at_xn + 16384 + 2 * tile_b)
    neg_f = place("neg_f", [H_C, T], F32, at_xn + 16384 + 3 * tile_b)
    logit = place("logit", [H_C, T], F32, at_g)

    ps = ctx.enter_context(nc.psum_tensor("ps", [P, 8, 512], F32))

    def unit_ap(u):
        return ps[:, 2 * u:2 * u + 2, 0:HALF]

    def flat(bank, n, cols):
        return ps[:, bank:bank + n, :].rearrange("p b c -> p (b c)")[:, 0:cols]

    def halves(ap):
        return ap.rearrange("p (a c) -> p a c", a=2)

    def tile_of(t, j):
        if isinstance(j, int):
            return halves(t[:, j, :])
        return t[:, bass.ds(j, 1), :].rearrange("p o (a c) -> p (o a) c", a=2)

    def row_of(t, j, lo=0, hi=None):
        if isinstance(j, int):
            return t[:, j, lo:hi]
        return t[:, bass.ds(j, 1), lo:hi].rearrange("p o c -> p (o c)")

    made = {}

    def sem(name):
        if name not in made:
            made[name] = ctx.enter_context(nc.semaphore(name))
        return made[name]

    x_loaded, consts_loaded = sem("x_loaded"), sem("consts_loaded")
    raw_loaded = [sem("raw_loaded0"), sem("raw_loaded1")]
    hi_done, lo_done = sem("hi_done"), sem("lo_done")
    unit_ready, unit_free = sem("unit_ready"), sem("unit_free")
    silu_done, h_hi_done, h_lo_done = sem("silu_done"), sem("h_hi_done"), sem("h_lo_done")
    sq_done, acc_done = sem("sq_done"), sem("acc_done")
    rs_step, diag_done = sem("rs_step"), sem("diag_done")
    xf_done, xn_hi_done, xn_lo_done = sem("xf_done"), sem("xn_hi_done"), sem("xn_lo_done")
    y_stored, masks_cast = sem("y_stored"), sem("masks_cast")

    def slab_src(ph, kind, s):
        k = ph["index"]
        mix = 0 if ph["kind"] == "even" else 1
        src = {"up_a": ins["w_up"][k], "down_a": ins["w_down_a"][k], "up_b": ins["w_up"][k],
               "down_b": ins["w_down_b"][k], "in": ins["w_in"][mix], "out": ins["w_out"][mix]}[kind]
        return src[bass.ds(s, 1)].rearrange("o p c -> p (o c)"), src.shape[2]

    def load_slabs(sp, ph, kind, first, count, n0, fresh=0):
        def one(s, n, slot):
            src, width = slab_src(ph, kind, s)
            sp.wait_ge(lo_done, n - 1)
            sp.dma_start(w_raw[:, slot, 0:width], src).then_inc(raw_loaded[slot], 16)
        for s in range(fresh):
            src, width = slab_src(ph, kind, first + s)
            sp.dma_start(w_raw[:, (n0 + s) % 2, 0:width], src).then_inc(raw_loaded[(n0 + s) % 2], 16)
        with sp.Fori(fresh // 2, count // 2) as i:
            for u in range(2):
                one(first + 2 * i + u, n0 + 2 * i + u, (n0 + u) % 2)

    def small_load(sp, ph):
        n = ph["slab"]
        sp.wait_ge(lo_done, n - 1)
        dst = w_raw[:, n % 2, 0:KT * P].rearrange("p (k c) -> p k c", c=P)[:, :, 0:R_A]
        sp.dma_start(dst, ins["w_small"][0 if ph["kind"] == "even" else 1]).then_inc(raw_loaded[n % 2], 16)

    def hi_next(i, step, u, n0, units_before):
        slot = (n0 + u + 1) % 2
        first_loads = (n0 + u + 1 - slot) // 2 + 1
        nc.scalar.wait_ge(raw_loaded[slot], (i * (step // 2) + first_loads) * 16)
        nc.scalar.wait_ge(unit_ready, units_before)
        nc.scalar.activation(w_hi[:, slot, :], w_raw[:, slot, :], ACT.Copy).then_inc(hi_done, 1)

    def lo_next(pool, n, slot):
        pool.wait_ge(hi_done, n + 1)
        nc.gpsimd.tensor_tensor(out=w_lo[:, slot, :], in0=w_raw[:, slot, :], in1=w_hi[:, slot, :].bitcast(F32),
                                op=ALU.subtract).then_inc(lo_done, 1)

    def mm_tile(unit, slot, tile0, kts, a_hi, a_lo, before_k=None):
        last = None
        for k in range(kts):
            if before_k:
                before_k(k)
            w = (tile0 + k) * P
            terms = [(w_hi, a_hi), (w_hi, a_lo), (w_lo, a_hi)]
            for t, (w_part, a_part) in enumerate(terms):
                for half in range(2):
                    last = nc.tensor.matmul(ps[:, 2 * unit + half, 0:HALF], w_part[:, slot, w:w + P],
                                            a_part[:, k, half * HALF:(half + 1) * HALF],
                                            start=k == 0 and t == 0, stop=k == kts - 1 and t == 2)
        return last

    def pe_slab_start(pe, n):
        pe.wait_ge(lo_done, n + 1)

    RS_OPS = 2 + 3 * 3

    def rs_chain(dve, src, cols, done0, scale=None):
        ms, y, a, b = (t[:, 0:cols] for t in rs)
        nc.vector.tensor_scalar(out=ms, in0=src, scalar1=EPS, scalar2=None, op0=ALU.add).then_inc(rs_step, 1)
        dve.wait_ge(rs_step, done0 + 1)
        nc.vector.tensor_scalar(out=y.bitcast(I32), in0=ms.bitcast(I32), scalar1=-0.5, scalar2=RSQRT_SEED,
                                op0=ALU.mult, op1=ALU.add).then_inc(rs_step, 1)
        n = done0 + 2
        for _ in range(3):
            dve.wait_ge(rs_step, n)
            nc.vector.tensor_tensor(out=a, in0=y, in1=y, op=ALU.mult).then_inc(rs_step, 1)
            dve.wait_ge(rs_step, n + 1)
            nc.vector.scalar_tensor_tensor(out=b, in0=a, scalar=-0.5, in1=ms, op0=ALU.mult,
                                           op1=ALU.mult).then_inc(rs_step, 1)
            dve.wait_ge(rs_step, n + 2)
            nc.vector.scalar_tensor_tensor(out=y, in0=b, scalar=1.5, in1=y, op0=ALU.add,
                                           op1=ALU.mult).then_inc(rs_step, 1)
            n += 3

    RS_NORM0 = {}
    at = 0
    for r in range(NORMS + 1):
        RS_NORM0[r] = at
        at += RS_OPS
        if r < len(PLAN) and PLAN[r]["kind"] == "even":
            RS_NORM0["gla"] = at
            at += RS_OPS
    DIAG0 = {}
    at = 0
    for r in range(NORMS + 1):
        DIAG0[r] = at
        at += TT
        if r < len(PLAN) and PLAN[r]["kind"] == "even":
            DIAG0["gla"] = at
            at += TT * H_A

    XN0 = {}
    at = 0
    for r in range(NORMS + 1):
        XN0[r] = at
        at += KT

    def norm_pe(pe, r, q0):
        pe.wait_ge(acc_done, SQ_STEPS * (r + 1))
        pe.wait_ge(unit_free, q0)
        for tt in range(TT):
            last = nc.tensor.matmul(ps[:, 0, tt:tt + 1], sq_sum[:, tt * P:(tt + 1) * P], mean_model[:, :],
                                    start=True, stop=True)
        last.then_inc(unit_ready, 1)
        pe.wait_ge(diag_done, DIAG0[r] + TT)
        for tt in range(TT):
            last = nc.tensor.matmul(ps[:, 2 + tt // 4, (tt % 4) * P:(tt % 4 + 1) * P], ones[:, :],
                                    gate[:, 0, tt * P:(tt + 1) * P], start=True, stop=True)
        last.then_inc(unit_ready, 3)

    def release(units):
        nc.vector.memset(mark[:, 0:1], 0.0).then_inc(unit_free, units)

    def norm_dve(dve, r, q0, final=False):
        dve.wait_ge(unit_ready, q0 + 1)
        rs_chain(dve, ps[:, 0, 0:TT], TT, RS_NORM0[r])
        dve.wait_ge(rs_step, RS_NORM0[r] + RS_OPS)
        release(1)
        for tt in range(TT):
            nc.vector.tensor_scalar(out=gate[:, 0, tt * P:(tt + 1) * P], in0=ident[:, :],
                                    scalar1=rs[1][:, tt:tt + 1], scalar2=None,
                                    op0=ALU.mult).then_inc(diag_done, 1)
        dve.wait_ge(unit_ready, q0 + 4)
        if r == 0:
            dve.wait_ge(masks_cast, 3)
        for k in range(KT):
            if final:
                dst = y_out[:, k, :]
            else:
                dst = prod[:, k % 2, :]
                if k >= 2:
                    dve.wait_ge(xn_lo_done, XN0[r] + k - 1)
            ins_ = nc.vector.scalar_tensor_tensor(out=dst, in0=x_res[:, k, :],
                                                  scalar=gains[:, r * KT + k:r * KT + k + 1],
                                                  in1=flat(2, 2, T), op0=ALU.mult, op1=ALU.mult)
            ins_.then_inc(xf_done, 1)
        dve.wait_ge(xf_done, XN0[r] + KT)
        release(NORM_UNITS - 1)

    def norm_act(act, r):
        for k in range(KT):
            act.wait_ge(xf_done, XN0[r] + k + 1)
            nc.scalar.activation(xn_hi[:, k, :], prod[:, k % 2, :], ACT.Copy).then_inc(xn_hi_done, 1)

    def norm_pool(pool, r):
        for k in range(KT):
            pool.wait_ge(xn_hi_done, XN0[r] + k + 1)
            nc.gpsimd.tensor_tensor(out=xn_lo[:, k, :], in0=prod[:, k % 2, :], in1=xn_hi[:, k, :].bitcast(F32),
                                    op=ALU.subtract).then_inc(xn_lo_done, 1)

    def add_dve(dve, m, q, u, coef, sq, sq_base):
        dve.wait_ge(unit_ready, q + 1)
        nc.vector.scalar_tensor_tensor(out=tile_of(x_res, m), in0=unit_ap(u), scalar=coef, in1=tile_of(x_res, m),
                                       op0=ALU.mult, op1=ALU.add).then_inc(unit_free, 1)
        if sq:
            acc_dve(dve, m, u, sq_base)

    def acc_dve(dve, m, u, sq_base):
        r_sq, r_acc = sq_base
        dve.wait_ge(sq_done, r_sq + m + 1)
        dve.wait_ge(acc_done, r_acc + 1 + m)
        nc.vector.tensor_tensor(out=sq_sum[:, :], in0=sq_sum[:, :], in1=gate[:, u % 2, :],
                                op=ALU.add).then_inc(acc_done, 1)

    def sq_act(act, m, u, sq_base):
        r_sq, r_acc = sq_base
        if isinstance(m, int):
            if m >= 2:
                act.wait_ge(acc_done, r_acc + m)
        else:
            act.wait_ge(acc_done, r_acc + m)
        nc.scalar.activation(gate[:, u % 2, :], row_of(x_res, m), ACT.Square).then_inc(sq_done, 1)

    def clear_sum(dve, r, after):
        nc.vector.memset(sq_sum[:, :], 0.0).then_inc(acc_done, 1)

    def ffn_segments(ph):
        q = ph["unit"] + NORM_UNITS
        n = ph["slab"]
        segs = []
        for kind, count, per in (("up_a", FF_A, 2), ("down_a", KT, 1), ("up_b", FF_B, 2), ("down_b", KT, 1)):
            segs.append((kind, count, per, n, q))
            n += count
            q += count * per
        return segs

    def ffn_pe(pe, ph):
        f = ph["index"]
        norm_pe(pe, ph["norm"], ph["unit"])
        h0 = f * (FF_A + FF_B)
        for kind, count, per, n0, q0 in ffn_segments(ph):
            if kind.startswith("up"):
                def body(s, u):
                    pe_slab_start(pe, s + n0)
                    for part in range(2):
                        un = (q0 + 2 * u + part) % 4
                        pe.wait_ge(unit_free, s * 2 + (q0 + part - 3))
                        before = (lambda k: pe.wait_ge(xn_lo_done, XN0[ph["norm"]] + k + 1)) if part == 0 else None
                        mm_tile(un, (n0 + u) % 2, part * KT, KT, xn_hi, xn_lo, before).then_inc(unit_ready, 1)
                with pe.Fori(0, count // 2) as i:
                    for u in range(2):
                        body(i * 2 + u, u)
            else:
                kts = FF_A if kind == "down_a" else FF_B
                hb = h0 + (0 if kind == "down_a" else FF_A)
                with pe.Fori(0, count // 4) as i:
                    for u in range(4):
                        s = i * 4 + u
                        pe_slab_start(pe, s + n0)
                        pe.wait_ge(unit_free, s + (q0 - 3))
                        mm_tile((q0 + u) % 4, (n0 + u) % 2, 0, kts, h_hi, h_lo,
                                lambda k: pe.wait_ge(h_lo_done, hb + k + 1)).then_inc(unit_ready, 1)

    def ffn_act(act, ph):
        f = ph["index"]
        norm_act(act, ph["norm"])
        h0 = f * (FF_A + FF_B)
        last_ph = ph is PLAN[-1]
        for kind, count, per, n0, q0 in ffn_segments(ph):
            if kind.startswith("up"):
                hb = h0 + (0 if kind == "up_a" else FF_A)
                with act.Fori(0, count // 2) as i:
                    for u in range(2):
                        s = i * 2 + u
                        hi_next(i, 2, u, n0, s * 2 + q0)
                        act.wait_ge(unit_ready, s * 2 + (q0 + 1))
                        act.wait_ge(unit_free, s * 2 + (q0 - 2))
                        nc.scalar.activation(halves(gate[:, u, :]), unit_ap((q0 + 2 * u) % 4),
                                             ACT.Silu).then_inc(silu_done, 1)
                        act.wait_ge(unit_free, s * 2 + (q0 + 2))
                        nc.scalar.activation(row_of(h_hi, s), prod[:, u, :], ACT.Copy).then_inc(h_hi_done, 1)
            else:
                sq = kind == "down_b"
                r = ph["norm"] + 1
                def body(i, u, step, nxt=True):
                    s = i * step + u
                    if nxt:
                        hi_next(i, step, u, n0, s + q0)
                    if sq:
                        act.wait_ge(unit_free, s + (q0 + 1))
                        sq_act(act, s, u, (KT * r, SQ_STEPS * r))
                if last_ph and kind == "down_b":
                    for s in range(count):
                        body(0, s, 8, s < count - 1)
                else:
                    with act.Fori(0, count // 4) as i:
                        for u in range(4):
                            body(i, u, 4)

    def ffn_pool(pool, ph):
        f = ph["index"]
        norm_pool(pool, ph["norm"])
        h0 = f * (FF_A + FF_B)
        for kind, count, per, n0, q0 in ffn_segments(ph):
            last = ph is PLAN[-1] and kind == "down_b"
            if last:
                for s in range(count - 1):
                    lo_next(pool, n0 + s + 1, (n0 + s + 1) % 2)
                continue
            hb = h0 + (0 if kind == "up_a" else FF_A)
            with pool.Fori(0, count // 2) as i:
                for u in range(2):
                    s = i * 2 + u
                    lo_next(pool, s + (n0 + 1), (n0 + u + 1) % 2)
                    if kind.startswith("up"):
                        pool.wait_ge(h_hi_done, s + (hb + 1))
                        nc.gpsimd.tensor_tensor(out=row_of(h_lo, s), in0=prod[:, u, :],
                                                in1=row_of(h_hi, s).bitcast(F32),
                                                op=ALU.subtract).then_inc(h_lo_done, 1)

    def ffn_dve(dve, ph):
        f = ph["index"]
        norm_dve(dve, ph["norm"], ph["unit"])
        h0 = f * (FF_A + FF_B)
        for kind, count, per, n0, q0 in ffn_segments(ph):
            if kind.startswith("up"):
                hb = h0 + (0 if kind == "up_a" else FF_A)
                if kind == "up_a":
                    dve.wait_ge(xn_lo_done, XN0[ph["norm"]] + KT)
                with dve.Fori(0, count // 2) as i:
                    for u in range(2):
                        s = i * 2 + u
                        dve.wait_ge(unit_ready, s * 2 + (q0 + 2))
                        dve.wait_ge(silu_done, s + (hb + 1))
                        dve.wait_ge(h_lo_done, s + hb)
                        nc.vector.tensor_tensor(out=halves(prod[:, u, :]), in0=halves(gate[:, u, :]),
                                                in1=unit_ap((q0 + 2 * u + 1) % 4),
                                                op=ALU.mult).then_inc(unit_free, 2)
            else:
                sq = kind == "down_b"
                r = ph["norm"] + 1
                if sq:
                    clear_sum(dve, r, None)
                with dve.Fori(0, count // 4) as i:
                    for u in range(4):
                        s = i * 4 + u
                        add_dve(dve, s, s + q0, (q0 + u) % 4, 0.5, False, None)
                        if sq:
                            acc_dve(dve, s, u, (KT * r, SQ_STEPS * r))

    def mix_at(ph):
        q = ph["unit"] + NORM_UNITS
        n = ph["slab"]
        return dict(small=(n, q), fm=(n + 1, q + 4), tok=(n + 1 + IN_SLABS, q + 4 + 2 * IN_SLABS),
                    out=(n + 1 + IN_SLABS + TOK_SLABS, q + IN_UNITS))

    def proj_pe(pe, ph):
        norm_pe(pe, ph["norm"], ph["unit"])
        m = mix_at(ph)
        n0, q0 = m["small"]
        pe_slab_start(pe, n0)
        mm_tile(0, n0 % 2, 0, KT, xn_hi, xn_lo,
                lambda k: pe.wait_ge(xn_lo_done, XN0[ph["norm"]] + k + 1)).then_inc(unit_ready, 4)
        n0, q0 = m["fm"]
        with pe.Fori(0, IN_SLABS // 2) as i:
            for u in range(2):
                s = i * 2 + u
                pe_slab_start(pe, s + n0)
                for part in range(2):
                    pe.wait_ge(unit_free, s * 2 + (q0 + part - 3))
                    mm_tile(2 * u + part, (n0 + u) % 2, part * KT, KT, xn_hi, xn_lo).then_inc(unit_ready, 1)
        n0, q0 = m["tok"]
        with pe.Fori(0, TOK_SLABS // 2) as i:
            for u in range(2):
                s = i * 2 + u
                slot = (n0 + u) % 2
                pe_slab_start(pe, s + n0)
                for tt in range(TT):
                    if tt % 2 == 0:
                        pe.wait_ge(unit_free, s * 4 + (q0 + tt // 2 - 3))
                    for k in range(KT):
                        for t, (a_part, w_part) in enumerate(((xn_hi, w_hi), (xn_hi, w_lo), (xn_lo, w_hi))):
                            last = nc.tensor.matmul(ps[:, tt, 0:256], a_part[:, k, tt * P:(tt + 1) * P],
                                                    w_part[:, slot, k * 256:(k + 1) * 256],
                                                    start=k == 0 and t == 0, stop=k == KT - 1 and t == 2)
                    if tt in (1, 3):
                        last.then_inc(unit_ready, 1)
                    elif tt == 4:
                        last.then_inc(unit_ready, 2)

    def out_pe(pe, ph, ready):
        n0, q0 = mix_at(ph)["out"]
        ready(pe)
        with pe.Fori(0, OUT_SLABS // 2) as i:
            for u in range(2):
                s = i * 2 + u
                pe_slab_start(pe, s + n0)
                for part in range(2):
                    pe.wait_ge(unit_free, s * 2 + (q0 + part - 3))
                    mm_tile(2 * u + part, (n0 + u) % 2, part * KT, KT, xn_hi, xn_lo).then_inc(unit_ready, 1)

    def proj_act(act, ph):
        norm_act(act, ph["norm"])
        m = mix_at(ph)
        n0, q0 = m["small"]
        hi_next(0, 2, 0, n0, q0)
        n0, q0 = m["fm"]
        with act.Fori(0, IN_SLABS // 2) as i:
            for u in range(2):
                hi_next(i, 2, u, n0, (i * 2 + u) * 2 + q0)
        n0, q0 = m["tok"]
        for s in range(TOK_SLABS - 1):
            hi_next(0, 8, s, n0, q0 + 4 * s)

    def out_act(act, ph):
        n0, q0 = mix_at(ph)["out"]
        r = ph["norm"] + 1
        hi_next(0, 8, -1, n0, q0)
        for s in range(OUT_SLABS):
            hi_next(0, 8, s, n0, q0 + 2 * s)
            for part in range(2):
                act.wait_ge(unit_free, q0 + 2 * s + part + 1)
                sq_act(act, 2 * s + part, part, (KT * r, SQ_STEPS * r))

    def proj_pool(pool, ph):
        norm_pool(pool, ph["norm"])
        n0 = ph["slab"]
        lo_next(pool, n0 + 1, (n0 + 1) % 2)
        lo_next(pool, n0 + 2, n0 % 2)
        with pool.Fori(0, (IN_SLABS + TOK_SLABS) // 2 - 1) as i:
            for u in range(2):
                lo_next(pool, i * 2 + (n0 + 3 + u), (n0 + 1 + u) % 2)

    def out_pool(pool, ph):
        n0 = mix_at(ph)["out"][0]
        for s in range(OUT_SLABS + 1):
            lo_next(pool, n0 + s, (n0 + s) % 2)

    def proj_dve(dve, ph, small, fm_tiles, tok_dst):
        norm_dve(dve, ph["norm"], ph["unit"])
        m = mix_at(ph)
        n0, q0 = m["small"]
        dve.wait_ge(unit_ready, q0 + 4)
        small()
        n0, q0 = m["fm"]
        for j, (dst, tile, scale) in enumerate(fm_tiles):
            dve.wait_ge(unit_ready, q0 + j + 1)
            nc.vector.tensor_scalar(out=halves(dst[:, tile, :]), in0=unit_ap(j % 4), scalar1=scale, scalar2=None,
                                    op0=ALU.mult).then_inc(unit_free, 1)
        n0, q0 = m["tok"]
        for s in range(TOK_SLABS):
            dst = tok_dst(s)
            for tt, n, inc in ((0, 2, 1), (2, 2, 1), (4, 1, 2)):
                dve.wait_ge(unit_ready, q0 + 4 * s + (1, 2, 4)[tt // 2])
                nc.vector.tensor_copy(dst[:, tt:tt + n, :], ps[:, tt:tt + n, 0:256]).then_inc(unit_free, inc)

    def out_dve(dve, ph):
        n0, q0 = mix_at(ph)["out"]
        r = ph["norm"] + 1
        clear_sum(dve, r, None)
        with dve.Fori(0, KT // 4) as i:
            for u in range(4):
                s = i * 4 + u
                add_dve(dve, s, s + q0, u, 1.0, True, (KT * r, SQ_STEPS * r))

    PE_ORDER = ("sS0 S0 S1 T0 S2 sT0a V0 sV0a T1 S3 sT0b V1 sV0b T2 X0 S4 sT0c V2 sV0c T3 S5 V3 sX0 sS1 "
                "T4 X1 S6 sT1a V4 sV1a T5 S7 sT1b V5 sV1b T6 X2 sT1c V6 sV1c T7 V7 sX1 X3").split()
    DVE_ORDER = ("sQ0 sQ1 sM0 M0 M1 M2 O0 M3 O1 L0 M4 O2 M5 sO0 O3 sL0 sM1 L1 M6 O4 M7 O5 L2 O6 sO1 O7 sL1 L3"
                 ).split()
    ACT_ORDER = ("Q sE0 E0 E1 C0 sC0a E2 C1 sC0b E3 C2 H0 sC0c E4 C3 E5 sH0 sE1 C4 H1 E6 sC1a C5 sC1b E7 C6 H2 "
                 "sC1c C7 sH1 H3").split()

    class Attention:
        def __init__(self, tag, loops, cached, q, k, v, out0, prompt_bias, bias_cols, masked, sample_bias_dmas):
            self.loops, self.cached, self.q, self.k, self.v, self.out0 = loops, cached, q, k, v, out0
            self.prompt_bias, self.bias_cols, self.masked = prompt_bias, bias_cols, masked
            self.sample_bias_dmas = sample_bias_dmas
            self.chunks = cached // 512
            self.groups = 2 if self.chunks == 2 else 1
            s = lambda n: sem(f"{tag}_{n}")
            two = lambda n: [s(n + "0"), s(n + "1")]
            self.zeroed, self.bias_loaded = s("zeroed"), two("bias_loaded")
            self.qz_done, self.logits_ready, self.max_step = s("qz_done"), s("logits_ready"), s("max_step")
            self.probs_ready, self.pt_ready, self.pt_copied = s("probs_ready"), s("pt_ready"), s("pt_copied")
            self.o_ready, self.inv_done, self.o_scaled = s("o_ready"), s("inv_done"), s("o_scaled")
            self.ot_ready, self.ot_hi, self.ot_lo = s("ot_ready"), s("ot_hi"), s("ot_lo")
            self.sk_loaded, self.sv_loaded, self.sbias_loaded = two("sk_loaded"), two("sv_loaded"), two("sbias_loaded")
            self.sqz_done, self.slogits_ready, self.smax_step = s("sqz_done"), s("slogits_ready"), s("smax_step")
            self.sprobs_ready, self.spt_ready, self.spt_copied = s("sprobs_ready"), s("spt_ready"), s("spt_copied")
            self.sv_used, self.so_ready = s("sv_used"), s("so_ready")
            self.sinv_done, self.so_scaled = s("sinv_done"), s("so_scaled")
            self.sot_ready, self.sot_hi, self.sot_lo = s("sot_ready"), s("sot_hi"), s("sot_lo")

        def stream(self, i, u):
            return (i, u) if self.groups == 2 else (i * 2 + u, 0)

        def parts(self):
            return {"a": (0, 4), "c": (4, 1)} if self.chunks == 1 else {"a": (0, 4), "b": (4, 4), "c": (8, 1)}

        def run(self, order, pieces, i):
            for name in order:
                stage, *arg = (name[:2], name[2:]) if name[0] == "s" else (name[:1], name[1:])
                arg = arg[0]
                if name[0] == "s" and len(arg) == 2:
                    if arg[1] in self.parts():
                        pieces[stage](i, int(arg[0]), arg[1])
                else:
                    pieces[stage](i, *([int(arg)] if arg else []))

        def sp(self, sp, loads):
            def body(i, first):
                def wait(s, value):
                    if not first:
                        sp.wait_ge(s, value)

                def keys(u):
                    wait(self.slogits_ready, i * 2 + (u - 1))
                    loads["keys"](i, u)

                def values(u):
                    for ch in range(self.chunks):
                        n = u * self.chunks + ch
                        if not first or n >= 2:
                            sp.wait_ge(self.sv_used, i * 2 * self.chunks + (n - 1))
                        loads["values"](i, u, ch, n % 2)

                def bias(u):
                    if not first or u:
                        sp.wait_ge(self.smax_step, i * 4 + 2 * u)
                    loads["bias"](i, u)

                keys(0)
                values(0)
                bias(0)
                for hh in range(2):
                    wait(self.max_step, i * 16 + (2 * hh - 2))
                    sp.dma_start(p_bias[:, hh, :], self.prompt_bias(i, hh)).then_inc(self.bias_loaded[hh], 16)
                keys(1)
                values(1)
                bias(1)

            body(0, True)
            with sp.Fori(1, self.loops) as i:
                body(i, False)

        def pe(self, pe):
            parts = self.parts()
            steps = 2 * len(parts)

            def logits(i, l):
                it, hh, n = l // 2, l % 2, P * (l // 2 + 1)
                if l == 0:
                    pe.wait_ge(self.qz_done, i * 2 + 2)
                last = nc.tensor.matmul(ps[:, l % 2, 0:n], qz[:, hh, it * P:(it + 1) * P],
                                        row_of(self.k, i, 0, n), start=True, stop=not self.masked)
                if self.masked:
                    last = nc.tensor.matmul(ps[:, l % 2, n - P:n], ident_b[:, :], causal_b[:, :], start=False,
                                            stop=True)
                last.then_inc(self.logits_ready, 1)

            def turn_probs(i, l):
                pe.wait_ge(self.probs_ready, i * 8 + (l + 1))
                for jt in range(l // 2 + 1):
                    last = nc.tensor.transpose(ps[:, 2, jt * P:(jt + 1) * P], p_s[:, l % 2, jt * P:(jt + 1) * P],
                                               ident[:, :])
                last.then_inc(self.pt_ready, 1)

            def values(i, l):
                it = l // 2
                pe.wait_ge(self.pt_copied, i * 8 + (l + 1))
                pe.wait_ge(self.o_scaled, i * 8 + l)
                pe.wait_ge(self.ot_lo, i * 4 + it)
                for jt in range(it + 1):
                    last = nc.tensor.matmul(ps[:, 3, 0:P], p_pt[:, jt * P:(jt + 1) * P],
                                            self.v[:, jt, bass.ds(i * P, P)], start=jt == 0, stop=jt == it)
                last.then_inc(self.o_ready, 1)

            def turn_out(i, it):
                pe.wait_ge(self.o_scaled, i * 8 + (2 * it + 2))
                nc.tensor.transpose(ps[:, 3, P:2 * P], p_o[:, :], ident[:, :]).then_inc(self.ot_ready, 1)

            def s_logits(i, u):
                b, g = self.stream(i, u)
                pe.wait_ge(self.sk_loaded[u], i * 16 + 16)
                pe.wait_ge(self.sqz_done, i * 4 + (2 * u + 2))
                bank = 4 + self.chunks
                if bank == 6:
                    pe.wait_ge(self.sot_lo, i * 4 + 2 * u)
                for ch in range(self.chunks):
                    for p in range(4):
                        nc.tensor.matmul(ps[32 * p:32 * p + 32, 4 + ch, 0:512], qz_s[:, u, p, :],
                                         k_cache[:, self.chunks * u + ch, p, :], start=True, stop=True)
                if self.masked:
                    nc.tensor.matmul(ps[:, bank, 0:P], ident_b[:, :], own_causal_b[:, bass.ds(112 - b * DEC_SEQ, P)],
                                     start=True, stop=False)
                for p in range(4):
                    last = nc.tensor.matmul(ps[32 * p:32 * p + 32, bank, 0:P], qz_s[:, u, p, :],
                                            self.k[:, 4 * g + p, SEQ:T], start=not self.masked, stop=True)
                last.then_inc(self.slogits_ready, 1)

            def s_turn_probs(i, u, part):
                pe.wait_ge(self.sprobs_ready, i * 2 + (u + 1))
                t0, n = parts[part]
                for j in range(n):
                    last = nc.tensor.transpose(ps[:, 7, j * P:(j + 1) * P], s_s[:, (t0 + j) * P:(t0 + j + 1) * P],
                                               ident[:, :])
                last.then_inc(self.spt_ready, 1)

            def s_values(i, u, part):
                b, g = self.stream(i, u)
                n_part = u * len(parts) + list(parts).index(part)
                pe.wait_ge(self.spt_copied, i * steps + (n_part + 1))
                t0, n = parts[part]
                if part != "c":
                    vi = u * self.chunks + t0 // 4
                    pe.wait_ge(self.sv_loaded[vi % 2], i * (16 * self.chunks) + 16 * (vi // 2 + 1))
                if part == "a" :
                    pe.wait_ge(self.sot_lo, i * 4 + 2 * u)
                for j in range(n):
                    for p in range(4):
                        if part == "c":
                            v = self.v[:, TT - 1, (4 * g + p) * P:(4 * g + p + 1) * P]
                        else:
                            v = v_cache[:, vi % 2, j, p * P:(p + 1) * P]
                        last = nc.tensor.matmul(ps[32 * p:32 * p + 32, 6, P:2 * P],
                                                s_pt[:, j * P + 32 * p:j * P + 32 * p + 32], v,
                                                start=part == "a" and j == 0, stop=part == "c")
                last.then_inc(self.so_ready if part == "c" else self.sv_used, 1)

            def s_turn_out(i, u):
                pe.wait_ge(self.so_scaled, i * 2 + (u + 1))
                nc.tensor.transpose(ps[:, 6, 2 * P:3 * P], s_o[:, :], ident[:, :]).then_inc(self.sot_ready, 1)

            pieces = dict(S=logits, T=turn_probs, V=values, X=turn_out, sS=s_logits, sT=s_turn_probs, sV=s_values,
                          sX=s_turn_out)
            with pe.Fori(0, self.loops) as i:
                self.run(PE_ORDER, pieces, i)

        def act(self, act):
            parts = self.parts()
            act.wait_ge(self.zeroed, 2)

            def queries(i):
                act.wait_ge(self.logits_ready, i * 8)
                for hh in range(2):
                    rows = slice(64 * hh, 64 * hh + 64)
                    src = self.q[rows, bass.ds(i, 1), 0:SEQ].rearrange("p o c -> p (o c)")
                    nc.scalar.activation(qz[rows, hh, :], src, ACT.Copy).then_inc(self.qz_done, 1)

            def exps(i, l):
                n = P * (l // 2 + 1)
                act.wait_ge(self.max_step, i * 16 + (2 * l + 2))
                nc.scalar.activation(p_s[:, l % 2, 0:n], p_s[:, l % 2, 0:n], ACT.Exp, bias=neg_max[:, l:l + 1],
                                     accum_out=row_sum[:, l:l + 1]).then_inc(self.probs_ready, 1)

            def copy_probs(i, l):
                n = P * (l // 2 + 1)
                act.wait_ge(self.pt_ready, i * 8 + (l + 1))
                nc.scalar.activation(p_pt[:, 0:n], ps[:, 2, 0:n], ACT.Copy).then_inc(self.pt_copied, 1)

            def out_hi(i, it):
                act.wait_ge(self.ot_ready, i * 4 + (it + 1))
                nc.scalar.activation(row_of(xn_hi, i + self.out0, it * P, (it + 1) * P), ps[:, 3, P:2 * P],
                                     ACT.Copy).then_inc(self.ot_hi, 1)

            def s_exps(i, u):
                act.wait_ge(self.smax_step, i * 4 + (2 * u + 2))
                cols = self.cached + P
                nc.scalar.activation(s_s[:, 0:cols], s_s[:, 0:cols], ACT.Exp, bias=s_neg_max[:, u:u + 1],
                                     accum_out=s_row_sum[:, u:u + 1]).then_inc(self.sprobs_ready, 1)

            def s_copy_probs(i, u, part):
                n_part = u * len(parts) + list(parts).index(part)
                act.wait_ge(self.spt_ready, i * (2 * len(parts)) + (n_part + 1))
                n = parts[part][1] * P
                nc.scalar.activation(s_pt[:, 0:n], ps[:, 7, 0:n], ACT.Copy).then_inc(self.spt_copied, 1)

            def s_out_hi(i, u):
                b, g = self.stream(i, u)
                act.wait_ge(self.sot_ready, i * 2 + (u + 1))
                for hh in range(2):
                    nc.scalar.activation(self.out_ap(xn_hi, b, g, hh), self.turned(hh),
                                         ACT.Copy).then_inc(self.sot_hi, 1)

            pieces = dict(Q=queries, E=exps, C=copy_probs, H=out_hi, sE=s_exps, sC=s_copy_probs, sH=s_out_hi)
            with act.Fori(0, self.loops) as i:
                self.run(ACT_ORDER, pieces, i)

        def out_ap(self, t, b, g, hh):
            return t[64 * hh:64 * hh + 64, self.out0 + 4 * g:self.out0 + 4 * g + 4,
                     bass.ds(b * DEC_SEQ + SEQ, DEC_SEQ)]

        def turned(self, hh):
            return ps[64 * hh:64 * hh + 64, 6, 2 * P:3 * P].rearrange("p (j h i) -> p j h i", j=4, h=2)[:, :, hh, :]

        def dve(self, dve):
            nc.vector.memset(qz[:, :, :], 0.0).then_inc(self.zeroed, 1)
            nc.vector.memset(qz_s[:, :, :, :], 0.0).then_inc(self.zeroed, 1)
            dve.wait_ge(self.zeroed, 2)

            def maxes(i, l):
                hh, n = l % 2, P * (l // 2 + 1)
                if l < 2:
                    dve.wait_ge(self.bias_loaded[hh], i * 16 + 16)
                dve.wait_ge(self.logits_ready, i * 8 + (l + 1))
                nc.vector.memset(marks[:, l:l + 1], 0.0)
                b0 = self.bias_cols(l // 2)
                nc.vector.tensor_tensor_reduce(out=p_s[:, l % 2, 0:n], in0=p_bias[:, hh, b0:b0 + n],
                                               in1=ps[:, l % 2, 0:n], scale=1.0, scalar=LOWEST, op0=ALU.add,
                                               op1=ALU.max, accum_out=row_max[:, l:l + 1]).then_inc(self.max_step, 1)
                dve.wait_ge(self.max_step, i * 16 + (2 * l + 1))
                nc.vector.tensor_scalar(out=neg_max[:, l:l + 1], in0=row_max[:, l:l + 1], scalar1=-1.0, scalar2=None,
                                        op0=ALU.mult).then_inc(self.max_step, 1)

            def scale_out(i, l):
                hh = l % 2
                dve.wait_ge(self.probs_ready, i * 8 + (l + 1))
                nc.vector.reciprocal(row_inv[:, l:l + 1], row_sum[:, l:l + 1]).then_inc(self.inv_done, 1)
                dve.wait_ge(self.inv_done, i * 8 + (l + 1))
                dve.wait_ge(self.o_ready, i * 8 + (l + 1))
                nc.vector.tensor_scalar(out=p_o[:, 64 * hh:64 * hh + 64], in0=ps[:, 3, 64 * hh:64 * hh + 64],
                                        scalar1=row_inv[:, l:l + 1], scalar2=None,
                                        op0=ALU.mult).then_inc(self.o_scaled, 1)

            def out_lo(i, it):
                dve.wait_ge(self.ot_hi, i * 4 + (it + 1))
                cols = (it * P, (it + 1) * P)
                nc.vector.tensor_tensor(out=row_of(xn_lo, i + self.out0, *cols), in0=ps[:, 3, P:2 * P],
                                        in1=row_of(xn_hi, i + self.out0, *cols).bitcast(F32),
                                        op=ALU.subtract).then_inc(self.ot_lo, 1)

            def s_queries(i, u):
                b, g = self.stream(i, u)
                dve.wait_ge(self.slogits_ready, i * 2)
                for hh in range(2):
                    rows = slice(64 * hh, 64 * hh + 64)
                    nc.vector.tensor_copy(qz_s[rows, u, :, 16 * hh:16 * hh + 16],
                                          self.q[rows, 4 * g:4 * g + 4, bass.ds(b * DEC_SEQ + SEQ, DEC_SEQ)]
                                          ).then_inc(self.sqz_done, 1)

            def s_maxes(i, u):
                cols = self.cached + P
                dmas = self.sample_bias_dmas
                dve.wait_ge(self.sbias_loaded[u], i * (16 * dmas) + 16 * dmas)
                dve.wait_ge(self.slogits_ready, i * 2 + (u + 1))
                nc.vector.memset(s_marks[:, u:u + 1], 0.0)
                nc.vector.tensor_tensor_reduce(out=s_s[:, 0:cols], in0=s_bias[:, 0:cols], in1=flat(4, 3, cols),
                                               scale=1.0, scalar=LOWEST, op0=ALU.add, op1=ALU.max,
                                               accum_out=s_row_max[:, u:u + 1]).then_inc(self.smax_step, 1)
                dve.wait_ge(self.smax_step, i * 4 + (2 * u + 1))
                nc.vector.tensor_scalar(out=s_neg_max[:, u:u + 1], in0=s_row_max[:, u:u + 1], scalar1=-1.0,
                                        scalar2=None, op0=ALU.mult).then_inc(self.smax_step, 1)

            def s_scale_out(i, u):
                dve.wait_ge(self.sprobs_ready, i * 2 + (u + 1))
                nc.vector.reciprocal(s_row_inv[:, u:u + 1], s_row_sum[:, u:u + 1]).then_inc(self.sinv_done, 1)
                dve.wait_ge(self.sinv_done, i * 2 + (u + 1))
                dve.wait_ge(self.so_ready, i * 2 + (u + 1))
                nc.vector.tensor_scalar(out=s_o[:, :], in0=ps[:, 6, P:2 * P], scalar1=s_row_inv[:, u:u + 1],
                                        scalar2=None, op0=ALU.mult).then_inc(self.so_scaled, 1)

            def s_out_lo(i, u):
                b, g = self.stream(i, u)
                for hh in range(2):
                    dve.wait_ge(self.sot_hi, i * 4 + (2 * u + hh + 1))
                    nc.vector.tensor_tensor(out=self.out_ap(xn_lo, b, g, hh), in0=self.turned(hh),
                                            in1=self.out_ap(xn_hi, b, g, hh).bitcast(F32),
                                            op=ALU.subtract).then_inc(self.sot_lo, 1)

            pieces = dict(M=maxes, O=scale_out, L=out_lo, sQ=s_queries, sM=s_maxes, sO=s_scale_out, sL=s_out_lo)
            with dve.Fori(0, self.loops) as i:
                self.run(DVE_ORDER, pieces, i)

        def finished(self, eng):
            eng.wait_ge(self.ot_lo, 4 * self.loops)
            eng.wait_ge(self.sot_lo, 4 * self.loops)

    neg_f_dram = nc.dram_tensor("neg_f_dram", (H_C, T), F32, kind="Internal").ap()
    after_dram = nc.dram_tensor("after_dram", (P, PAST), F32, kind="Internal").ap()
    band = Attention("band", H_B // 2, WIN, qb, kb, vb, 4,
                     lambda i, hh: ins["band_bias"][bass.ds(i, 1), :, hh, :].rearrange("o p c -> p (o c)"),
                     lambda it: 384 - P * it, False, 1)
    fox = Attention("fox", H_C // 2, PAST, qc, kc, vc, 0,
                    lambda i, hh: neg_f_dram[bass.ds(i * 2 + hh, 1), 0:SEQ].broadcast_to([P, SEQ]),
                    lambda it: 0, True, 2)

    def band_loads(sp):
        def keys(i, u):
            sp.dma_start(k_cache[:, u], ins["band_kc"][bass.ds(i * 2 + u, 1)].rearrange("o p j c -> p (o j) c")
                         ).then_inc(band.sk_loaded[u], 16)

        def values(i, u, ch, slot):
            sp.dma_start(v_cache[:, slot], ins["band_vc"][bass.ds(i * 2 + u, 1)].rearrange("o p j c -> p (o j) c")
                         ).then_inc(band.sv_loaded[slot], 16)

        def bias(i, u):
            sp.dma_start(s_bias[:, 0:WIN + P], ins["band_bias_s"][bass.ds(i * 2 + u, 1)]
                         .rearrange("o p c -> p (o c)")).then_inc(band.sbias_loaded[u], 16)

        return dict(keys=keys, values=values, bias=bias)

    def fox_loads(sp):
        def keys(i, u):
            dst = k_cache[:, 2 * u:2 * u + 2].rearrange("p h j c -> p (h j) c")
            sp.dma_start(dst, ins["fox_kc"][u][bass.ds(i, 1)].rearrange("o p j c -> p (o j) c")
                         ).then_inc(fox.sk_loaded[u], 16)

        def values(i, u, ch, slot):
            sp.dma_start(v_cache[:, slot], ins["fox_vc"][u][bass.ds(i, 1), :, 4 * ch:4 * ch + 4, :]
                         .rearrange("o p j c -> p (o j) c")).then_inc(fox.sv_loaded[slot], 16)

        def bias(i, u):
            sp.dma_start(s_bias[:, 0:PAST], after_dram[bass.ds(i * H_C + 8 * u, 8), :].unsqueeze(1)
                         .broadcast_to([8, DEC_SEQ, PAST])).then_inc(fox.sbias_loaded[u], 16)
            sp.dma_start(s_bias[:, PAST:PAST + P], neg_f_dram[8 * u:8 * u + 8, SEQ:T].unsqueeze(1)
                         .broadcast_to([8, DEC_SEQ, P])).then_inc(fox.sbias_loaded[u], 16)

        return dict(keys=keys, values=values, bias=bias)

    g = lambda name: sem("gla_" + name)
    g_pre, g_ls, g_loga, g_cum, g_exp, g_last, g_dec = (g(n) for n in ("pre", "ls", "loga", "cum", "exp", "last", "dec"))
    g_qk, g_kt, g_ktok, g_kown, g_att, g_attm = (g(n) for n in ("qk", "kt", "ktok", "kown", "att", "attm"))
    g_kv, g_s, g_sd, g_o, g_oc, g_sq, g_stat = (g(n) for n in ("kv", "s", "sd", "o", "oc", "sq", "stat"))
    g_r, g_on, g_sg, g_ohi, g_olo, g_ar = (g(n) for n in ("r", "on", "sg", "ohi", "olo", "ar"))
    s_dec_loaded, states_stored = sem("s_dec_loaded"), sem("states_stored")
    kv_even_stored, kv_odd_stored, logf_stored = sem("kv_even_stored"), sem("kv_odd_stored"), sem("logf_stored")
    q_head = (qa, qa1)
    head_rows = [slice(64 * (h % 2), 64 * (h % 2) + 64) for h in range(H_A)]

    def gla_pe(pe, ph):
        m = mix_at(ph)
        pe.wait_ge(unit_free, m["out"][1])
        for tt in range(TT):
            last = nc.tensor.matmul(flat(0, 3, 1280)[:, tt * 256:(tt + 1) * 256], ar[:, tt * P:(tt + 1) * P],
                                    w_alpha[:, :], start=True, stop=True)
        last.then_inc(g_pre, 1)
        pe.wait_ge(g_loga, 1)
        for ft in range(2):
            for tt in range(TT):
                last = nc.tensor.matmul(flat(3 + 2 * ft, 2, T)[:, tt * P:(tt + 1) * P],
                                        log_a[:, tt * 256 + ft * P:tt * 256 + (ft + 1) * P],
                                        (cum16 if tt == TT - 1 else cum64)[:, :], start=True, stop=True)
        last.then_inc(g_cum, 1)
        pe.wait_ge(g_qk, 6)
        for tt in range(TT):
            for ft in range(2):
                last = nc.tensor.transpose(flat(0, 3, 1280)[:, tt * 256 + ft * P:tt * 256 + (ft + 1) * P],
                                           ka[:, ft, tt * P:(tt + 1) * P], ident[:, :])
        last.then_inc(g_kt, 1)
        for tt in range(TT):
            for h in range(H_A):
                cols = slice(tt * P, (tt + 1) * P)
                last = nc.tensor.matmul(ps[:, 3 + tt, h * P:(h + 1) * P], k_in[:, h // 2, cols],
                                        q_head[h % 2][:, h // 2, cols], start=True, stop=True)
            last.then_inc(g_att, 1)
        pe.wait_ge(g_ktok, 1)
        for c in range(SEQ // CHUNK):
            rows = slice(64 * (c % 2), 64 * (c % 2) + 64)
            if c >= 2:
                pe.wait_ge(g_s, 4 * (c - 1))
            for pair in range(2):
                last = nc.tensor.matmul(ps[:, c % 2, pair * 256:(pair + 1) * 256],
                                        k_tok[rows, c // 2, pair * P:(pair + 1) * P],
                                        va[rows, c // 2, pair * 256:(pair + 1) * 256], start=True, stop=True)
            last.then_inc(g_kv, 1)
        pe.wait_ge(g_attm, TT)
        pe.wait_ge(g_s, 4 * (SEQ // CHUNK))
        pe.wait_ge(s_dec_loaded, 16)

        def head_out(h):
            q, pair = q_head[h % 2], h // 2
            o = flat(2 + 2 * (h % 2), 2, T)
            if h >= 2:
                pe.wait_ge(g_oc, h - 1)
            for tt in range(TT):
                nc.tensor.matmul(o[:, tt * P:(tt + 1) * P], va[:, tt, h * P:(h + 1) * P],
                                 att[:, tt, h * P:(h + 1) * P], start=True, stop=False)
                if tt < TT - 1:
                    for c in (2 * tt, 2 * tt + 1):
                        if c:
                            cols = slice(c * CHUNK, (c + 1) * CHUNK)
                            last = nc.tensor.matmul(o[:, cols], s_hist[:, c, pair, :], q[:, pair, cols],
                                                    start=False, stop=c % 2 == 1)
                else:
                    for b in range(DEC_BATCH):
                        cols = slice(SEQ + b * DEC_SEQ, SEQ + (b + 1) * DEC_SEQ)
                        last = nc.tensor.matmul(o[:, cols], s_dec[:, b, pair, :], q[:, pair, cols],
                                                start=False, stop=b == DEC_BATCH - 1)
            last.then_inc(g_o, 1)

        def head_stat(h):
            pe.wait_ge(g_sq, h + 1)
            for tt in range(TT):
                last = nc.tensor.matmul(ps[:, 6, h * TT + tt:h * TT + tt + 1], sq_head[:, tt * P:(tt + 1) * P],
                                        mean_head[:, :], start=True, stop=True)
            last.then_inc(g_stat, 1)

        head_out(0)
        for h in range(1, H_A):
            head_out(h)
            head_stat(h - 1)
        head_stat(H_A - 1)
        pe.wait_ge(g_kown, 1)
        for b in range(DEC_BATCH):
            if b >= 2:
                pe.wait_ge(g_sd, 4 * (b - 1))
            for pair in range(2):
                last = nc.tensor.matmul(ps[:, b % 2, pair * 256:(pair + 1) * 256],
                                        k_own[:, b, pair * P:(pair + 1) * P],
                                        va[:, TT - 1, pair * 256:(pair + 1) * 256], start=True, stop=True)
            last.then_inc(g_kv, 1)
        pe.wait_ge(g_sd, 4 * DEC_BATCH)
        for h in range(H_A):
            pe.wait_ge(diag_done, DIAG0["gla"] + TT * (h + 1))
            for tt in range(TT):
                last = nc.tensor.matmul(flat(0, 2, T)[:, tt * P:(tt + 1) * P], ones[:, :], diag_a[:, tt, :],
                                        start=True, stop=True)
            last.then_inc(g_r, 1)

    def gla_act(act, ph):
        act.wait_ge(g_pre, 1)
        nc.scalar.activation(ls_tmp[:, :], flat(0, 3, 1280), ACT.Abs).then_inc(g_ls, 1)
        act.wait_ge(g_ls, 1)
        nc.scalar.activation(ls_tmp[:, :], ls_tmp[:, :], ACT.Exp, scale=-1.0).then_inc(g_ls, 1)
        act.wait_ge(g_ls, 2)
        nc.scalar.activation(ls_tmp[:, :], ls_tmp[:, :], ACT.Ln, bias=1.0).then_inc(g_ls, 1)
        act.wait_ge(g_cum, 1)
        for ft in range(2):
            nc.scalar.activation(decay[:, ft, :], flat(3 + 2 * ft, 2, T), ACT.Copy).then_inc(g_exp, 1)
        act.wait_ge(g_exp, 2)
        nc.scalar.activation(e_cum[:, :, :], decay[:, :, :], ACT.Exp).then_inc(g_exp, 1)
        nc.scalar.activation(k_in[:, :, :], decay[:, :, :], ACT.Exp, scale=-1.0).then_inc(g_exp, 1)
        act.wait_ge(g_dec, 4)
        nc.scalar.activation(decay[:, :, :], decay[:, :, :], ACT.Exp, scale=-1.0).then_inc(g_exp, 1)
        act.wait_ge(g_kt, 1)
        nc.scalar.activation(k_tok[:, :, :].rearrange("p t c -> p (t c)"), flat(0, 3, 1280),
                             ACT.Copy).then_inc(g_ktok, 1)
        nc.scalar.activation(ag[:, :, :], ag[:, :, :], ACT.Silu).then_inc(g_sg, 1)
        for h in range(H_A):
            act.wait_ge(g_o, h + 1)
            nc.scalar.activation(o_head[:, h, :], flat(2 + 2 * (h % 2), 2, T), ACT.Copy).then_inc(g_oc, 1)
            act.wait_ge(g_oc, h + 1)
            if h:
                act.wait_ge(g_stat, h)
            nc.scalar.activation(sq_head[:, :], o_head[:, h, :], ACT.Square).then_inc(g_sq, 1)
        for h in range(H_A):
            act.wait_ge(g_on, 2 * h + 2)
            nc.scalar.activation(xn_hi[:, h, :], o_head[:, h, :], ACT.Copy).then_inc(g_ohi, 1)

    def gla_dve(dve, ph):
        dve.wait_ge(g_ls, 3)
        nc.vector.scalar_tensor_tensor(out=log_a[:, :], in0=flat(0, 3, 1280), scalar=0.0, in1=ls_tmp[:, :],
                                       op0=ALU.min, op1=ALU.subtract).then_inc(g_loga, 1)
        dve.wait_ge(g_exp, 2)
        spans = ((0, SEQ, CHUNK, 0), (SEQ, T, DEC_SEQ, 8))
        for ft in range(2):
            for lo, hi, n, at_ in spans:
                src = decay[:, ft, lo:hi].rearrange("p (c i) -> p c i", i=n)[:, :, n - 1]
                nc.vector.tensor_copy(chunk_last[:, ft, at_:at_ + 8], src).then_inc(g_last, 1)
        dve.wait_ge(g_last, 4)
        dve.wait_ge(g_exp, 4)
        for ft in range(2):
            for lo, hi, n, at_ in spans:
                nc.vector.tensor_tensor(
                    out=decay[:, ft, lo:hi].rearrange("p (c i) -> p c i", i=n),
                    in0=decay[:, ft, lo:hi].rearrange("p (c i) -> p c i", i=n),
                    in1=chunk_last[:, ft, at_:at_ + 8].unsqueeze(2).broadcast_to([P, 8, n]),
                    op=ALU.subtract).then_inc(g_dec, 1)
        nc.vector.tensor_tensor(out=qa1[64:P, :, :], in0=qa[64:P, :, :], in1=e_cum[64:P, :, :],
                                op=ALU.mult).then_inc(g_qk, 1)
        nc.vector.tensor_tensor(out=qa[0:64, :, :], in0=qa[0:64, :, :], in1=e_cum[0:64, :, :],
                                op=ALU.mult).then_inc(g_qk, 1)
        nc.vector.memset(qa1[0:64, :, :], 0.0).then_inc(g_qk, 1)
        dve.wait_ge(g_qk, 1)
        nc.vector.memset(qa[64:P, :, :], 0.0).then_inc(g_qk, 1)
        nc.vector.tensor_tensor(out=k_in[:, :, :], in0=k_in[:, :, :], in1=ka[:, :, :], op=ALU.mult).then_inc(g_qk, 1)
        dve.wait_ge(g_exp, 5)
        dve.wait_ge(g_qk, 5)
        nc.vector.tensor_tensor(out=ka[:, :, :], in0=ka[:, :, :], in1=decay[:, :, :], op=ALU.mult).then_inc(g_qk, 1)
        for tt in range(TT):
            dve.wait_ge(g_att, tt + 1)
            keep = (keep16 if tt == TT - 1 else keep64)[:, :].unsqueeze(1).broadcast_to([P, H_A, P])
            nc.vector.tensor_tensor(out=att[:, tt, :].rearrange("p (h c) -> p h c", h=H_A),
                                    in0=ps[:, 3 + tt, :].rearrange("p (h c) -> p h c", h=H_A), in1=keep,
                                    op=ALU.mult).then_inc(g_attm, 1)
        dve.wait_ge(g_ktok, 1)
        for c in range(SEQ // CHUNK):
            dve.wait_ge(g_kv, c + 1)
            if c:
                dve.wait_ge(g_s, 4 * c)
            for h in range(H_A):
                rows, pair = head_rows[h], h // 2
                kv = ps[rows, c % 2, pair * 256 + (h % 2) * P:pair * 256 + (h % 2 + 1) * P]
                if c == 0:
                    ins_ = nc.vector.tensor_copy(s_hist[rows, 1, pair, :], kv)
                else:
                    col = (c + 1) * CHUNK - 1
                    ins_ = nc.vector.scalar_tensor_tensor(out=s_hist[rows, c + 1, pair, :],
                                                          in0=s_hist[rows, c, pair, :],
                                                          scalar=e_cum[rows, pair, col:col + 1], in1=kv,
                                                          op0=ALU.mult, op1=ALU.add)
                ins_.then_inc(g_s, 1)
        nc.vector.tensor_tensor(out=k_own[:, :, :], in0=k_tok[:, TT - 1, :].unsqueeze(1).broadcast_to([P, DEC_BATCH, 256]),
                                in1=own_rows[:, :].unsqueeze(2).broadcast_to([P, DEC_BATCH, 256]),
                                op=ALU.mult).then_inc(g_kown, 1)
        for b in range(DEC_BATCH):
            dve.wait_ge(g_kv, SEQ // CHUNK + b + 1)
            for h in range(H_A):
                rows, pair = head_rows[h], h // 2
                col = SEQ + (b + 1) * DEC_SEQ - 1
                nc.vector.scalar_tensor_tensor(
                    out=s_dec[rows, b, pair, :], in0=s_dec[rows, b, pair, :], scalar=e_cum[rows, pair, col:col + 1],
                    in1=ps[rows, b % 2, pair * 256 + (h % 2) * P:pair * 256 + (h % 2 + 1) * P],
                    op0=ALU.mult, op1=ALU.add).then_inc(g_sd, 1)
        dve.wait_ge(g_stat, H_A)
        rs_chain(dve, ps[:, 6, 0:H_A * TT], H_A * TT, RS_NORM0["gla"])
        dve.wait_ge(rs_step, RS_NORM0["gla"] + RS_OPS)
        dve.wait_ge(g_sg, 1)
        dve.wait_ge(states_stored, 32)
        for h in range(H_A):
            if h:
                dve.wait_ge(g_r, h)
            for tt in range(TT):
                nc.vector.tensor_scalar(out=diag_a[:, tt, :], in0=ident[:, :],
                                        scalar1=rs[1][:, h * TT + tt:h * TT + tt + 1], scalar2=None,
                                        op0=ALU.mult).then_inc(diag_done, 1)
            dve.wait_ge(g_r, h + 1)
            if h:
                dve.wait_ge(g_on, 2 * h)
            nc.vector.scalar_tensor_tensor(out=o_tmp[:, :], in0=o_head[:, h, :], scalar=head_gain[:, 0:1],
                                           in1=flat(0, 2, T), op0=ALU.mult, op1=ALU.mult).then_inc(g_on, 1)
            dve.wait_ge(g_on, 2 * h + 1)
            nc.vector.tensor_tensor(out=o_head[:, h, :], in0=o_tmp[:, :], in1=ag[:, h, :],
                                    op=ALU.mult).then_inc(g_on, 1)
            dve.wait_ge(g_ohi, h + 1)
            nc.vector.tensor_tensor(out=xn_lo[:, h, :], in0=o_head[:, h, :], in1=xn_hi[:, h, :].bitcast(F32),
                                    op=ALU.subtract).then_inc(g_olo, 1)

    f_ls, f_lf, f_turned, f_tok, f_sums, f_sbuf = (sem("fgate_" + n) for n in ("ls", "lf", "turned", "tok", "sums", "sbuf"))
    f_loaded, f_scratch = sem("fgate_loaded"), sem("fgate_scratch")

    def fgate_pe(pe, ph):
        pe.wait_ge(unit_free, mix_at(ph)["out"][1])
        pe.wait_ge(f_lf, 1)
        for tt in range(TT):
            last = nc.tensor.transpose(ps[:, 0, tt * H_C:(tt + 1) * H_C], lf[:, tt * P:(tt + 1) * P],
                                       ident[0:H_C, 0:H_C])
        last.then_inc(f_turned, 1)
        pe.wait_ge(f_loaded, 48)
        for t in range(7, -1, -1):
            for bank in ((3, 4) if t >= 4 else (3,)):
                j0 = 512 * (bank - 3)
                n = min(512, P * (t + 1) - j0)
                c0 = 896 - P * t + j0
                nc.tensor.matmul(ps[:, bank, 0:n], clf[:, t, :], after_w[:, c0:c0 + n], start=t == 7,
                                 stop=t == 0 or (bank == 4 and t == 4))
        pe.wait_ge(f_tok, 1)
        for tt in range(TT - 1):
            nc.tensor.matmul(ps[0:H_C, 1, tt * P:SEQ], lf_tok[:, tt, :], upto_w[:, 0:SEQ - tt * P], start=tt == 0,
                             stop=tt == TT - 2)
        nc.tensor.matmul(ps[0:H_C, 2, 0:P], lf_tok[:, TT - 1, :], keep16[:, :], start=True,
                         stop=True).then_inc(f_sums, 1)

    def fgate_act(act, ph):
        act.wait_ge(unit_ready, mix_at(ph)["out"][1])
        act.wait_ge(unit_free, mix_at(ph)["out"][1])
        nc.scalar.activation(lf_tmp[:, :], logit[:, :], ACT.Abs).then_inc(f_ls, 1)
        act.wait_ge(f_ls, 1)
        nc.scalar.activation(lf_tmp[:, :], lf_tmp[:, :], ACT.Exp, scale=-1.0).then_inc(f_ls, 1)
        act.wait_ge(f_ls, 2)
        nc.scalar.activation(lf_tmp[:, :], lf_tmp[:, :], ACT.Ln, bias=1.0).then_inc(f_ls, 1)
        act.wait_ge(f_sums, 1)
        nc.scalar.activation(neg_f[:, :], ps[0:H_C, 1:3, :].rearrange("p b c -> p (b c)")[:, 0:T], ACT.Copy,
                             scale=-1.0).then_inc(f_sbuf, 1)
        nc.scalar.activation(c_after[:, :], flat(3, 2, PAST), ACT.Copy).then_inc(f_sbuf, 1)

    def fgate_dve(dve, ph):
        dve.wait_ge(f_ls, 3)
        nc.vector.scalar_tensor_tensor(out=lf[:, :], in0=logit[:, :], scalar=0.0, in1=lf_tmp[:, :], op0=ALU.min,
                                       op1=ALU.subtract).then_inc(f_lf, 1)
        dve.wait_ge(f_turned, 1)
        nc.vector.tensor_copy(lf_tok[:, :, :].rearrange("p t h -> p (t h)"), ps[:, 0, 0:TT * H_C]).then_inc(f_tok, 1)

    EVEN = next(ph for ph in PLAN if ph["kind"] == "even")
    ODD = next(ph for ph in PLAN if ph["kind"] == "odd")
    consts = [(ident, "ident"), (ones, "ones"), (mean_model, "mean_model"), (mean_head, "mean_head"),
              (gains, "gains"), (cum64, "cum64"), (cum16, "cum16"), (keep64, "keep64"), (keep16, "keep16"),
              (own_rows, "own_rows"), (w_alpha, "w_alpha"), (head_gain, "head_gain"), (bias_f, "bias_f"),
              (causal, "causal"), (own_causal, "own_causal")]
    block = ctx.enter_context(nc.Block())

    @block.sync
    def _(sp):
        for k in range(0, KT, 2):
            sp.dma_start(x_res[:, k:k + 2, :], ins["x"][:, k:k + 2, :]).then_inc(x_loaded, 16)
        for dst, name in consts:
            sp.dma_start(dst[tuple(slice(None) for _ in dst.shape)], ins[name]).then_inc(consts_loaded, 16)
        for ph in PLAN:
            if ph["kind"] == "ffn":
                for kind, count, per, n0, q0 in ffn_segments(ph):
                    first = FF_A if kind == "up_b" else 0
                    load_slabs(sp, ph, kind, first, count, n0, fresh=2 if n0 == 0 else 0)
                continue
            m = mix_at(ph)
            small_load(sp, ph)
            load_slabs(sp, ph, "in", 0, IN_SLABS + TOK_SLABS, m["fm"][0])
            if ph["kind"] == "even":
                sp.wait_ge(unit_free, m["out"][1])
                sp.dma_start(s_dec[:, :, :, :], ins["state"]).then_inc(s_dec_loaded, 16)
                sp.dma_start(outs["band_k"], kb[:, :, :]).then_inc(kv_even_stored, 16)
                sp.dma_start(outs["band_v"], vb[:, :, :]).then_inc(kv_even_stored, 16)
                sp.wait_ge(g_s, 4 * (SEQ // CHUNK))
                sp.dma_start(outs["p_state"], s_hist[:, SEQ // CHUNK, :, :]).then_inc(states_stored, 16)
                sp.wait_ge(g_sd, 4 * DEC_BATCH)
                sp.dma_start(outs["s_state"], s_dec[:, :, :, :]).then_inc(states_stored, 16)
                sp.wait_ge(g_olo, H_A)
                band.sp(sp, band_loads(sp))
                sp.wait_ge(band.slogits_ready, 2 * band.loops)
            else:
                sp.wait_ge(unit_free, m["out"][1])
                sp.dma_start(clf[:, :, :], ins["fox_clogf"]).then_inc(f_loaded, 16)
                sp.dma_start(after_w[:, :], ins["after_w"]).then_inc(f_loaded, 16)
                sp.dma_start(upto_w[:, :], ins["upto_w"]).then_inc(f_loaded, 16)
                sp.dma_start(outs["fox_k"], kc[:, :, :]).then_inc(kv_odd_stored, 16)
                sp.dma_start(outs["fox_v"], vc[:, :, :]).then_inc(kv_odd_stored, 16)
                sp.wait_ge(f_sbuf, 2)
                sp.dma_start(neg_f_dram, neg_f[:, :]).then_inc(f_scratch, 16)
                sp.dma_start(after_dram, c_after[:, :]).then_inc(f_scratch, 16)
                sp.dma_start(outs["fox_logf"], lf[:, :]).then_inc(logf_stored, 16)
                sp.wait_ge(f_scratch, 32)
                fox.sp(sp, fox_loads(sp))
                sp.wait_ge(fox.slogits_ready, 2 * fox.loops)
            load_slabs(sp, ph, "out", 0, 4, m["out"][0])
        for k in range(0, KT, 4):
            sp.wait_ge(xf_done, XN0[NORMS] + k + 4)
            sp.dma_start(outs["y"][:, k:k + 4, :], y_out[:, k:k + 4, :]).then_inc(y_stored, 16)
        sp.wait_ge(y_stored, 32)
        sp.wait_ge(states_stored, 32)
        sp.wait_ge(kv_even_stored, 32)
        sp.wait_ge(kv_odd_stored, 32)
        sp.wait_ge(logf_stored, 16)

    @block.gpsimd
    def _(pool):
        lo_next(pool, 0, 0)
        for ph in PLAN:
            if ph["kind"] == "ffn":
                ffn_pool(pool, ph)
            else:
                proj_pool(pool, ph)
                out_pool(pool, ph)

    @block.scalar
    def _(act):
        act.wait_ge(x_loaded, 64)
        act.wait_ge(consts_loaded, 16 * len(consts))
        for k in range(KT):
            sq_act(act, k, k, (0, 0))
        act.wait_ge(raw_loaded[0], 16)
        nc.scalar.activation(w_hi[:, 0, :], w_raw[:, 0, :], ACT.Copy).then_inc(hi_done, 1)
        for ph in PLAN:
            if ph["kind"] == "ffn":
                ffn_act(act, ph)
            elif ph["kind"] == "even":
                proj_act(act, ph)
                gla_act(act, ph)
                band.act(act)
                band.finished(act)
                act.wait_ge(kv_even_stored, 32)
                out_act(act, ph)
            else:
                proj_act(act, ph)
                fgate_act(act, ph)
                act.wait_ge(f_scratch, 32)
                act.wait_ge(logf_stored, 16)
                fox.act(act)
                fox.finished(act)
                act.wait_ge(kv_odd_stored, 32)
                out_act(act, ph)

    @block.vector
    def _(dve):
        dve.wait_ge(consts_loaded, 16 * len(consts))
        nc.vector.tensor_copy(ident_b[:, :], ident[:, :]).then_inc(masks_cast, 1)
        nc.vector.tensor_copy(causal_b[:, :], causal[:, :]).then_inc(masks_cast, 1)
        nc.vector.tensor_copy(own_causal_b[:, :], own_causal[:, :]).then_inc(masks_cast, 1)
        clear_sum(dve, 0, None)
        for k in range(KT):
            acc_dve(dve, k, k, (0, 0))
        for ph in PLAN:
            if ph["kind"] == "ffn":
                ffn_dve(dve, ph)
            elif ph["kind"] == "even":
                nc.vector.memset(ar[:, :], 1.0).then_inc(g_ar, 1)

                def take_ar():
                    dve.wait_ge(g_ar, 1)
                    nc.vector.tensor_copy(halves(ar[0:R_A, :]), ps[0:R_A, 0:2, 0:HALF]).then_inc(unit_free, 4)

                proj_dve(dve, ph, take_ar,
                         [(qa, 0, SCALE), (qa, 1, SCALE), (ka, 0, 1.0), (ka, 1, 1.0)]
                         + [(ag, j, 1.0) for j in range(4)] + [(qb, j, SCALE) for j in range(4)]
                         + [(kb, j, 1.0) for j in range(4)],
                         lambda s: (va, vb)[s // 2][:, :, (s % 2) * 256:(s % 2 + 1) * 256])
                gla_dve(dve, ph)
                band.dve(dve)
                out_dve(dve, ph)
            else:
                def take_logits():
                    nc.vector.tensor_scalar(out=halves(logit[:, :]), in0=ps[0:H_C, 0:2, 0:HALF],
                                            scalar1=bias_f[:, 0:1], scalar2=None, op0=ALU.add).then_inc(unit_free, 4)

                proj_dve(dve, ph, take_logits,
                         [(qc, j, SCALE) for j in range(KT)] + [(kc, j, 1.0) for j in range(KT)],
                         lambda s: vc[:, :, s * 256:(s + 1) * 256])
                fgate_dve(dve, ph)
                fox.dve(dve)
                out_dve(dve, ph)
        norm_dve(dve, NORMS, UNITS, final=True)

    @block.tensor
    def _(pe):
        pe.wait_ge(consts_loaded, 16 * len(consts))
        pe.wait_ge(masks_cast, 3)
        for ph in PLAN:
            if ph["kind"] == "ffn":
                ffn_pe(pe, ph)
            elif ph["kind"] == "even":
                proj_pe(pe, ph)
                gla_pe(pe, ph)
                pe.wait_ge(g_olo, H_A)
                band.pe(pe)
                out_pe(pe, ph, band.finished)
            else:
                proj_pe(pe, ph)
                fgate_pe(pe, ph)
                pe.wait_ge(f_sbuf, 2)
                fox.pe(pe)
                out_pe(pe, ph, fox.finished)
        norm_pe(pe, NORMS, UNITS)

    ctx.close()


def _layout(i):
    f = np.float32
    a = {k: np.asarray(v) for k, v in i.items()}
    out = {}
    x = np.concatenate([a["x_prompt"].reshape(SEQ, D_MODEL), a["x_sample"].reshape(T - SEQ, D_MODEL)])
    out["x"] = x.T.reshape(KT, P, T).transpose(1, 0, 2)
    gu = a["ffn_w_gu"].reshape(4, KT, P, 2, D_FF // P, P)
    out["w_up"] = gu.transpose(0, 4, 2, 3, 1, 5).reshape(4, D_FF // P, P, SLAB)
    dn = a["ffn_w_down"].reshape(4, D_FF // P, P, KT, P)
    dn = dn.transpose(0, 3, 2, 1, 4)
    out["w_down_a"] = dn[:, :, :, :FF_A].reshape(4, KT, P, FF_A * P)
    out["w_down_b"] = dn[:, :, :, FF_A:].reshape(4, KT, P, FF_B * P)

    def fm(w):
        return w.reshape(KT, P, -1, 2, P).transpose(2, 1, 3, 0, 4).reshape(-1, P, SLAB)

    def tok(w):
        return w.reshape(KT, P, -1, 256).transpose(2, 1, 0, 3).reshape(-1, P, SLAB)

    e, o = a["even_w_in"][0], a["odd_w_in"][0]
    qk, v = H_A * DK, H_A * DV
    aq, ak, av, ag, ar, bq, bk, bv = np.split(e, np.cumsum([qk, qk, v, v, R_A, 512, 512]), axis=1)
    cq, ck, cv, cf = np.split(o, np.cumsum([1024, 1024, 1024]), axis=1)
    out["w_in"] = np.stack([np.concatenate([fm(np.concatenate([aq, ak, ag, bq, bk], 1)), tok(av), tok(bv)]),
                            np.concatenate([fm(np.concatenate([cq, ck], 1)), tok(cv)])])
    out["w_small"] = np.stack([w.reshape(KT, P, R_A).transpose(1, 0, 2) for w in (ar, cf)])
    out["w_out"] = np.stack([fm(a["even_w_out"][0]), fm(a["odd_w_out"][0])])
    out["gains"] = np.concatenate([a["norm_g"].reshape(6, D_MODEL), a["final_norm_g"][None]]
                                  ).reshape(7 * KT, P).T
    out["w_alpha"] = np.concatenate([a["gla_w_alpha_up"][0], a["gla_b_alpha"]])
    out["head_gain"] = a["gla_norm_g"].reshape(P, 1)
    out["bias_f"] = a["fox_b_f"].reshape(H_C, 1)
    st = a["state_gla"][0].reshape(DEC_BATCH, 2, 2, DK, DV)
    out["state"] = st.transpose(2, 3, 0, 1, 4).reshape(P, DEC_BATCH, 2, DV)
    kb = a["cache_band_k"][0].reshape(DEC_BATCH, WIN, 4, P)
    out["band_kc"] = kb.transpose(0, 3, 2, 1)
    out["band_vc"] = a["cache_band_v"][0].reshape(DEC_BATCH, 4, P, 512).transpose(0, 2, 1, 3)
    kf = a["cache_fox_k"][0].reshape(DEC_BATCH, 2, 512, 2, 4, P)
    out["fox_kc"] = kf.transpose(3, 0, 5, 1, 4, 2).reshape(2, DEC_BATCH, P, 8, 512)
    vf = a["cache_fox_v"][0].reshape(DEC_BATCH, 8, P, 2, 512)
    out["fox_vc"] = vf.transpose(3, 0, 2, 1, 4)
    out["fox_clogf"] = a["cache_fox_logf"][0].reshape(DEC_BATCH, 8, P, H_C).transpose(2, 1, 0, 3).reshape(P, 8, P)
    rel = a["band_rel_bias"][0]
    r = np.arange(P)
    c = np.arange(512) - 384
    pb = rel[:, np.clip(r[:, None] - c[None], -128, 128) + 128]
    pb = np.where((c[None] // CHUNK <= r[:, None] // CHUNK)[None], pb, f(NEG))
    out["band_bias"] = pb.reshape(4, 2, P, 512).transpose(0, 2, 1, 3)
    fr = np.arange(DEC_SEQ)
    sb = np.full((DEC_BATCH, H_B, DEC_SEQ, WIN + P), f(NEG))
    for b in range(DEC_BATCH):
        sb[b, :, :, :WIN] = rel[:, np.clip(WIN + fr[:, None] - np.arange(WIN)[None], -128, 128) + 128]
        own = slice(WIN + b * DEC_SEQ, WIN + (b + 1) * DEC_SEQ)
        sb[b, :, :, own] = rel[:, fr[:, None] - fr[None] + 128]
    out["band_bias_s"] = sb.reshape(DEC_BATCH, P, WIN + P)
    eye = np.eye(P, dtype=f)
    t, j = r[:, None], r[None]
    out["ident"], out["ones"] = eye, np.ones((P, P), f)
    out["mean_model"], out["mean_head"] = np.full((P, 1), 1 / D_MODEL, f), np.full((P, 1), 1 / DV, f)
    out["keep64"] = ((t <= j) & (t // CHUNK == j // CHUNK)).astype(f)
    out["keep16"] = ((t <= j) & (t // DEC_SEQ == j // DEC_SEQ)).astype(f)
    out["cum64"] = np.where((t <= j) & (t // CHUNK == j // CHUNK), f(1 / 16), f(0))
    out["cum16"] = np.where((t <= j) & (t // DEC_SEQ == j // DEC_SEQ), f(1 / 16), f(0))
    out["own_rows"] = (t // DEC_SEQ == np.arange(DEC_BATCH)[None]).astype(f)
    out["causal"] = np.where(j > t, f(NEG), f(0))
    d = np.arange(240)[None] - 112
    out["own_causal"] = np.where((d >= 0) & (d <= t % DEC_SEQ), f(0), f(NEG))
    out["after_w"] = (np.arange(1024)[None] - 896 < t).astype(f)
    out["upto_w"] = (np.arange(SEQ)[None] >= t).astype(f)
    return {k: np.ascontiguousarray(v) for k, v in out.items()}


_OUTS = {"y": (P, KT, T), "p_state": (P, 2, P), "s_state": (P, DEC_BATCH, 2, P), "band_k": (P, 4, T),
         "band_v": (P, TT, 512), "fox_k": (P, KT, T), "fox_v": (P, TT, D_MODEL), "fox_logf": (H_C, T)}


def kernel(**inputs):
    import concourse.bacc as bacc
    from concourse.bass_utils import run_bass_kernel_spmd

    arrays = _layout(inputs)
    nc = bacc.Bacc("TRN2", target_bir_lowering=False, num_devices=1)
    ins = {k: nc.dram_tensor("in_" + k, v.shape, mybir.dt.from_np(v.dtype), kind="ExternalInput").ap()
           for k, v in arrays.items()}
    outs = {k: nc.dram_tensor("out_" + k, s, F32, kind="ExternalOutput").ap() for k, s in _OUTS.items()}
    trunk_program(nc, ins, outs)
    r = run_bass_kernel_spmd(nc, [{"in_" + k: v for k, v in arrays.items()}], core_ids=[0]).results[0]
    got = {k: np.asarray(r["out_" + k]) for k in _OUTS}

    def frames(t, width):
        return t.transpose(2, 1, 0).reshape(T, width)

    def tok(t, width):
        return t.transpose(1, 0, 2).reshape(T, width)

    def split(t, tail):
        return (t[:SEQ].reshape(1, SEQ, *tail), t[SEQ:].reshape(DEC_BATCH, DEC_SEQ, *tail))

    yp, ys = split(frames(got["y"], D_MODEL), (D_MODEL,))
    bkp, bks = split(frames(got["band_k"], 512), (H_B, DH))
    bvp, bvs = split(tok(got["band_v"], 512), (H_B, DH))
    fkp, fks = split(frames(got["fox_k"], D_MODEL), (H_C, DH))
    fvp, fvs = split(tok(got["fox_v"], D_MODEL), (H_C, DH))
    flp, fls = split(got["fox_logf"].T, (H_C,))
    ps_ = got["p_state"].reshape(2, DK, 2, DV).transpose(2, 0, 1, 3).reshape(1, 1, H_A, DK, DV)
    ss_ = got["s_state"].reshape(2, DK, DEC_BATCH, 2, DV).transpose(2, 3, 0, 1, 4).reshape(1, DEC_BATCH, H_A, DK, DV)
    out = (yp, ys, ps_, bkp[None], bvp[None], fkp[None], fvp[None], flp[None], ss_, bks[None], bvs[None],
           fks[None], fvs[None], fls[None])
    return tuple(np.ascontiguousarray(t) for t in out)
```

```python
import numpy as np
import concourse.bass as bass
from concourse import mybir
from contextlib import ExitStack

F32 = mybir.dt.float32
F32R = mybir.dt.float32r
BF16 = mybir.dt.bfloat16
I32 = mybir.dt.int32
ALU = mybir.AluOpType
ACT = mybir.ActivationFunctionType

P = 128
D_MODEL, SEQ, DEC_BATCH, DEC_SEQ, PAST = 1024, 512, 8, 16, 1024
T = SEQ + DEC_BATCH * DEC_SEQ
TT = T // P
KT = D_MODEL // P
HALF = T // 2
D_FF = 2816
FF_A = 12
FF_B = D_FF // P - FF_A
CHUNK, WIN = 64, 512
H_A, DK, DV = 4, 64, 128
R_A = 16
H_B, H_C, DH = 8, 16, 64
SCALE = DH ** -0.5
EPS = 1e-6
SLAB = 16 * P
NEG = -1e30
LOWEST = -3e38
RSQRT_SEED = 1597463007.0

FFN_SLABS = FF_A + KT + FF_B + KT
FFN_UNITS = 2 * FF_A + KT + 2 * FF_B + KT
IN_SLABS = 8
TOK_SLABS = 4
OUT_SLABS = 4
MIX_SLABS = 1 + IN_SLABS + TOK_SLABS + OUT_SLABS
IN_UNITS = 1 + 2 * IN_SLABS + 4 * TOK_SLABS
OUT_UNITS = KT
OWN_UNITS = {"even": {2: 2, 4: 2, 8: 2}, "odd": {4: 1, 8: 2}}
SQ_STEPS = KT + 1


def plan():
    out, slab, unit, norm, side = [], 0, 0, 0, 0
    for kind, index in (("ffn", 0), ("even", 0), ("ffn", 1), ("ffn", 2), ("odd", 0), ("ffn", 3)):
        out.append(dict(kind=kind, index=index, slab=slab, unit=unit, norm=norm, side=side,
                        next_side=side if kind == "ffn" else 1 - side))
        side = out[-1]["next_side"]
        slab += FFN_SLABS if kind == "ffn" else MIX_SLABS
        unit += 1 + (FFN_UNITS if kind == "ffn" else IN_UNITS + OUT_UNITS + sum(OWN_UNITS[kind].values()))
        norm += 1
    return out, slab, unit, norm


def trunk_program(nc, ins, outs):
    PLAN, _, UNITS, NORMS = plan()
    ctx = ExitStack()

    base = (nc.sbuf_base + 63) // 64 * 64
    at_x = base
    at_w = at_x + KT * T * 4
    at_a = at_w + 6 * SLAB * 4
    at_in = (at_a, at_a + 24 * T * 4)
    at_hid = (at_a + 16 * T * 4, at_a)
    at_xn, at_h = at_in[0], at_hid[0]
    at_g = at_a + 40 * T * 4
    at_acc = at_g + 4 * T * 4
    at_c = at_acc + T * 4

    def place(name, shape, dt, at):
        return nc.alloc_sbuf_tensor_at(name, shape, dt, offset=at)

    x_res = place("x_res", [P, KT, T], F32, at_x)
    xn = [(place(f"xn_hi{e}", [P, KT, T], F32R, at_in[e]), place(f"xn_lo{e}", [P, KT, T], F32R, at_in[e] + KT * T * 4))
          for e in range(2)]
    hid = [(place(f"h_hi{e}", [P, FF_A, T], F32R, at_hid[e]),
            place(f"h_lo{e}", [P, FF_A, T], F32R, at_hid[e] + FF_A * T * 4))
           for e in range(2)]
    first_squares = place("first_squares", [P, KT, T], F32, at_hid[0])
    y_out = place("y_out", [P, KT, T], F32, at_in[0])
    w_raw = place("w_raw", [P, 2, SLAB], F32, at_w)
    w_hi = place("w_hi", [P, 2, SLAB], F32R, at_w + 2 * SLAB * 4)
    w_lo = place("w_lo", [P, 2, SLAB], F32R, at_w + 4 * SLAB * 4)
    gate = place("gate", [P, 2, T], F32, at_g)
    prod = place("prod", [P, 2, T], F32, at_g + 2 * T * 4)
    sq_sum = place("sq_sum", [P, T], F32, at_acc)

    c_at = [at_c]

    def const(name, shape, dt=F32):
        size = int(np.prod(shape[1:])) * (2 if dt == BF16 else 4)
        t = place(name, shape, dt, c_at[0])
        c_at[0] += (size + 31) // 32 * 32
        return t

    ident = const("ident", [P, P])
    ones = const("ones", [P, P])
    mean_model = const("mean_model", [P, 1])
    mean_head = const("mean_head", [P, 1])
    gains = const("gains", [P, (NORMS + 1) * KT])
    cum64 = const("cum64", [P, P])
    cum16 = const("cum16", [P, P])
    keep64 = const("keep64", [P, P])
    keep16 = const("keep16", [P, P])
    own_rows = const("own_rows", [P, DEC_BATCH])
    w_alpha = const("w_alpha", [R_A + 1, H_A * DK])
    head_gain = const("head_gain", [P, 1])
    bias_f = const("bias_f", [H_C, 1])
    ident_b = const("ident_b", [P, P], BF16)
    causal_b = const("causal_b", [P, P], BF16)
    own_causal_b = const("own_causal_b", [P, 240], BF16)
    causal = place("causal", [P, P], F32, at_g + 2 * T * 4)
    own_causal = place("own_causal", [P, 240], F32, at_g + 2 * T * 4 + P * 4)
    rs = [const(f"rs{i}", [P, 20]) for i in range(4)]
    neg_max = const("neg_max", [P, 8])
    row_sum = const("row_sum", [P, 8])
    row_inv = const("row_inv", [P, 8])
    row_max = const("row_max", [P, 8])
    s_neg_max, s_row_sum, s_row_inv, s_row_max, s_marks = (
        const(n, [P, 2]) for n in ("s_neg_max", "s_row_sum", "s_row_inv", "s_row_max", "s_marks"))
    start_marks = const("start_marks", [P, 5])
    marks = const("marks", [P, 8])
    chunk_last = const("chunk_last", [P, 2, 16])
    at_e = (c_at[0] + 63) // 64 * 64
    end = nc.sbuf_usable_end

    tile_b = T * 4
    inv_rms = place("inv_rms", [P, T], F32, at_e + 7 * tile_b)
    qa = place("qa", [P, 2, T], F32, at_h)
    ka = place("ka", [P, 2, T], F32, at_h + 2 * tile_b)
    ag = place("ag", [P, 4, T], F32, at_h + 4 * tile_b)
    va = place("va", [P, TT, 512], F32, at_h + 8 * tile_b)
    qb = place("qb", [P, 4, T], F32, at_h + 12 * tile_b)
    kb = place("kb", [P, 4, T], F32, at_h + 16 * tile_b)
    vb = place("vb", [P, TT, 512], F32, at_h + 20 * tile_b)
    ls_tmp = place("ls_tmp", [P, TT * 256], F32, at_g)
    decay = place("decay", [P, 2, T], F32, at_g)
    o_head = place("o_head", [P, H_A, T], F32, at_g)
    ar = place("ar", [R_A + 1, T], F32, at_e)
    log_a = place("log_a", [P, TT * 256], F32, at_e + tile_b)
    e_cum = place("e_cum", [P, 2, T], F32, at_e + 3 * tile_b)
    qa1 = place("qa1", [P, 2, T], F32, at_e + tile_b)
    k_in = place("k_in", [P, 2, T], F32, at_e + 5 * tile_b)
    assert at_e + 7 * tile_b <= end
    sq_head = place("sq_head", [P, T], F32, at_e)
    diag_a = place("diag_a", [P, 2, TT, P], F32, at_e + 5 * tile_b)
    o_tmp = place("o_tmp", [P, T], F32, at_e + 7 * tile_b)
    assert at_e + 8 * tile_b <= end
    att = place("att", [P, TT, 512], F32, at_xn)
    k_own = place("k_own", [P, DEC_BATCH, 256], F32, at_xn + 10240)
    s_hist = place("s_hist", [P, 9, 2, P], F32, at_xn + 18432)
    k_tok = place("k_tok", [P, TT, 256], F32, at_g + 2 * tile_b)
    s_dec = place("s_dec", [P, DEC_BATCH, 2, P], F32, at_xn + 32768)
    qz = place("qz", [P, 2, SEQ], F32, at_e)
    p_s = place("p_s", [P, 2, SEQ], F32, at_e + 4096)
    p_bias = place("p_bias", [P, 2, SEQ], F32, at_e + 8192)
    p_pt = place("p_pt", [P, SEQ], F32, at_e + 12288)
    p_o = place("p_o", [P, P], F32, at_e + 14336)
    s_pt = place("s_pt", [P, PAST + P], F32, at_e + 14848)
    assert at_e + 14848 + 4608 <= end
    s_s = place("s_s", [P, PAST + P], F32, at_g)
    s_bias = place("s_bias", [P, PAST + P], F32, at_g + 4608)
    qz_s = place("qz_s", [P, 2, 4, 32], F32, at_g + 9216)
    s_o = place("s_o", [P, P], F32, at_g + 10240)
    assert at_g + 10752 <= at_c
    k_cache = place("k_cache", [P, 4, 4, 512], F32, at_w)
    v_cache = place("v_cache", [P, 2, 4, 512], F32, at_w + 4 * SLAB * 4)
    qc = place("qc", [P, KT, T], F32, at_hid[1])
    kc = place("kc", [P, KT, T], F32, at_hid[1] + KT * tile_b)
    vc = place("vc", [P, TT, D_MODEL], F32, at_hid[1] + 2 * KT * tile_b)
    clf = place("clf", [P, 8, P], F32, at_e)
    after_w = place("after_w", [P, 1024], F32, at_e + 4096)
    c_after = place("c_after", [P, 1024], F32, at_e + 8192)
    upto_w = place("upto_w", [P, SEQ], F32, at_e + 12288)
    lf_tok = place("lf_tok", [P, TT, H_C], F32, at_e + 14336)
    logit = place("logit", [H_C, T], F32, at_g)
    lf = place("lf", [H_C, T], F32, at_g + tile_b)
    lf_tmp = place("lf_tmp", [H_C, T], F32, at_g + 2 * tile_b)
    neg_f = place("neg_f", [H_C, T], F32, at_g + 3 * tile_b)

    ps = ctx.enter_context(nc.psum_tensor("ps", [P, 8, 512], F32))

    def unit_ap(u):
        return ps[:, 2 * u:2 * u + 2, 0:HALF]

    def flat(bank, n, cols):
        return ps[:, bank:bank + n, :].rearrange("p b c -> p (b c)")[:, 0:cols]

    def halves(ap):
        return ap.rearrange("p (a c) -> p a c", a=2)

    def tile_of(t, j):
        if isinstance(j, int):
            return halves(t[:, j, :])
        return t[:, bass.ds(j, 1), :].rearrange("p o (a c) -> p (o a) c", a=2)

    def row_of(t, j, lo=0, hi=None):
        if isinstance(j, int):
            return t[:, j, lo:hi]
        return t[:, bass.ds(j, 1), lo:hi].rearrange("p o c -> p (o c)")

    made = {}

    def sem(name):
        if name not in made:
            made[name] = ctx.enter_context(nc.semaphore(name))
        return made[name]

    x_loaded = [sem(f"x_loaded{i}") for i in range(KT // 2)]
    gains_loaded, consts_loaded = sem("gains_loaded"), sem("consts_loaded")
    raw_loaded = [sem("raw_loaded0"), sem("raw_loaded1")]
    hi_done, lo_done = sem("hi_done"), sem("lo_done")
    half_loaded, half_hi, half_lo = sem("half_loaded"), sem("half_hi"), sem("half_lo")
    unit_ready, unit_free = sem("unit_ready"), sem("unit_free")
    silu_done, h_hi_done, h_lo_done = sem("silu_done"), sem("h_hi_done"), sem("h_lo_done")
    sq_done, acc_done = sem("sq_done"), sem("acc_done")
    rs_step, diag_done = sem("rs_step"), sem("diag_done")
    stats_ready, y_done, xn_hi_done, xn_lo_done = sem("stats_ready"), sem("y_done"), sem("xn_hi_done"), sem("xn_lo_done")
    prod_done, logit_done = sem("prod_done"), sem("logit_done")
    y_stored, masks_cast = sem("y_stored"), sem("masks_cast")

    def slab_src(ph, kind, s):
        k = ph["index"]
        mix = 0 if ph["kind"] == "even" else 1
        src = {"up_a": ins["w_up"][k], "down_a": ins["w_down_a"][k], "up_b": ins["w_up"][k],
               "down_b": ins["w_down_b"][k], "in": ins["w_in"][mix], "out": ins["w_out"][mix]}[kind]
        return src[bass.ds(s, 1)].rearrange("o p c -> p (o c)"), src.shape[2]

    def load_slabs(sp, ph, kind, first, count, n0, fresh=0, given=0):
        def one(s, n, slot):
            src, width = slab_src(ph, kind, s)
            sp.wait_ge(lo_done, n - 1)
            sp.dma_start(w_raw[:, slot, 0:width], src).then_inc(raw_loaded[slot], 16)
        for s in range(given, fresh):
            src, width = slab_src(ph, kind, first + s)
            sp.dma_start(w_raw[:, (n0 + s) % 2, 0:width], src).then_inc(raw_loaded[(n0 + s) % 2], 16)
        with sp.Fori(fresh // 2, count // 2) as i:
            for u in range(2):
                one(first + 2 * i + u, n0 + 2 * i + u, (n0 + u) % 2)

    def small_load(sp, ph):
        n = ph["slab"]
        sp.wait_ge(lo_done, n - 1)
        dst = w_raw[:, n % 2, 0:KT * P].rearrange("p (k c) -> p k c", c=P)[:, :, 0:R_A]
        sp.dma_start(dst, ins["w_small"][0 if ph["kind"] == "even" else 1]).then_inc(raw_loaded[n % 2], 16)

    def hi_next(i, step, u, n0, units_before, cols=SLAB):
        slot = (n0 + u + 1) % 2
        first_loads = (n0 + u + 1 - slot) // 2 + 1
        nc.scalar.wait_ge(raw_loaded[slot], (i * (step // 2) + first_loads) * 16)
        nc.scalar.wait_ge(unit_ready, units_before)
        nc.scalar.activation(w_hi[:, slot, 0:cols], w_raw[:, slot, 0:cols], ACT.Copy).then_inc(hi_done, 1)

    def lo_next(pool, n, slot, cols=SLAB):
        pool.wait_ge(hi_done, n + 1)
        nc.gpsimd.tensor_tensor(out=w_lo[:, slot, 0:cols], in0=w_raw[:, slot, 0:cols],
                                in1=w_hi[:, slot, 0:cols].bitcast(F32),
                                op=ALU.subtract).then_inc(lo_done, 1)

    def mm_tile(unit, slot, tile0, kts, a_hi, a_lo, before_k=None):
        last = None
        for k in range(kts):
            if before_k:
                before_k(k)
            w = (tile0 + k) * P
            terms = [(w_hi, a_hi), (w_hi, a_lo), (w_lo, a_hi)]
            for t, (w_part, a_part) in enumerate(terms):
                for half in range(2):
                    last = nc.tensor.matmul(ps[:, 2 * unit + half, 0:HALF], w_part[:, slot, w:w + P],
                                            a_part[:, k, half * HALF:(half + 1) * HALF],
                                            start=k == 0 and t == 0, stop=k == kts - 1 and t == 2)
        return last

    def pe_slab_start(pe, n):
        pe.wait_ge(lo_done, n + 1)

    RS_OPS = 2 + 3 * 3

    def rs_chain(dve, src, c0, cols, done0):
        ms, y, a, b = (t[:, c0:c0 + cols] for t in rs)
        nc.vector.tensor_scalar(out=ms, in0=src, scalar1=EPS, scalar2=None, op0=ALU.add).then_inc(rs_step, 1)
        dve.wait_ge(rs_step, done0 + 1)
        nc.vector.tensor_scalar(out=y.bitcast(I32), in0=ms.bitcast(I32), scalar1=-0.5, scalar2=RSQRT_SEED,
                                op0=ALU.mult, op1=ALU.add).then_inc(rs_step, 1)
        n = done0 + 2
        for _ in range(3):
            dve.wait_ge(rs_step, n)
            nc.vector.tensor_tensor(out=a, in0=y, in1=y, op=ALU.mult).then_inc(rs_step, 1)
            dve.wait_ge(rs_step, n + 1)
            nc.vector.scalar_tensor_tensor(out=b, in0=a, scalar=-0.5, in1=ms, op0=ALU.mult,
                                           op1=ALU.mult).then_inc(rs_step, 1)
            dve.wait_ge(rs_step, n + 2)
            nc.vector.scalar_tensor_tensor(out=y, in0=b, scalar=1.5, in1=y, op0=ALU.add,
                                           op1=ALU.mult).then_inc(rs_step, 1)
            n += 3

    RS_NORM0 = {}
    at = 0
    for r in range(NORMS + 1):
        RS_NORM0[r] = at
        at += RS_OPS
        if r < len(PLAN) and PLAN[r]["kind"] == "even":
            RS_NORM0["gla"] = at
            at += RS_OPS * H_A
    DIAG0 = {}
    at = 0
    for r in range(NORMS + 1):
        DIAG0[r] = at
        at += TT
        if r < len(PLAN) and PLAN[r]["kind"] == "even":
            DIAG0["gla"] = at
            at += TT * H_A

    def norm_stats(pe, r, q0):
        if r == 0:
            pe.wait_ge(consts_loaded, 16 * len(consts))
        pe.wait_ge(acc_done, SQ_STEPS * (r + 1))
        if q0:
            pe.wait_ge(unit_free, q0 - 2)
        bank = 2 * ((q0 + 1) % 4)
        for tt in range(TT):
            last = nc.tensor.matmul(ps[:, bank, tt:tt + 1], sq_sum[:, tt * P:(tt + 1) * P], mean_model[:, :],
                                    start=True, stop=True)
        last.then_inc(stats_ready, 1)

    def norm_spread(pe, r, q0):
        pe.wait_ge(diag_done, DIAG0[r] + TT)
        bank = 2 * ((q0 + 1) % 4)
        for tt in range(TT):
            last = nc.tensor.matmul(flat(bank, 2, T)[:, tt * P:(tt + 1) * P], ones[:, :],
                                    gate[:, 0, tt * P:(tt + 1) * P], start=True, stop=True)
        last.then_inc(unit_ready, 1)

    def norm_dve(dve, r, q0):
        bank = 2 * ((q0 + 1) % 4)
        dve.wait_ge(stats_ready, r + 1)
        rs_chain(dve, ps[:, bank, 0:TT], 0, TT, RS_NORM0[r])
        dve.wait_ge(rs_step, RS_NORM0[r] + RS_OPS)
        for tt in range(TT):
            nc.vector.tensor_scalar(out=gate[:, 0, tt * P:(tt + 1) * P], in0=ident[:, :],
                                    scalar1=rs[1][:, tt:tt + 1], scalar2=None,
                                    op0=ALU.mult).then_inc(diag_done, 1)
        if r == NORMS:
            return
        dve.wait_ge(unit_ready, q0 + 3)
        nc.vector.tensor_copy(inv_rms[:, :], flat(bank, 2, T)).then_inc(unit_free, 1)
        dve.wait_ge(unit_free, q0 + 1)

    def final_norm(dve, q0):
        norm_dve(dve, NORMS, q0)
        dve.wait_ge(unit_ready, q0 + 1)
        for k in range(KT):
            nc.vector.scalar_tensor_tensor(out=y_out[:, k, :], in0=x_res[:, k, :],
                                           scalar=gains[:, NORMS * KT + k:NORMS * KT + k + 1],
                                           in1=flat(2 * ((q0 + 1) % 4), 2, T), op0=ALU.mult,
                                           op1=ALU.mult).then_inc(y_done, 1)

    def split_dve(dve, r, m, k0, side):
        hi, lo = xn[side]
        g_col = gains[:, r * KT + m:r * KT + m + 1] if isinstance(m, int) else gains[:, bass.ds(m + r * KT, 1)]
        nc.vector.tensor_scalar(out=row_of(hi, m), in0=row_of(x_res, m), scalar1=g_col, scalar2=None,
                                op0=ALU.mult).then_inc(xn_hi_done, 1)
        dve.wait_ge(xn_hi_done, m + (k0 + 1))
        nc.vector.scalar_tensor_tensor(out=row_of(lo, m), in0=row_of(x_res, m), scalar=g_col,
                                       in1=row_of(hi, m).bitcast(F32), op0=ALU.mult,
                                       op1=ALU.subtract).then_inc(xn_lo_done, 1)

    def add_dve(dve, m, q, u, coef):
        dve.wait_ge(unit_ready, q + 1)
        nc.vector.scalar_tensor_tensor(out=tile_of(x_res, m), in0=unit_ap(u), scalar=coef, in1=tile_of(x_res, m),
                                       op0=ALU.mult, op1=ALU.add).then_inc(unit_free, 1)

    def acc_dve(dve, m, u, sq_base):
        r_sq, r_acc = sq_base
        dve.wait_ge(sq_done, r_sq + m + 1)
        dve.wait_ge(acc_done, r_acc + 1 + m)
        nc.vector.tensor_tensor(out=sq_sum[:, :], in0=sq_sum[:, :], in1=gate[:, u % 2, :],
                                op=ALU.add).then_inc(acc_done, 1)

    def sq_act(act, m, u, sq_base):
        r_sq, r_acc = sq_base
        if isinstance(m, int):
            if m >= 2:
                act.wait_ge(acc_done, r_acc + m)
        else:
            act.wait_ge(acc_done, r_acc + m)
        nc.scalar.activation(gate[:, u % 2, :], row_of(x_res, m), ACT.Square).then_inc(sq_done, 1)

    def clear_sum(dve):
        nc.vector.memset(sq_sum[:, :], 0.0).then_inc(acc_done, 1)

    def ffn_segments(ph):
        q = ph["unit"] + 1
        n = ph["slab"]
        segs = []
        for kind, count, per in (("up_a", FF_A, 2), ("down_a", KT, 1), ("up_b", FF_B, 2), ("down_b", KT, 1)):
            segs.append((kind, count, per, n, q))
            n += count
            q += count * per
        return segs

    def next_cols(kind, u):
        return SLAB if u % 4 == 3 else P * (FF_A if kind == "down_a" else FF_B)

    def ffn_pe(pe, ph):
        f, r, first_unit = ph["index"], ph["norm"], ph["unit"]
        (x_hi, x_lo), (h_hi, h_lo) = xn[ph["side"]], hid[ph["side"]]
        h0 = f * (FF_A + FF_B)
        for kind, count, per, n0, q0 in ffn_segments(ph):
            if kind.startswith("up"):
                def tile(s, u, part, q, free, before=None):
                    if free is not None:
                        pe.wait_ge(unit_free, free)
                    mm_tile(q % 4, (n0 + u) % 2, part * KT, KT, x_hi, x_lo, before).then_inc(unit_ready, 1)

                if kind == "up_a":
                    q = first_unit
                    if n0 == 0:
                        pe.wait_ge(half_lo, 1)
                    else:
                        pe_slab_start(pe, n0)
                    tile(0, 0, 0, q, q - 3 if q else None, lambda k: pe.wait_ge(xn_lo_done, KT * r + k + 1))
                    if n0:
                        norm_stats(pe, r, q)
                    pe_slab_start(pe, n0)
                    tile(0, 0, 1, q + 2, q - 1 if q else None)
                    if not n0:
                        norm_stats(pe, r, q)
                    norm_spread(pe, r, q)
                    pe_slab_start(pe, n0 + 1)
                    tile(1, 1, 0, q + 3, q if q else None)
                    tile(1, 1, 1, q + 4, q + 2)
                with pe.Fori(1 if kind == "up_a" else 0, count // 2) as i:
                    for u in range(2):
                        s = i * 2 + u
                        pe_slab_start(pe, s + n0)
                        for part in range(2):
                            tile(s, u, part, q0 + 2 * u + part, s * 2 + (q0 + part - 3))
            else:
                kts = FF_A if kind == "down_a" else FF_B
                hb = h0 + (0 if kind == "down_a" else FF_A)
                with pe.Fori(0, count // 4) as i:
                    for u in range(4):
                        s = i * 4 + u
                        pe_slab_start(pe, s + n0)
                        pe.wait_ge(unit_free, s + (q0 - 3))
                        mm_tile((q0 + u) % 4, (n0 + u) % 2, 0, kts, h_hi, h_lo,
                                lambda k: pe.wait_ge(h_lo_done, hb + k + 1)).then_inc(unit_ready, 1)

    def ffn_act(act, ph):
        f = ph["index"]
        h_hi, h_lo = hid[ph["side"]]
        h0 = f * (FF_A + FF_B)
        last_ph = ph is PLAN[-1]
        for kind, count, per, n0, q0 in ffn_segments(ph):
            if kind.startswith("up"):
                hb = h0 + (0 if kind == "up_a" else FF_A)

                def body(i, u, before):
                    s = i * 2 + u
                    hi_next(i, 2, u, n0, before)
                    act.wait_ge(unit_free, s * 2 + (q0 + 1))
                    nc.scalar.activation(gate[:, u, :], gate[:, u, :], ACT.Silu).then_inc(silu_done, 1)
                    act.wait_ge(prod_done, s + (hb + 1))
                    nc.scalar.activation(row_of(h_hi, s), prod[:, u, :], ACT.Copy).then_inc(h_hi_done, 1)

                if kind == "up_a":
                    body(0, 0, q0 - 1)
                    body(0, 1, q0 + 1)
                with act.Fori(1 if kind == "up_a" else 0, count // 2) as i:
                    for u in range(2):
                        body(i, u, (i * 2 + u) * 2 + q0)
            else:
                sq = kind == "down_b"
                r = ph["norm"] + 1
                def body(i, u, step, nxt=True):
                    s = i * step + u
                    if nxt:
                        hi_next(i, step, u, n0, s + q0, next_cols(kind, u))
                    if sq:
                        act.wait_ge(unit_free, s + (q0 + 1))
                        sq_act(act, s, u, (KT * r, SQ_STEPS * r))
                if last_ph and kind == "down_b":
                    for s in range(count):
                        body(0, s, 8, s < count - 1)
                else:
                    with act.Fori(0, count // 4) as i:
                        for u in range(4):
                            body(i, u, 4)

    def ffn_pool(pool, ph):
        f = ph["index"]
        h_hi, h_lo = hid[ph["side"]]
        h0 = f * (FF_A + FF_B)
        for kind, count, per, n0, q0 in ffn_segments(ph):
            last = ph is PLAN[-1] and kind == "down_b"
            if last:
                for s in range(count - 1):
                    lo_next(pool, n0 + s + 1, (n0 + s + 1) % 2, next_cols(kind, s))
                continue
            if kind.startswith("down"):
                with pool.Fori(0, count // 4) as i:
                    for u in range(4):
                        lo_next(pool, i * 4 + (u + n0 + 1), (n0 + u + 1) % 2, next_cols(kind, u))
                continue
            hb = h0 + (0 if kind == "up_a" else FF_A)
            with pool.Fori(0, count // 2) as i:
                for u in range(2):
                    s = i * 2 + u
                    lo_next(pool, s + (n0 + 1), (n0 + u + 1) % 2)
                    pool.wait_ge(h_hi_done, s + (hb + 1))
                    nc.gpsimd.tensor_tensor(out=row_of(h_lo, s), in0=prod[:, u, :],
                                            in1=row_of(h_hi, s).bitcast(F32),
                                            op=ALU.subtract).then_inc(h_lo_done, 1)

    def ffn_dve(dve, ph):
        f = ph["index"]
        norm_dve(dve, ph["norm"], ph["unit"])
        h0 = f * (FF_A + FF_B)
        for kind, count, per, n0, q0 in ffn_segments(ph):
            if kind.startswith("up"):
                hb = h0 + (0 if kind == "up_a" else FF_A)

                def body(s, u, g_unit, u_unit):
                    dve.wait_ge(unit_ready, s * 2 + (q0 + 1))
                    if not isinstance(s, int) or s + hb - 1 > 0:
                        dve.wait_ge(h_lo_done, s + (hb - 1))
                    nc.vector.tensor_tensor(out=halves(gate[:, u, :]), in0=unit_ap(g_unit % 4),
                                            in1=halves(inv_rms[:, :]), op=ALU.mult).then_inc(unit_free, 1)
                    dve.wait_ge(unit_ready, s * 2 + (q0 + 2))
                    nc.vector.tensor_tensor(out=halves(prod[:, u, :]), in0=unit_ap(u_unit % 4),
                                            in1=halves(inv_rms[:, :]), op=ALU.mult).then_inc(unit_free, 1)
                    dve.wait_ge(silu_done, s + (hb + 1))
                    dve.wait_ge(unit_free, s * 2 + (q0 + 2))
                    nc.vector.tensor_tensor(out=prod[:, u, :], in0=prod[:, u, :], in1=gate[:, u, :],
                                            op=ALU.mult).then_inc(prod_done, 1)

                if kind == "up_a":
                    if ph["norm"] == 0:
                        dve.wait_ge(masks_cast, 3)
                    body(0, 0, q0 - 1, q0 + 1)
                    body(1, 1, q0 + 2, q0 + 3)
                with dve.Fori(1 if kind == "up_a" else 0, count // 2) as i:
                    for u in range(2):
                        body(i * 2 + u, u, q0 + 2 * u, q0 + 2 * u + 1)
            else:
                sq = kind == "down_b"
                r = ph["norm"] + 1
                if sq:
                    clear_sum(dve)
                with dve.Fori(0, count // 4) as i:
                    for u in range(4):
                        s = i * 4 + u
                        add_dve(dve, s, s + q0, (q0 + u) % 4, 0.5)
                        if sq:
                            dve.wait_ge(unit_free, s + (q0 + 1))
                            if r < NORMS:
                                split_dve(dve, r, s, KT * r, ph["next_side"])
                            acc_dve(dve, s, u, (KT * r, SQ_STEPS * r))

    def mix_at(ph):
        q = ph["unit"]
        n = ph["slab"]
        own = sum(OWN_UNITS[ph["kind"]].values())
        return dict(small=(n, q), fm=(n + 1, q + 2), tok=(n + 1 + IN_SLABS, q + 2 + 2 * IN_SLABS + own),
                    out=(n + 1 + IN_SLABS + TOK_SLABS, q + 1 + IN_UNITS + own))

    def fm_unit(ph, s):
        return ph["unit"] + 2 + sum(n for at_, n in OWN_UNITS[ph["kind"]].items() if at_ <= s)

    def fm_runs(ph):
        cuts = [2] + [at_ for at_ in OWN_UNITS[ph["kind"]] if 2 < at_ < IN_SLABS] + [IN_SLABS]
        return list(zip(cuts, cuts[1:]))

    def proj_pe(pe, ph, own):
        m, r = mix_at(ph), ph["norm"]
        x_hi, x_lo = xn[ph["side"]]
        n0, q = m["small"]
        pe_slab_start(pe, n0)
        pe.wait_ge(unit_free, q - 3)
        mm_tile(q % 4, n0 % 2, 0, KT, x_hi, x_lo, lambda k: pe.wait_ge(xn_lo_done, KT * r + k + 1)
                ).then_inc(unit_ready, 1)
        norm_stats(pe, r, q)
        n0, q0 = m["fm"]

        def tile(u, part, free):
            pe.wait_ge(unit_free, free)
            mm_tile((q0 + 2 * u + part) % 4, (n0 + u) % 2, part * KT, KT, x_hi, x_lo).then_inc(unit_ready, 1)

        pe_slab_start(pe, n0)
        tile(0, 0, q0 - 3)
        norm_spread(pe, r, q)
        tile(0, 1, q0 - 2)
        pe_slab_start(pe, n0 + 1)
        tile(1, 0, q0)
        tile(1, 1, q0)
        for lo, hi in fm_runs(ph):
            own(lo)
            q0 = fm_unit(ph, lo)
            with pe.Fori(lo // 2, hi // 2) as i:
                for u in range(2):
                    s = i * 2 + u
                    pe_slab_start(pe, s + n0)
                    for part in range(2):
                        tile(u, part, s * 2 + (q0 + part - 3))
        own(IN_SLABS)
        n0, q0 = m["tok"]
        with pe.Fori(0, TOK_SLABS // 2) as i:
            for u in range(2):
                s = i * 2 + u
                slot = (n0 + u) % 2
                pe_slab_start(pe, s + n0)
                for tt in range(TT):
                    if tt % 2 == 0:
                        pe.wait_ge(unit_free, s * 4 + (q0 + tt // 2 - 3))
                    for k in range(KT):
                        for t, (a_part, w_part) in enumerate(((x_hi, w_hi), (x_hi, w_lo), (x_lo, w_hi))):
                            last = nc.tensor.matmul(ps[:, (2 * q0 + tt) % 8, 0:256], a_part[:, k, tt * P:(tt + 1) * P],
                                                    w_part[:, slot, k * 256:(k + 1) * 256],
                                                    start=k == 0 and t == 0, stop=k == KT - 1 and t == 2)
                    if tt in (1, 3):
                        last.then_inc(unit_ready, 1)
                    elif tt == 4:
                        last.then_inc(unit_ready, 2)

    def out_pe(pe, ph, ready):
        n0, q0 = mix_at(ph)["out"]
        ready(pe)
        with pe.Fori(0, OUT_SLABS // 2) as i:
            for u in range(2):
                s = i * 2 + u
                pe_slab_start(pe, s + n0)
                for part in range(2):
                    pe.wait_ge(unit_free, s * 2 + (q0 + part - 3))
                    mm_tile((q0 + 2 * u + part) % 4, (n0 + u) % 2, part * KT, KT, *xn[ph["side"]]
                            ).then_inc(unit_ready, 1)

    def proj_act(act, ph, own):
        m = mix_at(ph)
        n0, q0 = m["small"]
        hi_next(0, 2, 0, n0, q0)
        n0, q0 = m["fm"]
        hi_next(0, 2, 0, n0, q0 - 1)
        hi_next(0, 2, 1, n0, q0 + 2)
        for s in range(2, IN_SLABS):
            hi_next(0, 8, s, n0, fm_unit(ph, s - 1) + 2 * s)
            own(s)
        n0, q0 = m["tok"]
        for s in range(TOK_SLABS - 1):
            hi_next(0, 8, s, n0, q0 + 4 * s)
            own(IN_SLABS + s)

    def out_first(act, ph, attention):
        act.wait_ge(attention.slogits_ready, 2 * attention.loops + 1)
        hi_next(0, 8, -1, *mix_at(ph)["out"])

    def out_act(act, ph):
        n0, q0 = mix_at(ph)["out"]
        r = ph["norm"] + 1
        for s in range(OUT_SLABS):
            hi_next(0, 8, s, n0, q0 + 2 * s)
            for part in range(2):
                act.wait_ge(unit_free, q0 + 2 * s + part + 1)
                sq_act(act, 2 * s + part, part, (KT * r, SQ_STEPS * r))

    def proj_pool(pool, ph):
        n0 = ph["slab"]
        lo_next(pool, n0 + 1, (n0 + 1) % 2)
        lo_next(pool, n0 + 2, n0 % 2)
        with pool.Fori(0, (IN_SLABS + TOK_SLABS) // 2 - 1) as i:
            for u in range(2):
                lo_next(pool, i * 2 + (n0 + 3 + u), (n0 + 1 + u) % 2)

    def out_pool(pool, ph, attention):
        n0 = mix_at(ph)["out"][0]
        pool.wait_ge(attention.sv_used, 2 * attention.loops * attention.chunks)
        for s in range(OUT_SLABS + 1):
            lo_next(pool, n0 + s, (n0 + s) % 2)

    def proj_dve(dve, ph, small, fm_tiles, tok_dst, own):
        norm_dve(dve, ph["norm"], ph["unit"])
        m = mix_at(ph)
        small(m["small"][1] % 4)
        n0, q0 = m["fm"]
        for j, (dst, tile, scale) in enumerate(fm_tiles):
            own(j)
            q0 = fm_unit(ph, j // 2)
            dve.wait_ge(unit_ready, q0 + j + 1)
            nc.vector.scalar_tensor_tensor(out=halves(dst[:, tile, :]), in0=unit_ap((q0 + j) % 4), scalar=scale,
                                           in1=halves(inv_rms[:, :]), op0=ALU.mult, op1=ALU.mult
                                           ).then_inc(unit_free, 1)
        own(2 * IN_SLABS)
        n0, q0 = m["tok"]
        for s in range(TOK_SLABS):
            dst = tok_dst(s)
            for tt in range(TT):
                dve.wait_ge(unit_ready, q0 + 4 * s + (1, 2, 4)[tt // 2])
                ins_ = nc.vector.tensor_scalar(out=dst[:, tt, :], in0=ps[:, (2 * q0 + tt) % 8, 0:256],
                                               scalar1=rs[1][:, tt:tt + 1], scalar2=None, op0=ALU.mult)
                if tt in (1, 3, 4):
                    ins_.then_inc(unit_free, 2 if tt == 4 else 1)

    def out_dve(dve, ph):
        n0, q0 = mix_at(ph)["out"]
        r = ph["norm"] + 1
        clear_sum(dve)
        with dve.Fori(0, KT // 4) as i:
            for u in range(4):
                s = i * 4 + u
                add_dve(dve, s, s + q0, (q0 + u) % 4, 1.0)
                dve.wait_ge(unit_free, s + (q0 + 1))
                split_dve(dve, r, s, KT * r, ph["next_side"])
                acc_dve(dve, s, u, (KT * r, SQ_STEPS * r))

    PE_HEAD, DVE_HEAD, ACT_HEAD = "S0 S1 sS0".split(), "sQ0 sQ1 M0 M1 sM0".split(), "Q E0 E1 sE0".split()
    PE_ORDER = ("T0 S2 sT0a sT0b sT0c V0 sV0a T1 S3 V1 sV0b sS1 T2 X0 S4 V2 sV0c T3 S5 V3 sX0 T4 X1 S6 "
                "sT1a sT1b sT1c V4 sV1a T5 S7 V5 sV1b sS0+ T6 X2 V6 sV1c T7 S0+ S1+ V7 sX1 X3").split()
    DVE_ORDER = ("M2 O0 M3 O1 sM1 L0 M4 O2 sO0 M5 O3 sL0 L1 sQ0+ sQ1+ M6 O4 M7 O5 sM0+ L2 O6 sO1 M0+ O7 M1+ sL1 L3"
                 ).split()
    ACT_ORDER = ("C0 E2 sC0a sC0b sC0c C1 E3 C2 H0 E4 sE1 C3 E5 sH0 C4 H1 E6 sC1a sC1b sC1c C5 E7 Q+ C6 W H2 sE0+ "
                 "C7 E0+ E1+ sH1 H3").split()

    class Attention:
        def __init__(self, tag, loops, cached, q, k, v, out0, out, prompt_bias, bias_cols, masked, sample_bias_dmas):
            self.loops, self.cached, self.q, self.k, self.v, self.out0 = loops, cached, q, k, v, out0
            self.o_hi, self.o_lo = out
            self.prompt_bias, self.bias_cols, self.masked = prompt_bias, bias_cols, masked
            self.sample_bias_dmas = sample_bias_dmas
            self.chunks = cached // 512
            self.groups = 2 if self.chunks == 2 else 1
            s = lambda n: sem(f"{tag}_{n}")
            two = lambda n: [s(n + "0"), s(n + "1")]
            self.zeroed, self.bias_loaded = s("zeroed"), two("bias_loaded")
            self.qz_done, self.logits_ready, self.max_step = s("qz_done"), s("logits_ready"), s("max_step")
            self.probs_ready, self.pt_ready, self.pt_copied = s("probs_ready"), s("pt_ready"), s("pt_copied")
            self.o_ready, self.inv_done, self.o_scaled = s("o_ready"), s("inv_done"), s("o_scaled")
            self.ot_ready, self.ot_hi, self.ot_lo = s("ot_ready"), s("ot_hi"), s("ot_lo")
            self.sk_loaded, self.sv_loaded, self.sbias_loaded = two("sk_loaded"), two("sv_loaded"), two("sbias_loaded")
            self.sqz_done, self.slogits_ready, self.smax_step = s("sqz_done"), s("slogits_ready"), s("smax_step")
            self.sprobs_ready, self.spt_ready, self.spt_copied = s("sprobs_ready"), s("spt_ready"), s("spt_copied")
            self.sv_used, self.so_ready = s("sv_used"), s("so_ready")
            self.sinv_done, self.so_scaled = s("sinv_done"), s("so_scaled")
            self.sot_ready, self.sot_hi, self.sot_lo = s("sot_ready"), s("sot_hi"), s("sot_lo")

            self.started = [self.logits_ready, self.slogits_ready, self.o_scaled, self.ot_lo, self.sot_lo]

        def stream(self, i, u):
            return (i, u) if self.groups == 2 else (i * 2 + u, 0)

        def parts(self):
            return {"a": (0, 4), "c": (4, 1)} if self.chunks == 1 else {"a": (0, 4), "b": (4, 4), "c": (8, 1)}

        def run(self, order, pieces, i, last=False):
            for name in order:
                ahead, name = name.endswith("+"), name.rstrip("+")
                if (ahead and last) or (name == "W" and not last):
                    continue
                it = i + 1 if ahead else i
                stage, arg = (name[:2], name[2:]) if name[0] == "s" else (name[:1], name[1:])
                if len(arg) == 2:
                    if arg[1] in self.parts():
                        pieces[stage](it, int(arg[0]), arg[1])
                else:
                    pieces[stage](it, *([int(arg)] if arg else []))

        def loop(self, eng, head, order, pieces):
            self.run(head, pieces, 0)
            with eng.Fori(0, self.loops - 1) as i:
                self.run(order, pieces, i)
            self.run(order, pieces, self.loops - 1, last=True)

        def sp(self, sp, loads, space_free=None, then=None):
            def body(i, first):
                def wait(s, value):
                    if not first:
                        sp.wait_ge(s, value)

                def keys(u):
                    wait(self.slogits_ready, i * 2 + u)
                    loads["keys"](i, u)

                def value_chunk(u, ch):
                    n = u * self.chunks + ch
                    if not first or n >= 2:
                        sp.wait_ge(self.sv_used, i * 2 * self.chunks + (n - 1))
                    loads["values"](i, u, ch, n % 2)

                def bias(u):
                    if not first or u:
                        sp.wait_ge(self.smax_step, i * 4 + 2 * u)
                    loads["bias"](i, u)

                def prompt_bias():
                    for hh in range(2):
                        wait(self.max_step, i * 16 + (2 * hh - 2))
                        sp.dma_start(p_bias[:, hh, :], self.prompt_bias(i, hh)).then_inc(self.bias_loaded[hh], 16)

                keys(0)
                if first:
                    if space_free:
                        keys(1)
                        value_chunk(0, 0)
                        space_free()
                    bias(0)
                    prompt_bias()
                    if not space_free:
                        for ch in range(self.chunks):
                            value_chunk(0, ch)
                        keys(1)
                else:
                    keys(1)
                    bias(0)
                    value_chunk(0, 0)
                    prompt_bias()
                    if self.chunks == 2:
                        value_chunk(0, 1)
                bias(1)
                for ch in range(self.chunks):
                    value_chunk(1, ch)

            body(0, True)
            if then:
                then()
            with sp.Fori(1, self.loops) as i:
                body(i, False)

        def pe(self, pe):
            parts = self.parts()
            steps = 2 * len(parts)

            def logits(i, l):
                it, hh, n = l // 2, l % 2, P * (l // 2 + 1)
                if l == 0:
                    pe.wait_ge(self.qz_done, i * 2 + 2)
                last = nc.tensor.matmul(ps[:, l % 2, 0:n], qz[:, hh, it * P:(it + 1) * P],
                                        row_of(self.k, i, 0, n), start=True, stop=not self.masked)
                if self.masked:
                    last = nc.tensor.matmul(ps[:, l % 2, n - P:n], ident_b[:, :], causal_b[:, :], start=False,
                                            stop=True)
                last.then_inc(self.logits_ready, 1)

            def turn_probs(i, l):
                pe.wait_ge(self.probs_ready, i * 8 + (l + 1))
                for jt in range(l // 2 + 1):
                    last = nc.tensor.transpose(ps[:, 2, jt * P:(jt + 1) * P], p_s[:, l % 2, jt * P:(jt + 1) * P],
                                               ident[:, :])
                last.then_inc(self.pt_ready, 1)

            def values(i, l):
                it = l // 2
                pe.wait_ge(self.pt_copied, i * 8 + (l + 1))
                pe.wait_ge(self.o_scaled, i * 8 + (l + 1))
                pe.wait_ge(self.ot_lo, i * 4 + (it + 1))
                for jt in range(it + 1):
                    last = nc.tensor.matmul(ps[:, 3, 0:P], p_pt[:, jt * P:(jt + 1) * P],
                                            self.v[:, jt, bass.ds(i * P, P)], start=jt == 0, stop=jt == it)
                last.then_inc(self.o_ready, 1)

            def turn_out(i, it):
                pe.wait_ge(self.o_scaled, i * 8 + (2 * it + 3))
                nc.tensor.transpose(ps[:, 3, P:2 * P], p_o[:, :], ident[:, :]).then_inc(self.ot_ready, 1)

            def s_logits(i, u):
                b, g = self.stream(i, u)
                pe.wait_ge(self.sk_loaded[u], i * 16 + 16)
                pe.wait_ge(self.sqz_done, i * 4 + (2 * u + 2))
                if not isinstance(i, int) or 2 * i + u:
                    pe.wait_ge(self.spt_copied, i * steps + u * len(parts))
                bank = 4 + self.chunks
                for ch in range(self.chunks):
                    for p in range(4):
                        nc.tensor.matmul(ps[32 * p:32 * p + 32, 4 + ch, 0:512], qz_s[:, u, p, :],
                                         k_cache[:, self.chunks * u + ch, p, :], start=True, stop=True)
                if self.masked:
                    nc.tensor.matmul(ps[:, bank, 0:P], ident_b[:, :], own_causal_b[:, bass.ds(112 - b * DEC_SEQ, P)],
                                     start=True, stop=False)
                for p in range(4):
                    last = nc.tensor.matmul(ps[32 * p:32 * p + 32, bank, 0:P], qz_s[:, u, p, :],
                                            self.k[:, 4 * g + p, SEQ:T], start=not self.masked, stop=True)
                last.then_inc(self.slogits_ready, 1)

            def s_turn_probs(i, u, part):
                pe.wait_ge(self.sprobs_ready, i * 2 + (u + 1))
                t0, n = parts[part]
                for j in range(n):
                    last = nc.tensor.transpose(ps[:, 4 + t0 // 4, j * P:(j + 1) * P], s_s[:, (t0 + j) * P:(t0 + j + 1) * P],
                                               ident[:, :])
                last.then_inc(self.spt_ready, 1)

            def s_values(i, u, part):
                b, g = self.stream(i, u)
                n_part = u * len(parts) + list(parts).index(part)
                pe.wait_ge(self.spt_copied, i * steps + (n_part + 1))
                t0, n = parts[part]
                if part != "c":
                    vi = u * self.chunks + t0 // 4
                    pe.wait_ge(self.sv_loaded[vi % 2], i * (16 * self.chunks) + 16 * (vi // 2 + 1))
                if part == "a":
                    pe.wait_ge(self.sot_lo, i * 4 + (2 * u + 1))
                for j in range(n):
                    for p in range(4):
                        if part == "c":
                            v = self.v[:, TT - 1, (4 * g + p) * P:(4 * g + p + 1) * P]
                        else:
                            v = v_cache[:, vi % 2, j, p * P:(p + 1) * P]
                        last = nc.tensor.matmul(ps[32 * p:32 * p + 32, 7, 0:P],
                                                s_pt[:, (t0 + j) * P + 32 * p:(t0 + j) * P + 32 * p + 32], v,
                                                start=part == "a" and j == 0, stop=part == "c")
                last.then_inc(self.so_ready if part == "c" else self.sv_used, 1)

            def s_turn_out(i, u):
                pe.wait_ge(self.so_scaled, i * 2 + (u + 1))
                nc.tensor.transpose(ps[:, 7, P:2 * P], s_o[:, :], ident[:, :]).then_inc(self.sot_ready, 1)

            pieces = dict(S=logits, T=turn_probs, V=values, X=turn_out, sS=s_logits, sT=s_turn_probs, sV=s_values,
                          sX=s_turn_out)
            self.loop(pe, PE_HEAD, PE_ORDER, pieces)

        def act(self, act, first_slab):
            parts = self.parts()
            act.wait_ge(self.zeroed, 2)

            def queries(i):
                act.wait_ge(self.logits_ready, i * 8 + 1)
                for hh in range(2):
                    rows = slice(64 * hh, 64 * hh + 64)
                    src = self.q[rows, bass.ds(i, 1), 0:SEQ].rearrange("p o c -> p (o c)")
                    nc.scalar.activation(qz[rows, hh, :], src, ACT.Copy).then_inc(self.qz_done, 1)

            def exps(i, l):
                n = P * (l // 2 + 1)
                act.wait_ge(self.max_step, i * 16 + (2 * l + 2))
                nc.scalar.activation(p_s[:, l % 2, 0:n], p_s[:, l % 2, 0:n], ACT.Exp, bias=neg_max[:, l:l + 1],
                                     accum_out=row_sum[:, l:l + 1]).then_inc(self.probs_ready, 1)

            def copy_probs(i, l):
                n = P * (l // 2 + 1)
                act.wait_ge(self.pt_ready, i * 8 + (l + 1))
                nc.scalar.activation(p_pt[:, 0:n], ps[:, 2, 0:n], ACT.Copy).then_inc(self.pt_copied, 1)

            def out_hi(i, it):
                act.wait_ge(self.ot_ready, i * 4 + (it + 1))
                nc.scalar.activation(row_of(self.o_hi, i + self.out0, it * P, (it + 1) * P), ps[:, 3, P:2 * P],
                                     ACT.Copy).then_inc(self.ot_hi, 1)

            def s_exps(i, u):
                act.wait_ge(self.smax_step, i * 4 + (2 * u + 2))
                cols = self.cached + P
                nc.scalar.activation(s_s[:, 0:cols], s_s[:, 0:cols], ACT.Exp, bias=s_neg_max[:, u:u + 1],
                                     accum_out=s_row_sum[:, u:u + 1]).then_inc(self.sprobs_ready, 1)

            def s_copy_probs(i, u, part):
                n_part = u * len(parts) + list(parts).index(part)
                act.wait_ge(self.spt_ready, i * (2 * len(parts)) + (n_part + 1))
                t0, n = parts[part]
                nc.scalar.activation(s_pt[:, t0 * P:(t0 + n) * P], ps[:, 4 + t0 // 4, 0:n * P],
                                     ACT.Copy).then_inc(self.spt_copied, 1)

            def s_out_hi(i, u):
                b, g = self.stream(i, u)
                act.wait_ge(self.sot_ready, i * 2 + (u + 1))
                for hh in range(2):
                    nc.scalar.activation(self.out_ap(self.o_hi, b, g, hh), self.turned(hh),
                                         ACT.Copy).then_inc(self.sot_hi, 1)

            pieces = dict(Q=queries, E=exps, C=copy_probs, H=out_hi, sE=s_exps, sC=s_copy_probs, sH=s_out_hi)
            pieces["W"] = lambda i: first_slab()
            self.loop(act, ACT_HEAD, ACT_ORDER, pieces)

        def out_ap(self, t, b, g, hh):
            return t[64 * hh:64 * hh + 64, self.out0 + 4 * g:self.out0 + 4 * g + 4,
                     bass.ds(b * DEC_SEQ + SEQ, DEC_SEQ)]

        def turned(self, hh):
            return ps[64 * hh:64 * hh + 64, 7, P:2 * P].rearrange("p (j h i) -> p j h i", j=4, h=2)[:, :, hh, :]

        def clear_queries(self):
            nc.gpsimd.memset(qz[:, :, :], 0.0).then_inc(self.zeroed, 1)

        def dve(self, dve):
            nc.vector.memset(qz_s[:, :, :, :], 0.0).then_inc(self.zeroed, 1)
            for n, s in enumerate(self.started):
                nc.vector.memset(start_marks[:, n:n + 1], 0.0).then_inc(s, 1)
            dve.wait_ge(self.zeroed, 2)

            def maxes(i, l):
                hh, n = l % 2, P * (l // 2 + 1)
                if l < 2:
                    dve.wait_ge(self.bias_loaded[hh], i * 16 + 16)
                dve.wait_ge(self.logits_ready, i * 8 + (l + 2))
                nc.vector.memset(marks[:, l:l + 1], 0.0)
                b0 = self.bias_cols(l // 2)
                nc.vector.tensor_tensor_reduce(out=p_s[:, l % 2, 0:n], in0=p_bias[:, hh, b0:b0 + n],
                                               in1=ps[:, l % 2, 0:n], scale=1.0, scalar=LOWEST, op0=ALU.add,
                                               op1=ALU.max, accum_out=row_max[:, l:l + 1]).then_inc(self.max_step, 1)
                dve.wait_ge(self.max_step, i * 16 + (2 * l + 1))
                nc.vector.tensor_scalar(out=neg_max[:, l:l + 1], in0=row_max[:, l:l + 1], scalar1=-1.0, scalar2=None,
                                        op0=ALU.mult).then_inc(self.max_step, 1)

            def scale_out(i, l):
                hh = l % 2
                dve.wait_ge(self.probs_ready, i * 8 + (l + 1))
                nc.vector.reciprocal(row_inv[:, l:l + 1], row_sum[:, l:l + 1]).then_inc(self.inv_done, 1)
                dve.wait_ge(self.inv_done, i * 8 + (l + 1))
                dve.wait_ge(self.o_ready, i * 8 + (l + 1))
                nc.vector.tensor_scalar(out=p_o[:, 64 * hh:64 * hh + 64], in0=ps[:, 3, 64 * hh:64 * hh + 64],
                                        scalar1=row_inv[:, l:l + 1], scalar2=None,
                                        op0=ALU.mult).then_inc(self.o_scaled, 1)

            def out_lo(i, it):
                dve.wait_ge(self.ot_hi, i * 4 + (it + 1))
                cols = (it * P, (it + 1) * P)
                nc.vector.tensor_tensor(out=row_of(self.o_lo, i + self.out0, *cols), in0=ps[:, 3, P:2 * P],
                                        in1=row_of(self.o_hi, i + self.out0, *cols).bitcast(F32),
                                        op=ALU.subtract).then_inc(self.ot_lo, 1)

            def s_queries(i, u):
                b, g = self.stream(i, u)
                dve.wait_ge(self.slogits_ready, i * 2 + 1)
                for hh in range(2):
                    rows = slice(64 * hh, 64 * hh + 64)
                    nc.vector.tensor_copy(qz_s[rows, u, :, 16 * hh:16 * hh + 16],
                                          self.q[rows, 4 * g:4 * g + 4, bass.ds(b * DEC_SEQ + SEQ, DEC_SEQ)]
                                          ).then_inc(self.sqz_done, 1)

            def s_maxes(i, u):
                cols = self.cached + P
                dmas = self.sample_bias_dmas
                dve.wait_ge(self.sbias_loaded[u], i * (16 * dmas) + 16 * dmas)
                dve.wait_ge(self.slogits_ready, i * 2 + (u + 2))
                nc.vector.memset(s_marks[:, u:u + 1], 0.0)
                nc.vector.tensor_tensor_reduce(out=s_s[:, 0:cols], in0=s_bias[:, 0:cols], in1=flat(4, 3, cols),
                                               scale=1.0, scalar=LOWEST, op0=ALU.add, op1=ALU.max,
                                               accum_out=s_row_max[:, u:u + 1]).then_inc(self.smax_step, 1)
                dve.wait_ge(self.smax_step, i * 4 + (2 * u + 1))
                nc.vector.tensor_scalar(out=s_neg_max[:, u:u + 1], in0=s_row_max[:, u:u + 1], scalar1=-1.0,
                                        scalar2=None, op0=ALU.mult).then_inc(self.smax_step, 1)

            def s_scale_out(i, u):
                dve.wait_ge(self.sprobs_ready, i * 2 + (u + 1))
                nc.vector.reciprocal(s_row_inv[:, u:u + 1], s_row_sum[:, u:u + 1]).then_inc(self.sinv_done, 1)
                dve.wait_ge(self.sinv_done, i * 2 + (u + 1))
                dve.wait_ge(self.so_ready, i * 2 + (u + 1))
                nc.vector.tensor_scalar(out=s_o[:, :], in0=ps[:, 7, 0:P], scalar1=s_row_inv[:, u:u + 1],
                                        scalar2=None, op0=ALU.mult).then_inc(self.so_scaled, 1)

            def s_out_lo(i, u):
                b, g = self.stream(i, u)
                for hh in range(2):
                    dve.wait_ge(self.sot_hi, i * 4 + (2 * u + hh + 1))
                    nc.vector.tensor_tensor(out=self.out_ap(self.o_lo, b, g, hh), in0=self.turned(hh),
                                            in1=self.out_ap(self.o_hi, b, g, hh).bitcast(F32),
                                            op=ALU.subtract).then_inc(self.sot_lo, 1)

            pieces = dict(M=maxes, O=scale_out, L=out_lo, sQ=s_queries, sM=s_maxes, sO=s_scale_out, sL=s_out_lo)
            self.loop(dve, DVE_HEAD, DVE_ORDER, pieces)

        def finished(self, eng):
            eng.wait_ge(self.ot_lo, 4 * self.loops + 1)
            eng.wait_ge(self.sot_lo, 4 * self.loops + 1)

    neg_f_dram = nc.dram_tensor("neg_f_dram", (H_C, T), F32, kind="Internal").ap()
    after_dram = nc.dram_tensor("after_dram", (P, PAST), F32, kind="Internal").ap()
    band = Attention("band", H_B // 2, WIN, qb, kb, vb, 4, xn[0],
                     lambda i, hh: ins["band_bias"][bass.ds(i, 1), :, hh, :].rearrange("o p c -> p (o c)"),
                     lambda it: 384 - P * it, False, 1)
    fox = Attention("fox", H_C // 2, PAST, qc, kc, vc, 0, xn[1],
                    lambda i, hh: neg_f_dram[bass.ds(i * 2 + hh, 1), 0:SEQ].broadcast_to([P, SEQ]),
                    lambda it: 0, True, 2)

    def band_loads(sp):
        def keys(i, u):
            sp.dma_start(k_cache[:, u], ins["band_kc"][bass.ds(i * 2 + u, 1)].rearrange("o p j c -> p (o j) c")
                         ).then_inc(band.sk_loaded[u], 16)

        def values(i, u, ch, slot):
            sp.dma_start(v_cache[:, slot], ins["band_vc"][bass.ds(i * 2 + u, 1)].rearrange("o p j c -> p (o j) c")
                         ).then_inc(band.sv_loaded[slot], 16)

        def bias(i, u):
            sp.dma_start(s_bias[:, 0:WIN + P], ins["band_bias_s"][bass.ds(i * 2 + u, 1)]
                         .rearrange("o p c -> p (o c)")).then_inc(band.sbias_loaded[u], 16)

        return dict(keys=keys, values=values, bias=bias)

    def fox_loads(sp):
        def keys(i, u):
            dst = k_cache[:, 2 * u:2 * u + 2].rearrange("p h j c -> p (h j) c")
            sp.dma_start(dst, ins["fox_kc"][u][bass.ds(i, 1)].rearrange("o p j c -> p (o j) c")
                         ).then_inc(fox.sk_loaded[u], 16)

        def values(i, u, ch, slot):
            sp.dma_start(v_cache[:, slot], ins["fox_vc"][u][bass.ds(i, 1), :, 4 * ch:4 * ch + 4, :]
                         .rearrange("o p j c -> p (o j) c")).then_inc(fox.sv_loaded[slot], 16)

        def bias(i, u):
            sp.dma_start(s_bias[:, 0:PAST], after_dram[bass.ds(i * H_C + 8 * u, 8), :].unsqueeze(1)
                         .broadcast_to([8, DEC_SEQ, PAST])).then_inc(fox.sbias_loaded[u], 16)
            sp.dma_start(s_bias[:, PAST:PAST + P], neg_f_dram[8 * u:8 * u + 8, SEQ:T].unsqueeze(1)
                         .broadcast_to([8, DEC_SEQ, P])).then_inc(fox.sbias_loaded[u], 16)

        return dict(keys=keys, values=values, bias=bias)

    g = lambda name: sem("gla_" + name)
    g_ls, g_loga, g_exp, g_last, g_dec = (g(n) for n in ("ls", "loga", "exp", "last", "dec"))
    g_qk, g_kown, g_att, g_attm = (g(n) for n in ("qk", "kown", "att", "attm"))
    g_kv, g_s, g_sd, g_o, g_oc, g_sq, g_stat = (g(n) for n in ("kv", "s", "sd", "o", "oc", "sq", "stat"))
    g_r, g_on, g_sg, g_ohi, g_olo, g_ar = (g(n) for n in ("r", "on", "sg", "ohi", "olo", "ar"))
    s_dec_loaded, p_state_stored, s_state_stored = sem("s_dec_loaded"), sem("p_state_stored"), sem("s_state_stored")
    kv_even_stored, kv_odd_stored, logf_stored = sem("kv_even_stored"), sem("kv_odd_stored"), sem("logf_stored")
    q_head = (qa, qa1)
    head_rows = [slice(64 * (h % 2), 64 * (h % 2) + 64) for h in range(H_A)]

    def gla_among_pe(pe, ph, s):
        q = fm_unit(ph, s) + 2 * s - 2
        unit = lambda n: flat(2 * ((q + n) % 4), 2, 1024)
        if s == 2:
            for tt in range(TT):
                if tt in (0, 4):
                    pe.wait_ge(unit_free, q - 3 + tt // 4)
                last = nc.tensor.matmul(unit(tt // 4)[:, tt % 4 * 256:(tt % 4 + 1) * 256], ar[:, tt * P:(tt + 1) * P],
                                        w_alpha[:, :], start=True, stop=True)
                if tt in (3, 4):
                    last.then_inc(unit_ready, 1)
        elif s == 4:
            pe.wait_ge(g_loga, 1)
            for ft in range(2):
                pe.wait_ge(unit_free, q - 3 + ft)
                for tt in range(TT):
                    last = nc.tensor.matmul(unit(ft)[:, tt * P:(tt + 1) * P],
                                            log_a[:, tt * 256 + ft * P:tt * 256 + (ft + 1) * P],
                                            (cum16 if tt == TT - 1 else cum64)[:, :], start=True, stop=True)
                last.then_inc(unit_ready, 1)
        elif s == IN_SLABS:
            pe.wait_ge(g_qk, 6)
            for tt in range(TT):
                if tt in (0, 4):
                    pe.wait_ge(unit_free, q - 3 + tt // 4)
                for ft in range(2):
                    c0 = tt % 4 * 256 + ft * P
                    last = nc.tensor.transpose(unit(tt // 4)[:, c0:c0 + P], ka[:, ft, tt * P:(tt + 1) * P],
                                               ident[:, :])
                if tt in (3, 4):
                    last.then_inc(unit_ready, 1)

    def gla_pe(pe, ph):
        m = mix_at(ph)
        pe.wait_ge(unit_free, m["out"][1])
        for tt in range(TT):
            for h in range(H_A):
                cols = slice(tt * P, (tt + 1) * P)
                last = nc.tensor.matmul(ps[:, 3 + tt, h * P:(h + 1) * P], k_in[:, h // 2, cols],
                                        q_head[h % 2][:, h // 2, cols], start=True, stop=True)
            last.then_inc(g_att, 1)
        for c in range(SEQ // CHUNK):
            rows = slice(64 * (c % 2), 64 * (c % 2) + 64)
            if c >= 2:
                pe.wait_ge(g_s, 4 * (c - 1))
            for pair in range(2):
                last = nc.tensor.matmul(ps[:, c % 2, pair * 256:(pair + 1) * 256],
                                        k_tok[rows, c // 2, pair * P:(pair + 1) * P],
                                        va[rows, c // 2, pair * 256:(pair + 1) * 256], start=True, stop=True)
            last.then_inc(g_kv, 1)
        pe.wait_ge(g_attm, TT)
        pe.wait_ge(g_s, 4 * (SEQ // CHUNK))
        pe.wait_ge(s_dec_loaded, 16)

        def head_out(h):
            q, pair = q_head[h % 2], h // 2
            o = flat(2 + 2 * (h % 2), 2, T)
            if h >= 2:
                pe.wait_ge(g_oc, h - 1)
            for tt in range(TT):
                nc.tensor.matmul(o[:, tt * P:(tt + 1) * P], va[:, tt, h * P:(h + 1) * P],
                                 att[:, tt, h * P:(h + 1) * P], start=True, stop=False)
                if tt < TT - 1:
                    for c in (2 * tt, 2 * tt + 1):
                        if c:
                            cols = slice(c * CHUNK, (c + 1) * CHUNK)
                            last = nc.tensor.matmul(o[:, cols], s_hist[:, c, pair, :], q[:, pair, cols],
                                                    start=False, stop=c % 2 == 1)
                else:
                    for b in range(DEC_BATCH):
                        cols = slice(SEQ + b * DEC_SEQ, SEQ + (b + 1) * DEC_SEQ)
                        last = nc.tensor.matmul(o[:, cols], s_dec[:, b, pair, :], q[:, pair, cols],
                                                start=False, stop=b == DEC_BATCH - 1)
            last.then_inc(g_o, 1)

        def head_stat(h):
            pe.wait_ge(g_sq, h + 1)
            for tt in range(TT):
                last = nc.tensor.matmul(ps[:, 6, h * TT + tt:h * TT + tt + 1], sq_head[:, tt * P:(tt + 1) * P],
                                        mean_head[:, :], start=True, stop=True)
            last.then_inc(g_stat, 1)

        def head_spread(h):
            pe.wait_ge(diag_done, DIAG0["gla"] + TT * (h + 1))
            if h:
                pe.wait_ge(g_on, 2 * h - 1)
            for tt in range(TT):
                last = nc.tensor.matmul(flat(0, 2, T)[:, tt * P:(tt + 1) * P], ones[:, :], diag_a[:, h % 2, tt, :],
                                        start=True, stop=True)
            last.then_inc(g_r, 1)

        head_out(0)
        head_out(1)
        head_stat(0)
        head_out(2)
        head_spread(0)
        head_stat(1)
        head_out(3)
        head_spread(1)
        head_stat(2)
        pe.wait_ge(g_kown, 1)
        pe.wait_ge(g_oc, 3)
        for b in range(DEC_BATCH):
            if b >= 2:
                pe.wait_ge(g_sd, 4 * (b - 1))
            for pair in range(2):
                last = nc.tensor.matmul(ps[:, 2 + b % 2, pair * 256:(pair + 1) * 256],
                                        k_own[:, b, pair * P:(pair + 1) * P],
                                        va[:, TT - 1, pair * 256:(pair + 1) * 256], start=True, stop=True)
            last.then_inc(g_kv, 1)
            if b == 3:
                head_stat(3)
                head_spread(2)
        head_spread(3)

    def gla_among_act(act, ph, s):
        if s == 2:
            act.wait_ge(unit_free, fm_unit(ph, 2) + 4)
            nc.scalar.activation(ls_tmp[:, :], log_a[:, :], ACT.Abs).then_inc(g_ls, 1)
            act.wait_ge(g_ls, 1)
            nc.scalar.activation(ls_tmp[:, :], ls_tmp[:, :], ACT.Exp, scale=-1.0).then_inc(g_ls, 1)
            act.wait_ge(g_ls, 2)
            nc.scalar.activation(ls_tmp[:, :], ls_tmp[:, :], ACT.Ln, bias=1.0).then_inc(g_ls, 1)
        elif s == 4:
            act.wait_ge(unit_free, fm_unit(ph, 4) + 8)
            nc.scalar.activation(e_cum[:, :, :], decay[:, :, :], ACT.Exp).then_inc(g_exp, 1)
            nc.scalar.activation(k_in[:, :, :], decay[:, :, :], ACT.Exp, scale=-1.0).then_inc(g_exp, 1)
        elif s == 5:
            act.wait_ge(g_dec, 4)
            nc.scalar.activation(decay[:, :, :], decay[:, :, :], ACT.Exp, scale=-1.0).then_inc(g_exp, 1)
        elif s == 6:
            nc.scalar.activation(ag[:, :, :], ag[:, :, :], ACT.Silu).then_inc(g_sg, 1)

    def gla_act(act, ph):
        for h in range(H_A):
            act.wait_ge(g_o, h + 1)
            if h == 2:
                act.wait_ge(g_kown, 1)
            nc.scalar.activation(o_head[:, h, :], flat(2 + 2 * (h % 2), 2, T), ACT.Copy).then_inc(g_oc, 1)
            act.wait_ge(g_oc, h + 1)
            if h:
                act.wait_ge(g_stat, h)
            nc.scalar.activation(sq_head[:, :], o_head[:, h, :], ACT.Square).then_inc(g_sq, 1)
        act.wait_ge(g_o, H_A)
        for h in range(H_A):
            act.wait_ge(g_on, 2 * h + 2)
            nc.scalar.activation(xn[0][0][:, h, :], o_head[:, h, :], ACT.Copy).then_inc(g_ohi, 1)

    def gla_among_dve(dve, ph, j):
        def take_units(s, copies):
            q = fm_unit(ph, s) + 2 * s - 2
            for n, (dst, cols) in enumerate(copies):
                dve.wait_ge(unit_ready, q + n + 1)
                nc.vector.tensor_copy(dst, flat(2 * ((q + n) % 4), 2, cols)).then_inc(unit_free, 1)

        spans = ((0, SEQ, CHUNK, 0), (SEQ, T, DEC_SEQ, 8))
        if j == 4:
            take_units(2, ((log_a[:, 0:1024], 1024), (log_a[:, 1024:1280], 256)))
        elif j == 6:
            dve.wait_ge(g_ls, 3)
            nc.vector.scalar_tensor_tensor(out=log_a[:, :], in0=log_a[:, :], scalar=0.0, in1=ls_tmp[:, :],
                                           op0=ALU.min, op1=ALU.subtract).then_inc(g_loga, 1)
        elif j == 8:
            dve.wait_ge(g_loga, 1)
            take_units(4, ((decay[:, 0, :], T), (decay[:, 1, :], T)))
            dve.wait_ge(unit_free, fm_unit(ph, 4) + 8)
            for ft in range(2):
                for lo, hi, n, at_ in spans:
                    src = decay[:, ft, lo:hi].rearrange("p (c i) -> p c i", i=n)[:, :, n - 1]
                    nc.vector.tensor_copy(chunk_last[:, ft, at_:at_ + 8], src).then_inc(g_last, 1)
        elif j == 9:
            dve.wait_ge(g_last, 4)
            dve.wait_ge(g_exp, 2)
            for ft in range(2):
                for lo, hi, n, at_ in spans:
                    nc.vector.tensor_tensor(
                        out=decay[:, ft, lo:hi].rearrange("p (c i) -> p c i", i=n),
                        in0=decay[:, ft, lo:hi].rearrange("p (c i) -> p c i", i=n),
                        in1=chunk_last[:, ft, at_:at_ + 8].unsqueeze(2).broadcast_to([P, 8, n]),
                        op=ALU.subtract).then_inc(g_dec, 1)
        elif j == 10:
            nc.vector.tensor_tensor(out=qa1[64:P, :, :], in0=qa[64:P, :, :], in1=e_cum[64:P, :, :],
                                    op=ALU.mult).then_inc(g_qk, 1)
            nc.vector.tensor_tensor(out=qa[0:64, :, :], in0=qa[0:64, :, :], in1=e_cum[0:64, :, :],
                                    op=ALU.mult).then_inc(g_qk, 1)
        elif j == 11:
            nc.vector.memset(qa1[0:64, :, :], 0.0).then_inc(g_qk, 1)
            dve.wait_ge(g_qk, 1)
            nc.vector.memset(qa[64:P, :, :], 0.0).then_inc(g_qk, 1)
        elif j == 12:
            nc.vector.tensor_tensor(out=k_in[:, :, :], in0=k_in[:, :, :], in1=ka[:, :, :],
                                    op=ALU.mult).then_inc(g_qk, 1)
        elif j == 13:
            dve.wait_ge(g_exp, 3)
            dve.wait_ge(g_qk, 5)
            nc.vector.tensor_tensor(out=ka[:, :, :], in0=ka[:, :, :], in1=decay[:, :, :],
                                    op=ALU.mult).then_inc(g_qk, 1)
        elif j == 2 * IN_SLABS:
            turned = k_tok[:, :, :].rearrange("p t c -> p (t c)")
            take_units(IN_SLABS, ((turned[:, 0:1024], 1024), (turned[:, 1024:1280], 256)))

    def gla_dve(dve, ph):
        for tt in range(TT):
            dve.wait_ge(g_att, tt + 1)
            keep = (keep16 if tt == TT - 1 else keep64)[:, :].unsqueeze(1).broadcast_to([P, H_A, P])
            nc.vector.tensor_tensor(out=att[:, tt, :].rearrange("p (h c) -> p h c", h=H_A),
                                    in0=ps[:, 3 + tt, :].rearrange("p (h c) -> p h c", h=H_A), in1=keep,
                                    op=ALU.mult).then_inc(g_attm, 1)
        for c in range(SEQ // CHUNK):
            dve.wait_ge(g_kv, c + 1)
            if c:
                dve.wait_ge(g_s, 4 * c)
            for h in range(H_A):
                rows, pair = head_rows[h], h // 2
                kv = ps[rows, c % 2, pair * 256 + (h % 2) * P:pair * 256 + (h % 2 + 1) * P]
                if c == 0:
                    ins_ = nc.vector.tensor_copy(s_hist[rows, 1, pair, :], kv)
                else:
                    col = (c + 1) * CHUNK - 1
                    ins_ = nc.vector.scalar_tensor_tensor(out=s_hist[rows, c + 1, pair, :],
                                                          in0=s_hist[rows, c, pair, :],
                                                          scalar=e_cum[rows, pair, col:col + 1], in1=kv,
                                                          op0=ALU.mult, op1=ALU.add)
                ins_.then_inc(g_s, 1)
        dve.wait_ge(unit_free, mix_at(ph)["out"][1])
        nc.vector.tensor_tensor(out=k_own[:, :, :], in0=k_tok[:, TT - 1, :].unsqueeze(1).broadcast_to([P, DEC_BATCH, 256]),
                                in1=own_rows[:, :].unsqueeze(2).broadcast_to([P, DEC_BATCH, 256]),
                                op=ALU.mult).then_inc(g_kown, 1)

        def head_norm(h):
            dve.wait_ge(g_stat, h + 1)
            rs_chain(dve, ps[:, 6, h * TT:(h + 1) * TT], h * TT, TT, RS_NORM0["gla"] + h * RS_OPS)
            dve.wait_ge(rs_step, RS_NORM0["gla"] + (h + 1) * RS_OPS)
            if h >= 2:
                dve.wait_ge(g_r, h - 1)
            for tt in range(TT):
                nc.vector.tensor_scalar(out=diag_a[:, h % 2, tt, :], in0=ident[:, :],
                                        scalar1=rs[1][:, h * TT + tt:h * TT + tt + 1], scalar2=None,
                                        op0=ALU.mult).then_inc(diag_done, 1)

        def head_gated(h):
            dve.wait_ge(g_r, h + 1)
            if h:
                dve.wait_ge(g_on, 2 * h)
            else:
                dve.wait_ge(g_sg, 1)
            nc.vector.scalar_tensor_tensor(out=o_tmp[:, :], in0=o_head[:, h, :], scalar=head_gain[:, 0:1],
                                           in1=flat(0, 2, T), op0=ALU.mult, op1=ALU.mult).then_inc(g_on, 1)
            dve.wait_ge(g_on, 2 * h + 1)
            nc.vector.tensor_tensor(out=o_head[:, h, :], in0=o_tmp[:, :], in1=ag[:, h, :],
                                    op=ALU.mult).then_inc(g_on, 1)

        def stream_states(b):
            dve.wait_ge(g_kv, SEQ // CHUNK + b + 1)
            for h in range(H_A):
                rows, pair = head_rows[h], h // 2
                col = SEQ + (b + 1) * DEC_SEQ - 1
                nc.vector.scalar_tensor_tensor(
                    out=s_dec[rows, b, pair, :], in0=s_dec[rows, b, pair, :], scalar=e_cum[rows, pair, col:col + 1],
                    in1=ps[rows, 2 + b % 2, pair * 256 + (h % 2) * P:pair * 256 + (h % 2 + 1) * P],
                    op0=ALU.mult, op1=ALU.add).then_inc(g_sd, 1)

        head_norm(0)
        head_norm(1)
        head_gated(0)
        head_norm(2)
        head_gated(1)
        for b in range(3):
            stream_states(b)
        head_gated(2)
        for b in range(3, 6):
            stream_states(b)
        head_norm(3)
        for b in range(6, DEC_BATCH):
            stream_states(b)
        head_gated(3)

    def gla_pool(pool, ph):
        pool.wait_ge(p_state_stored, 16)
        for h in range(H_A):
            pool.wait_ge(g_ohi, h + 1)
            nc.gpsimd.tensor_tensor(out=xn[0][1][:, h, :], in0=o_head[:, h, :], in1=xn[0][0][:, h, :].bitcast(F32),
                                    op=ALU.subtract).then_inc(g_olo, 1)
            if h == 2:
                pool.wait_ge(g_stat, H_A)
                band.clear_queries()

    f_ls, f_lf, f_loaded, f_scratch = (sem("fgate_" + n) for n in ("ls", "lf", "loaded", "scratch"))

    def fgate_pe(pe, ph, s):
        n = OWN_UNITS["odd"].get(s, 0)
        q = fm_unit(ph, s) + 2 * s - n
        bank = lambda k: 2 * ((q + k) % 4)
        if s == 4:
            pe.wait_ge(unit_free, q - 3)
            pe.wait_ge(f_lf, 1)
            for tt in range(TT):
                last = nc.tensor.transpose(ps[:, bank(0), tt * H_C:(tt + 1) * H_C], lf[:, tt * P:(tt + 1) * P],
                                           ident[0:H_C, 0:H_C])
            last.then_inc(unit_ready, 1)
        elif s == IN_SLABS:
            pe.wait_ge(f_loaded, 48)
            pe.wait_ge(unit_free, q - 3)
            b = bank(0)
            for tt in range(TT - 1):
                nc.tensor.matmul(ps[0:H_C, b, tt * P:SEQ], lf_tok[:, tt, :], upto_w[:, 0:SEQ - tt * P],
                                 start=tt == 0, stop=tt == TT - 2)
            nc.tensor.matmul(ps[0:H_C, b + 1, 0:P], lf_tok[:, TT - 1, :], keep16[:, :], start=True,
                             stop=True).then_inc(unit_ready, 1)
            pe.wait_ge(unit_free, q - 2)
            b = bank(1)
            for t in range(7, -1, -1):
                for half in ((0, 1) if t >= 4 else (0,)):
                    j0 = 512 * half
                    n_keys = min(512, P * (t + 1) - j0)
                    c0 = 896 - P * t + j0
                    last = nc.tensor.matmul(ps[:, b + half, 0:n_keys], clf[:, t, :], after_w[:, c0:c0 + n_keys],
                                            start=t == 7, stop=t == 0 or (half == 1 and t == 4))
            last.then_inc(unit_ready, 1)

    def fgate_act(act, ph, s):
        if s == 2:
            act.wait_ge(logit_done, 1)
            nc.scalar.activation(lf_tmp[:, :], logit[:, :], ACT.Abs).then_inc(f_ls, 1)
            act.wait_ge(f_ls, 1)
            nc.scalar.activation(lf_tmp[:, :], lf_tmp[:, :], ACT.Exp, scale=-1.0).then_inc(f_ls, 1)
            act.wait_ge(f_ls, 2)
            nc.scalar.activation(lf_tmp[:, :], lf_tmp[:, :], ACT.Ln, bias=1.0).then_inc(f_ls, 1)

    def fgate_dve(dve, ph, j):
        if j == 6:
            dve.wait_ge(f_ls, 3)
            nc.vector.scalar_tensor_tensor(out=lf[:, :], in0=logit[:, :], scalar=0.0, in1=lf_tmp[:, :], op0=ALU.min,
                                           op1=ALU.subtract).then_inc(f_lf, 1)
        elif j == 8:
            q = fm_unit(ph, 4) + 8 - 1
            dve.wait_ge(unit_ready, q + 1)
            nc.vector.tensor_copy(lf_tok[:, :, :].rearrange("p t h -> p (t h)"),
                                  ps[:, 2 * (q % 4), 0:TT * H_C]).then_inc(unit_free, 1)
        elif j == 2 * IN_SLABS:
            q = fm_unit(ph, IN_SLABS) + 2 * IN_SLABS - 2
            dve.wait_ge(unit_ready, q + 1)
            nc.vector.tensor_scalar(out=neg_f[:, :], in0=flat(2 * (q % 4), 2, T)[0:H_C], scalar1=-1.0, scalar2=None,
                                    op0=ALU.mult).then_inc(unit_free, 1)
            dve.wait_ge(unit_ready, q + 2)
            nc.vector.tensor_copy(c_after[:, :], flat(2 * ((q + 1) % 4), 2, PAST)).then_inc(unit_free, 1)

    EVEN = next(ph for ph in PLAN if ph["kind"] == "even")
    ODD = next(ph for ph in PLAN if ph["kind"] == "odd")
    consts = [(ident, "ident"), (ones, "ones"), (mean_model, "mean_model"), (mean_head, "mean_head"),
              (cum64, "cum64"), (cum16, "cum16"), (keep64, "keep64"), (keep16, "keep16"),
              (own_rows, "own_rows"), (w_alpha, "w_alpha"), (head_gain, "head_gain"), (bias_f, "bias_f"),
              (causal, "causal"), (own_causal, "own_causal")]
    block = ctx.enter_context(nc.Block())

    @block.sync
    def _(sp):
        sp.dma_start(gains[:, :], ins["gains"]).then_inc(gains_loaded, 16)
        src, width = slab_src(PLAN[0], "up_a", 0)
        for k in range(0, KT, 2):
            sp.dma_start(x_res[:, k:k + 2, :], ins["x"][:, k:k + 2, :]).then_inc(x_loaded[k // 2], 16)
            if k == 0:
                sp.dma_start(w_raw[:, 0, 0:SLAB // 2], src[:, 0:SLAB // 2]).then_inc(half_loaded, 16)
                sp.dma_start(w_raw[:, 0, SLAB // 2:], src[:, SLAB // 2:]).then_inc(raw_loaded[0], 16)
        for dst, name in consts:
            sp.dma_start(dst[tuple(slice(None) for _ in dst.shape)], ins[name]).then_inc(consts_loaded, 16)
        for ph in PLAN:
            if ph["kind"] == "ffn":
                for kind, count, per, n0, q0 in ffn_segments(ph):
                    first = FF_A if kind == "up_b" else 0
                    load_slabs(sp, ph, kind, first, count, n0, fresh=2 if n0 == 0 else 0, given=1 if n0 == 0 else 0)
                continue
            m = mix_at(ph)
            small_load(sp, ph)
            load_slabs(sp, ph, "in", 0, 4, m["fm"][0])
            if ph["kind"] == "odd":
                sp.dma_start(clf[:, :, :], ins["fox_clogf"]).then_inc(f_loaded, 16)
                sp.dma_start(after_w[:, :], ins["after_w"]).then_inc(f_loaded, 16)
                sp.dma_start(upto_w[:, :], ins["upto_w"]).then_inc(f_loaded, 16)
            load_slabs(sp, ph, "in", 4, IN_SLABS + TOK_SLABS - 4, m["fm"][0] + 4)
            if ph["kind"] == "even":
                def gla_stores():
                    sp.wait_ge(g_s, 4 * (SEQ // CHUNK))
                    sp.dma_start(outs["p_state"], s_hist[:, SEQ // CHUNK, :, :]).then_inc(p_state_stored, 16)
                    sp.wait_ge(g_sd, 4 * DEC_BATCH)
                    sp.dma_start(outs["s_state"], s_dec[:, :, :, :]).then_inc(s_state_stored, 16)
                    sp.wait_ge(g_olo, H_A)

                sp.wait_ge(unit_free, m["out"][1])
                sp.dma_start(s_dec[:, :, :, :], ins["state"]).then_inc(s_dec_loaded, 16)
                sp.dma_start(outs["band_k"], kb[:, :, :]).then_inc(kv_even_stored, 16)
                sp.dma_start(outs["band_v"], vb[:, :, :]).then_inc(kv_even_stored, 16)
                band.sp(sp, band_loads(sp), gla_stores)
                sp.wait_ge(band.slogits_ready, 2 * band.loops + 1)
            else:
                sp.wait_ge(unit_free, fm_unit(ph, IN_SLABS) + 2 * IN_SLABS)
                sp.dma_start(neg_f_dram, neg_f[:, :]).then_inc(f_scratch, 16)
                sp.dma_start(after_dram, c_after[:, :]).then_inc(f_scratch, 16)
                sp.dma_start(outs["fox_logf"], lf[:, :]).then_inc(logf_stored, 16)
                sp.dma_start(outs["fox_k"], kc[:, :, :]).then_inc(kv_odd_stored, 16)
                early = D_MODEL * 3 // 4
                sp.wait_ge(unit_free, m["tok"][1] + 3 * 4)
                sp.dma_start(outs["fox_v"][:, :, 0:early], vc[:, :, 0:early]).then_inc(kv_odd_stored, 16)
                sp.wait_ge(unit_free, m["out"][1])
                sp.wait_ge(f_scratch, 32)
                sp.wait_ge(logf_stored, 16)

                def store_values():
                    sp.dma_start(outs["fox_v"][:, :, early:], vc[:, :, early:]).then_inc(kv_odd_stored, 16)

                fox.sp(sp, fox_loads(sp), then=store_values)
                sp.wait_ge(fox.slogits_ready, 2 * fox.loops + 1)
            load_slabs(sp, ph, "out", 0, 4, m["out"][0])
        for k in range(0, KT, 2):
            sp.wait_ge(y_done, k + 2)
            sp.dma_start(outs["y"][:, k:k + 2, :], y_out[:, k:k + 2, :]).then_inc(y_stored, 16)
        sp.wait_ge(y_stored, 16 * KT // 2)
        sp.wait_ge(p_state_stored, 16)
        sp.wait_ge(s_state_stored, 16)
        sp.wait_ge(kv_even_stored, 32)
        sp.wait_ge(kv_odd_stored, 48)
        sp.wait_ge(logf_stored, 16)

    @block.gpsimd
    def _(pool):
        pool.wait_ge(half_hi, 1)
        half = slice(0, SLAB // 2)
        nc.gpsimd.tensor_tensor(out=w_lo[:, 0, half], in0=w_raw[:, 0, half], in1=w_hi[:, 0, half].bitcast(F32),
                                op=ALU.subtract).then_inc(half_lo, 1)
        pool.wait_ge(hi_done, 1)
        half = slice(SLAB // 2, SLAB)
        nc.gpsimd.tensor_tensor(out=w_lo[:, 0, half], in0=w_raw[:, 0, half], in1=w_hi[:, 0, half].bitcast(F32),
                                op=ALU.subtract).then_inc(lo_done, 1)
        for ph in PLAN:
            if ph["kind"] == "ffn":
                ffn_pool(pool, ph)
            else:
                proj_pool(pool, ph)
                if ph["kind"] == "even":
                    gla_pool(pool, ph)
                else:
                    pool.wait_ge(f_scratch, 32)
                    pool.wait_ge(logf_stored, 16)
                    fox.clear_queries()
                out_pool(pool, ph, band if ph["kind"] == "even" else fox)

    @block.scalar
    def _(act):
        act.wait_ge(half_loaded, 16)
        nc.scalar.activation(w_hi[:, 0, 0:SLAB // 2], w_raw[:, 0, 0:SLAB // 2], ACT.Copy).then_inc(half_hi, 1)
        act.wait_ge(raw_loaded[0], 16)
        nc.scalar.activation(w_hi[:, 0, SLAB // 2:], w_raw[:, 0, SLAB // 2:], ACT.Copy).then_inc(hi_done, 1)
        for k in range(KT):
            act.wait_ge(x_loaded[k // 2], 16)
            nc.scalar.activation(first_squares[:, k, :], x_res[:, k, :], ACT.Square).then_inc(sq_done, 1)
        for ph in PLAN:
            if ph["kind"] == "ffn":
                ffn_act(act, ph)
            elif ph["kind"] == "even":
                proj_act(act, ph, lambda s: gla_among_act(act, ph, s))
                gla_act(act, ph)
                band.act(act, lambda: out_first(act, ph, band))
                act.wait_ge(kv_even_stored, 32)
                out_act(act, ph)
            else:
                proj_act(act, ph, lambda s: fgate_act(act, ph, s))
                act.wait_ge(f_scratch, 32)
                act.wait_ge(logf_stored, 16)
                fox.act(act, lambda: out_first(act, ph, fox))
                act.wait_ge(kv_odd_stored, 48)
                out_act(act, ph)

    @block.vector
    def _(dve):
        clear_sum(dve)
        dve.wait_ge(gains_loaded, 16)
        for k in range(KT):
            dve.wait_ge(x_loaded[k // 2], 16)
            split_dve(dve, 0, k, 0, 0)
        for k in range(KT):
            dve.wait_ge(sq_done, k + 1)
            dve.wait_ge(acc_done, k + 1)
            nc.vector.tensor_tensor(out=sq_sum[:, :], in0=sq_sum[:, :], in1=first_squares[:, k, :],
                                    op=ALU.add).then_inc(acc_done, 1)
        dve.wait_ge(consts_loaded, 16 * len(consts))
        nc.vector.tensor_copy(ident_b[:, :], ident[:, :]).then_inc(masks_cast, 1)
        nc.vector.tensor_copy(causal_b[:, :], causal[:, :]).then_inc(masks_cast, 1)
        nc.vector.tensor_copy(own_causal_b[:, :], own_causal[:, :]).then_inc(masks_cast, 1)
        for ph in PLAN:
            if ph["kind"] == "ffn":
                ffn_dve(dve, ph)
            elif ph["kind"] == "even":
                nc.vector.memset(ar[:, :], 1.0).then_inc(g_ar, 1)

                def take_ar(unit):
                    dve.wait_ge(g_ar, 1)
                    nc.vector.tensor_tensor(out=halves(ar[0:R_A, :]), in0=unit_ap(unit)[0:R_A],
                                            in1=halves(inv_rms[0:R_A, :]), op=ALU.mult).then_inc(unit_free, 1)

                proj_dve(dve, ph, take_ar,
                         [(qa, 0, SCALE), (qa, 1, SCALE), (ka, 0, 1.0), (ka, 1, 1.0)]
                         + [(ag, j, 1.0) for j in range(4)] + [(qb, j, SCALE) for j in range(4)]
                         + [(kb, j, 1.0) for j in range(4)],
                         lambda s: (va, vb)[s // 2][:, :, (s % 2) * 256:(s % 2 + 1) * 256],
                         lambda j: gla_among_dve(dve, ph, j))
                gla_dve(dve, ph)
                dve.wait_ge(g_olo, H_A)
                dve.wait_ge(s_state_stored, 16)
                band.dve(dve)
                dve.wait_ge(kv_even_stored, 32)
                out_dve(dve, ph)
            else:
                def take_logits(unit):
                    nc.vector.tensor_tensor(out=halves(logit[:, :]), in0=unit_ap(unit)[0:H_C],
                                            in1=halves(inv_rms[0:H_C, :]), op=ALU.mult).then_inc(unit_free, 1)
                    dve.wait_ge(unit_free, ph["unit"] + 2)
                    nc.vector.tensor_scalar(out=logit[:, :], in0=logit[:, :], scalar1=bias_f[:, 0:1], scalar2=None,
                                            op0=ALU.add).then_inc(logit_done, 1)

                proj_dve(dve, ph, take_logits,
                         [(qc, j, SCALE) for j in range(KT)] + [(kc, j, 1.0) for j in range(KT)],
                         lambda s: vc[:, :, s * 256:(s + 1) * 256], lambda j: fgate_dve(dve, ph, j))
                dve.wait_ge(f_scratch, 32)
                dve.wait_ge(logf_stored, 16)
                fox.dve(dve)
                dve.wait_ge(kv_odd_stored, 48)
                out_dve(dve, ph)
        final_norm(dve, UNITS)

    @block.tensor
    def _(pe):
        for ph in PLAN:
            if ph["kind"] == "ffn":
                ffn_pe(pe, ph)
            elif ph["kind"] == "even":
                pe.wait_ge(masks_cast, 3)
                proj_pe(pe, ph, lambda s: gla_among_pe(pe, ph, s))
                gla_pe(pe, ph)
                pe.wait_ge(g_olo, H_A)
                band.pe(pe)
                out_pe(pe, ph, band.finished)
            else:
                proj_pe(pe, ph, lambda s: fgate_pe(pe, ph, s))
                pe.wait_ge(unit_free, mix_at(ph)["out"][1])
                fox.pe(pe)
                out_pe(pe, ph, fox.finished)
        norm_stats(pe, NORMS, UNITS)
        norm_spread(pe, NORMS, UNITS)

    ctx.close()


def _layout(i):
    f = np.float32
    a = {k: np.asarray(v) for k, v in i.items()}
    out = {}
    x = np.concatenate([a["x_prompt"].reshape(SEQ, D_MODEL), a["x_sample"].reshape(T - SEQ, D_MODEL)])
    out["x"] = x.T.reshape(KT, P, T).transpose(1, 0, 2)
    gu = a["ffn_w_gu"].reshape(4, KT, P, 2, D_FF // P, P)
    out["w_up"] = gu.transpose(0, 4, 2, 3, 1, 5).reshape(4, D_FF // P, P, SLAB)
    dn = a["ffn_w_down"].reshape(4, D_FF // P, P, KT, P)
    dn = dn.transpose(0, 3, 2, 1, 4)
    out["w_down_a"] = dn[:, :, :, :FF_A].reshape(4, KT, P, FF_A * P)
    out["w_down_b"] = dn[:, :, :, FF_A:].reshape(4, KT, P, FF_B * P)

    def fm(w):
        return w.reshape(KT, P, -1, 2, P).transpose(2, 1, 3, 0, 4).reshape(-1, P, SLAB)

    def tok(w):
        return w.reshape(KT, P, -1, 256).transpose(2, 1, 0, 3).reshape(-1, P, SLAB)

    e, o = a["even_w_in"][0], a["odd_w_in"][0]
    qk, v = H_A * DK, H_A * DV
    aq, ak, av, ag, ar, bq, bk, bv = np.split(e, np.cumsum([qk, qk, v, v, R_A, 512, 512]), axis=1)
    cq, ck, cv, cf = np.split(o, np.cumsum([1024, 1024, 1024]), axis=1)
    out["w_in"] = np.stack([np.concatenate([fm(np.concatenate([aq, ak, ag, bq, bk], 1)), tok(av), tok(bv)]),
                            np.concatenate([fm(np.concatenate([cq, ck], 1)), tok(cv)])])
    out["w_small"] = np.stack([w.reshape(KT, P, R_A).transpose(1, 0, 2) for w in (ar, cf)])
    out["w_out"] = np.stack([fm(a["even_w_out"][0]), fm(a["odd_w_out"][0])])
    out["gains"] = np.concatenate([a["norm_g"].reshape(6, D_MODEL), a["final_norm_g"][None]]
                                  ).reshape(7 * KT, P).T
    out["w_alpha"] = np.concatenate([a["gla_w_alpha_up"][0], a["gla_b_alpha"]])
    out["head_gain"] = a["gla_norm_g"].reshape(P, 1)
    out["bias_f"] = a["fox_b_f"].reshape(H_C, 1)
    st = a["state_gla"][0].reshape(DEC_BATCH, 2, 2, DK, DV)
    out["state"] = st.transpose(2, 3, 0, 1, 4).reshape(P, DEC_BATCH, 2, DV)
    kb = a["cache_band_k"][0].reshape(DEC_BATCH, WIN, 4, P)
    out["band_kc"] = kb.transpose(0, 3, 2, 1)
    out["band_vc"] = a["cache_band_v"][0].reshape(DEC_BATCH, 4, P, 512).transpose(0, 2, 1, 3)
    kf = a["cache_fox_k"][0].reshape(DEC_BATCH, 2, 512, 2, 4, P)
    out["fox_kc"] = kf.transpose(3, 0, 5, 1, 4, 2).reshape(2, DEC_BATCH, P, 8, 512)
    vf = a["cache_fox_v"][0].reshape(DEC_BATCH, 8, P, 2, 512)
    out["fox_vc"] = vf.transpose(3, 0, 2, 1, 4)
    out["fox_clogf"] = a["cache_fox_logf"][0].reshape(DEC_BATCH, 8, P, H_C).transpose(2, 1, 0, 3).reshape(P, 8, P)
    rel = a["band_rel_bias"][0]
    r = np.arange(P)
    c = np.arange(512) - 384
    pb = rel[:, np.clip(r[:, None] - c[None], -128, 128) + 128]
    pb = np.where((c[None] // CHUNK <= r[:, None] // CHUNK)[None], pb, f(NEG))
    out["band_bias"] = pb.reshape(4, 2, P, 512).transpose(0, 2, 1, 3)
    fr = np.arange(DEC_SEQ)
    sb = np.full((DEC_BATCH, H_B, DEC_SEQ, WIN + P), f(NEG))
    for b in range(DEC_BATCH):
        sb[b, :, :, :WIN] = rel[:, np.clip(WIN + fr[:, None] - np.arange(WIN)[None], -128, 128) + 128]
        own = slice(WIN + b * DEC_SEQ, WIN + (b + 1) * DEC_SEQ)
        sb[b, :, :, own] = rel[:, fr[:, None] - fr[None] + 128]
    out["band_bias_s"] = sb.reshape(DEC_BATCH, P, WIN + P)
    eye = np.eye(P, dtype=f)
    t, j = r[:, None], r[None]
    out["ident"], out["ones"] = eye, np.ones((P, P), f)
    out["mean_model"], out["mean_head"] = np.full((P, 1), 1 / D_MODEL, f), np.full((P, 1), 1 / DV, f)
    out["keep64"] = ((t <= j) & (t // CHUNK == j // CHUNK)).astype(f)
    out["keep16"] = ((t <= j) & (t // DEC_SEQ == j // DEC_SEQ)).astype(f)
    out["cum64"] = np.where((t <= j) & (t // CHUNK == j // CHUNK), f(1 / 16), f(0))
    out["cum16"] = np.where((t <= j) & (t // DEC_SEQ == j // DEC_SEQ), f(1 / 16), f(0))
    out["own_rows"] = (t // DEC_SEQ == np.arange(DEC_BATCH)[None]).astype(f)
    out["causal"] = np.where(j > t, f(NEG), f(0))
    d = np.arange(240)[None] - 112
    out["own_causal"] = np.where((d >= 0) & (d <= t % DEC_SEQ), f(0), f(NEG))
    out["after_w"] = (np.arange(1024)[None] - 896 < t).astype(f)
    out["upto_w"] = (np.arange(SEQ)[None] >= t).astype(f)
    return {k: np.ascontiguousarray(v) for k, v in out.items()}


_OUTS = {"y": (P, KT, T), "p_state": (P, 2, P), "s_state": (P, DEC_BATCH, 2, P), "band_k": (P, 4, T),
         "band_v": (P, TT, 512), "fox_k": (P, KT, T), "fox_v": (P, TT, D_MODEL), "fox_logf": (H_C, T)}


def kernel(**inputs):
    import concourse.bacc as bacc
    from concourse.bass_utils import run_bass_kernel_spmd

    arrays = _layout(inputs)
    nc = bacc.Bacc("TRN2", target_bir_lowering=False, num_devices=1)
    ins = {k: nc.dram_tensor("in_" + k, v.shape, mybir.dt.from_np(v.dtype), kind="ExternalInput").ap()
           for k, v in arrays.items()}
    outs = {k: nc.dram_tensor("out_" + k, s, F32, kind="ExternalOutput").ap() for k, s in _OUTS.items()}
    trunk_program(nc, ins, outs)
    r = run_bass_kernel_spmd(nc, [{"in_" + k: v for k, v in arrays.items()}], core_ids=[0]).results[0]
    got = {k: np.asarray(r["out_" + k]) for k in _OUTS}

    def frames(t, width):
        return t.transpose(2, 1, 0).reshape(T, width)

    def tok(t, width):
        return t.transpose(1, 0, 2).reshape(T, width)

    def split(t, tail):
        return (t[:SEQ].reshape(1, SEQ, *tail), t[SEQ:].reshape(DEC_BATCH, DEC_SEQ, *tail))

    yp, ys = split(frames(got["y"], D_MODEL), (D_MODEL,))
    bkp, bks = split(frames(got["band_k"], 512), (H_B, DH))
    bvp, bvs = split(tok(got["band_v"], 512), (H_B, DH))
    fkp, fks = split(frames(got["fox_k"], D_MODEL), (H_C, DH))
    fvp, fvs = split(tok(got["fox_v"], D_MODEL), (H_C, DH))
    flp, fls = split(got["fox_logf"].T, (H_C,))
    ps_ = got["p_state"].reshape(2, DK, 2, DV).transpose(2, 0, 1, 3).reshape(1, 1, H_A, DK, DV)
    ss_ = got["s_state"].reshape(2, DK, DEC_BATCH, 2, DV).transpose(2, 3, 0, 1, 4).reshape(1, DEC_BATCH, H_A, DK, DV)
    out = (yp, ys, ps_, bkp[None], bvp[None], fkp[None], fvp[None], flp[None], ss_, bks[None], bvs[None],
           fks[None], fvs[None], fls[None])
    return tuple(np.ascontiguousarray(t) for t in out)
```
